# Optimizing a Trainium2 kernel written in Bass

```python
import jax, jax.numpy as jnp
from jax import lax
import numpy as np
import math

D_MODEL = 1024
BATCH = 1
SEQ = 256
DEPTH = 2

HEAD_DIM = 64
N_ATTN_HEADS = 8
N_KV_HEADS = 2
GQA_GROUP = N_ATTN_HEADS // N_KV_HEADS
ATTN_WIDTH = N_ATTN_HEADS * HEAD_DIM
KV_WIDTH = N_KV_HEADS * HEAD_DIM
ROPE_DIM = HEAD_DIM // 4
ROPE_THETA = 500000.0
DILATED_PATTERNS = ((128, 1), (512, 4), (2048, 16))
ATTN_BLOCK = 128

SSM_HEAD_DIM = 64
SSM_HEADS = 16
SSM_INNER = SSM_HEADS * SSM_HEAD_DIM
SSM_GROUPS = 2
D_STATE = 128
CONV_WIDTH = 4
CHUNK = 128
CONV_CH = SSM_INNER + 2 * SSM_GROUPS * D_STATE

MIX_WIDTH = ATTN_WIDTH + SSM_INNER
Q_END = ATTN_WIDTH
K_END = Q_END + KV_WIDTH
V_END = K_END + KV_WIDTH
Z_END = V_END + SSM_INNER
XBC_END = Z_END + CONV_CH
IN_PROJ = XBC_END + SSM_HEADS

FFN_HIDDEN = ((8 * D_MODEL + 3 * 256 - 1) // (3 * 256)) * 256
EPS = 1e-5


def rmsnorm(x, w):
    xf = x.astype(jnp.float32)
    y = xf * lax.rsqrt(jnp.mean(xf * xf, axis=-1, keepdims=True) + EPS)
    return (y * w.astype(jnp.float32)).astype(x.dtype)

def rotary_tables(positions, dtype):
    inv_freq = ROPE_THETA ** (-jnp.arange(0, ROPE_DIM, 2, dtype=jnp.float32) / ROPE_DIM)
    ang = positions.astype(jnp.float32)[..., None] * inv_freq
    return jnp.cos(ang)[:, :, None, :].astype(dtype), jnp.sin(ang)[:, :, None, :].astype(dtype)

def partial_rotary(t, cos, sin):
    half = ROPE_DIM // 2
    t1, t2, rest = t[..., :half], t[..., half:ROPE_DIM], t[..., ROPE_DIM:]
    return jnp.concatenate([t1 * cos - t2 * sin, t2 * cos + t1 * sin, rest], axis=-1)

def dilated_window_branch(q, k, v, window, dilation):
    bsz, s = q.shape[0], q.shape[1]
    length = s // dilation
    w_d = window // dilation
    nb = -(-length // ATTN_BLOCK)
    lp = nb * ATTN_BLOCK
    qd = q.reshape((bsz, length, dilation) + q.shape[2:])
    kd = k.reshape((bsz, length, dilation) + k.shape[2:])
    vd = v.reshape((bsz, length, dilation) + v.shape[2:])
    qd = jnp.pad(qd, [(0, 0), (0, lp - length)] + [(0, 0)] * (qd.ndim - 2))
    kv_pad = [(0, 0), (ATTN_BLOCK, lp - length)] + [(0, 0)] * (kd.ndim - 2)
    kd = jnp.pad(kd, kv_pad)
    vd = jnp.pad(vd, kv_pad)
    qb = qd.reshape((bsz, nb, ATTN_BLOCK) + qd.shape[2:])
    kb = kd.reshape((bsz, nb + 1, ATTN_BLOCK) + kd.shape[2:])
    vb = vd.reshape((bsz, nb + 1, ATTN_BLOCK) + vd.shape[2:])
    kb = jnp.concatenate([kb[:, :-1], kb[:, 1:]], axis=2)
    vb = jnp.concatenate([vb[:, :-1], vb[:, 1:]], axis=2)
    scores = jnp.einsum('bnqrhgc,bnkrhc->bnrhgqk', qb, kb).astype(jnp.float32)
    qi = jnp.arange(ATTN_BLOCK)[:, None]
    ki = jnp.arange(2 * ATTN_BLOCK)[None, :]
    delta = qi + ATTN_BLOCK - ki
    kpos = jnp.arange(nb)[:, None, None] * ATTN_BLOCK - ATTN_BLOCK + ki[None]
    valid = (delta >= 0)[None] & (delta <= w_d)[None] & (kpos >= 0)
    scores = jnp.where(valid[None, :, None, None, None], scores, -jnp.inf)
    m = jnp.max(scores, axis=-1, keepdims=True)
    p = jnp.exp(scores - m)
    den = jnp.sum(p, axis=-1, keepdims=True)
    o = jnp.einsum('bnrhgqk,bnkrhc->bnrhgqc', p, vb.astype(jnp.float32)) / den
    lse = (m + jnp.log(den))[..., 0]
    o = jnp.transpose(o, (0, 1, 5, 2, 3, 4, 6)).reshape((bsz, lp, dilation) + q.shape[2:])
    lse = jnp.transpose(lse, (0, 1, 5, 2, 3, 4)).reshape((bsz, lp, dilation) + q.shape[2:4])
    o = o[:, :length].reshape(q.shape)
    lse = lse[:, :length].reshape(q.shape[:4])
    return o, lse

def dilated_attention(q, k, v):
    outs, lses = [], []
    for window, dilation in DILATED_PATTERNS:
        o, l = dilated_window_branch(q, k, v, window, dilation)
        outs.append(o)
        lses.append(l)
    wts = jax.nn.softmax(jnp.stack(lses, axis=0), axis=0)
    return jnp.einsum('ibshg,ibshgc->bshgc', wts, jnp.stack(outs, axis=0))

def causal_depthwise_conv(u, w, b):
    y = lax.conv_general_dilated(u, w[:, None, :], window_strides=(1,),
                                 padding=[(CONV_WIDTH - 1, 0)],
                                 dimension_numbers=('NWC', 'WIO', 'NWC'),
                                 feature_group_count=u.shape[-1])
    return y + b

def segsum_exp(a):
    cs = jnp.cumsum(a, axis=-1)
    diff = cs[..., :, None] - cs[..., None, :]
    t = a.shape[-1]
    mask = jnp.tril(jnp.ones((t, t), dtype=bool))
    return jnp.exp(jnp.where(mask, diff, -jnp.inf))

def ssd_chunked(xs, dt, a_neg, bm, cm):
    bsz, s, nh, hp = xs.shape
    nc = s // CHUNK
    e = nh // SSM_GROUPS
    xg = (xs.astype(jnp.float32) * dt[..., None]).reshape(bsz, nc, CHUNK, SSM_GROUPS, e, hp)
    a = jnp.transpose((dt * a_neg).reshape(bsz, nc, CHUNK, SSM_GROUPS, e), (0, 1, 3, 4, 2))
    bc = bm.astype(jnp.float32).reshape(bsz, nc, CHUNK, SSM_GROUPS, D_STATE)
    cc = cm.astype(jnp.float32).reshape(bsz, nc, CHUNK, SSM_GROUPS, D_STATE)
    a_cs = jnp.cumsum(a, axis=-1)
    cb = jnp.einsum('bclgn,bcsgn->bcgls', cc, bc)
    m_mat = cb[:, :, :, None] * segsum_exp(a)
    y_diag = jnp.einsum('bcgels,bcsgep->bclgep', m_mat, xg)
    decay_states = jnp.exp(a_cs[..., -1:] - a_cs)
    states = jnp.einsum('bclgn,bcgel,bclgep->bcgepn', bc, decay_states, xg)
    chunk_decay = jnp.exp(a_cs[..., -1])

    def step(h, inp):
        dec, st = inp
        return h * dec[..., None, None] + st, h

    h0 = jnp.zeros((bsz, SSM_GROUPS, e, hp, D_STATE), jnp.float32)
    _, prev = lax.scan(step, h0, (jnp.moveaxis(chunk_decay, 1, 0), jnp.moveaxis(states, 1, 0)))
    prev_states = jnp.moveaxis(prev, 0, 1)
    y_off = jnp.einsum('bclgn,bcgepn,bcgel->bclgep', cc, prev_states, jnp.exp(a_cs))
    return (y_diag + y_off).reshape(bsz, s, nh, hp)

def hybrid_mixer(h, w_in, conv_w, conv_b, dt_bias, a_log, d_skip, ssm_norm, w_out, cos, sin):
    bsz, s, _ = h.shape
    proj = h @ w_in
    q, k, v, z, xbc, dt = jnp.split(proj, [Q_END, K_END, V_END, Z_END, XBC_END], axis=-1)
    q = partial_rotary(q.reshape(bsz, s, N_ATTN_HEADS, HEAD_DIM), cos, sin)
    k = partial_rotary(k.reshape(bsz, s, N_KV_HEADS, HEAD_DIM), cos, sin)
    v = v.reshape(bsz, s, N_KV_HEADS, HEAD_DIM)
    q = (q * (HEAD_DIM ** -0.5)).reshape(bsz, s, N_KV_HEADS, GQA_GROUP, HEAD_DIM)
    attn = dilated_attention(q, k, v).reshape(bsz, s, ATTN_WIDTH).astype(h.dtype)
    xbc = jax.nn.silu(causal_depthwise_conv(xbc, conv_w, conv_b))
    xs, bm, cm = jnp.split(xbc, [SSM_INNER, SSM_INNER + SSM_GROUPS * D_STATE], axis=-1)
    xs = xs.reshape(bsz, s, SSM_HEADS, SSM_HEAD_DIM)
    bm = bm.reshape(bsz, s, SSM_GROUPS, D_STATE)
    cm = cm.reshape(bsz, s, SSM_GROUPS, D_STATE)
    dt = jax.nn.softplus(dt.astype(jnp.float32) + dt_bias.astype(jnp.float32))
    a_neg = -jnp.exp(a_log.astype(jnp.float32))
    y = ssd_chunked(xs, dt, a_neg, bm, cm) + d_skip.astype(jnp.float32)[:, None] * xs.astype(jnp.float32)
    y = y.reshape(bsz, s, SSM_INNER).astype(h.dtype) * jax.nn.silu(z)
    gsize = SSM_INNER // SSM_GROUPS
    y = rmsnorm(y.reshape(bsz, s, SSM_GROUPS, gsize), ssm_norm.reshape(SSM_GROUPS, gsize))
    y = y.reshape(bsz, s, SSM_INNER)
    return jnp.concatenate([attn, y], axis=-1) @ w_out

def swiglu(h, w_gate, w_up, w_down):
    return (jax.nn.silu(h @ w_gate) * (h @ w_up)) @ w_down

def first_inputs(seed: int = 0) -> dict:
    key = jax.random.key(seed)
    ks = jax.random.split(key, 16)
    f32 = jnp.float32
    x = jax.random.normal(ks[0], (BATCH, SEQ, D_MODEL), f32)
    positions = jnp.broadcast_to(jnp.arange(SEQ, dtype=jnp.int32), (BATCH, SEQ))
    norm_mix = 1.0 + 0.02 * jax.random.normal(ks[1], (DEPTH, D_MODEL), f32)
    w_in = jax.random.normal(ks[2], (DEPTH, D_MODEL, IN_PROJ), f32) * D_MODEL ** -0.5
    conv_w = jax.random.normal(ks[3], (DEPTH, CONV_WIDTH, CONV_CH), f32) * CONV_WIDTH ** -0.5
    conv_b = 0.01 * jax.random.normal(ks[4], (DEPTH, CONV_CH), f32)
    dt0 = jnp.exp(jax.random.uniform(ks[5], (DEPTH, SSM_HEADS), f32, np.log(1e-3), np.log(1e-1)))
    dt_bias = dt0 + jnp.log(-jnp.expm1(-dt0))
    a_log = jnp.log(jax.random.uniform(ks[6], (DEPTH, SSM_HEADS), f32, 1.0, 16.0))
    d_skip = 1.0 + 0.1 * jax.random.normal(ks[7], (DEPTH, SSM_HEADS), f32)
    ssm_norm = 1.0 + 0.02 * jax.random.normal(ks[8], (DEPTH, SSM_INNER), f32)
    w_out = jax.random.normal(ks[9], (DEPTH, MIX_WIDTH, D_MODEL), f32) * MIX_WIDTH ** -0.5
    norm_ffn = 1.0 + 0.02 * jax.random.normal(ks[10], (DEPTH, D_MODEL), f32)
    w_gate = jax.random.normal(ks[11], (DEPTH, D_MODEL, FFN_HIDDEN), f32) * D_MODEL ** -0.5
    w_up = jax.random.normal(ks[12], (DEPTH, D_MODEL, FFN_HIDDEN), f32) * D_MODEL ** -0.5
    w_down = jax.random.normal(ks[13], (DEPTH, FFN_HIDDEN, D_MODEL), f32) * FFN_HIDDEN ** -0.5
    final_norm = 1.0 + 0.02 * jax.random.normal(ks[14], (D_MODEL,), f32)
    return {"x": x, "positions": positions, "norm_mix": norm_mix, "w_in": w_in,
            "conv_w": conv_w, "conv_b": conv_b, "dt_bias": dt_bias, "a_log": a_log,
            "d_skip": d_skip, "ssm_norm": ssm_norm, "w_out": w_out, "norm_ffn": norm_ffn,
            "w_gate": w_gate, "w_up": w_up, "w_down": w_down, "final_norm": final_norm}

def first_block(x, positions, norm_mix, w_in, conv_w, conv_b, dt_bias, a_log, d_skip, ssm_norm,
              w_out, norm_ffn, w_gate, w_up, w_down, final_norm):
    cos, sin = rotary_tables(positions, x.dtype)
    h = x
    for layer in range(DEPTH):
        h = h + hybrid_mixer(rmsnorm(h, norm_mix[layer]), w_in[layer], conv_w[layer],
                             conv_b[layer], dt_bias[layer], a_log[layer], d_skip[layer],
                             ssm_norm[layer], w_out[layer], cos, sin)
        h = h + swiglu(rmsnorm(h, norm_ffn[layer]), w_gate[layer], w_up[layer], w_down[layer])
    return rmsnorm(h, final_norm)


DEPTH_2 = 4

N_HEADS = D_MODEL // HEAD_DIM
D_FF = 2816
NORM_EPS = 1e-6
N_MIXERS = 3

REL_BUCKETS = 32
REL_MAX_DIST = 1024

QBLK = 128

A_KV_HEADS = 2
A_WINDOW = 128

B_KV_GROUPS = 4
CMP_LEN = 32
CMP_STRIDE = 16
CMP_HIDDEN = 256
SLC_BLK = 64
SLC_TOPK = 16
B_WINDOW = 512
B_QCHUNK = 128

MOBA_BLK = 256
MOBA_TOPK = 3
MOBA_QCHUNK = 64

NEG = -1e30
TINY = 1e-30

A_IN = N_HEADS * HEAD_DIM + 2 * A_KV_HEADS * HEAD_DIM
B_IN = N_HEADS * HEAD_DIM + 6 * B_KV_GROUPS * HEAD_DIM + 3 * N_HEADS
C_IN = 3 * N_HEADS * HEAD_DIM

N_A_LAYERS = (DEPTH_2 + 2) // 3
N_B_LAYERS = (DEPTH_2 + 1) // 3
N_C_LAYERS = DEPTH_2 // 3


def rms_norm(x, g):
    xf = x.astype(jnp.float32)
    y = xf * lax.rsqrt(jnp.mean(xf * xf, axis=-1, keepdims=True) + NORM_EPS)
    return (y * g.astype(jnp.float32)).astype(x.dtype)

def swiglu_2(h, w_in, w_out):
    gate, up = jnp.split(h @ w_in, 2, axis=-1)
    return (jax.nn.silu(gate) * up) @ w_out

def rel_bucket(dist):
    dist = jnp.maximum(dist, 0)
    exact = REL_BUCKETS // 2
    d = jnp.maximum(dist, 1).astype(jnp.float32)
    log_b = exact + (jnp.log(d / exact) / math.log(REL_MAX_DIST / exact)
                     * (REL_BUCKETS - exact)).astype(jnp.int32)
    return jnp.where(dist < exact, dist, jnp.minimum(log_b, REL_BUCKETS - 1))

def masked_softmax(s, ok, sink=None):
    s = jnp.where(ok, s, NEG)
    m = jnp.max(s, axis=-1, keepdims=True)
    if sink is not None:
        m = jnp.maximum(m, sink)
    e = jnp.where(ok, jnp.exp(s - m), 0.0)
    denom = jnp.sum(e, axis=-1, keepdims=True)
    if sink is not None:
        denom = denom + jnp.exp(sink - m)
    return e / jnp.maximum(denom, TINY)

def banded_attention(q, k, v, rel_table, window, sinks=None):
    B, S, H, dh = q.shape
    G = k.shape[2]
    R = H // G
    n_prev = -(-(window - 1) // QBLK)
    pad = n_prev * QBLK
    slab = pad + QBLK
    kp = jnp.pad(k, ((0, 0), (pad, 0), (0, 0), (0, 0)))
    vp = jnp.pad(v, ((0, 0), (pad, 0), (0, 0), (0, 0)))
    n_blk = S // QBLK
    qb = q.reshape(B, n_blk, QBLK, G, R, dh).transpose(1, 0, 2, 3, 4, 5)
    qi = jnp.arange(QBLK)[:, None]
    kj = jnp.arange(slab)[None, :]
    dist = pad + qi - kj
    in_band = (dist >= 0) & (dist < window)
    bias = rel_table.astype(jnp.float32)[rel_bucket(dist)]
    bias = bias.reshape(QBLK, slab, G, R).transpose(2, 3, 0, 1)
    sink = None if sinks is None else sinks.astype(jnp.float32).reshape(G, R, 1, 1)
    scale = dh ** -0.5

    def block(args):
        n, q_n = args
        start = n * QBLK
        k_n = lax.dynamic_slice_in_dim(kp, start, slab, axis=1)
        v_n = lax.dynamic_slice_in_dim(vp, start, slab, axis=1)
        s = jnp.einsum("bqgrd,bkgd->bgrqk", q_n, k_n).astype(jnp.float32) * scale + bias
        ok = in_band & (start - pad + kj >= 0)
        p = masked_softmax(s, ok, sink)
        o = jnp.einsum("bgrqk,bkgd->bqgrd", p.astype(v.dtype), v_n)
        return o.reshape(B, QBLK, H, dh)

    out = lax.map(block, (jnp.arange(n_blk), qb))
    return out.transpose(1, 0, 2, 3, 4).reshape(B, S, H, dh)

def sliding_sink_attention(h, w_in, w_out, sinks, rel_table):
    B, S, _ = h.shape
    qw, kw = N_HEADS * HEAD_DIM, A_KV_HEADS * HEAD_DIM
    q, k, v = jnp.split(h @ w_in, [qw, qw + kw], axis=-1)
    q = q.reshape(B, S, N_HEADS, HEAD_DIM)
    k = k.reshape(B, S, A_KV_HEADS, HEAD_DIM)
    v = v.reshape(B, S, A_KV_HEADS, HEAD_DIM)
    o = banded_attention(q, k, v, rel_table, A_WINDOW, sinks)
    return o.reshape(B, S, -1) @ w_out

def compress_kv(kv, pos, w1, w2):
    B, S, G, dh = kv.shape
    n_cmp = (S - CMP_LEN) // CMP_STRIDE + 1
    idx = jnp.arange(n_cmp)[:, None] * CMP_STRIDE + jnp.arange(CMP_LEN)[None, :]
    blocks = kv[:, idx] + pos[:, None, :]
    flat = blocks.transpose(0, 1, 3, 2, 4).reshape(B, n_cmp, G, CMP_LEN * dh)
    return jax.nn.gelu(flat @ w1) @ w2

def selected_block_attention(q, k, v, sel_idx, rel_table):
    B, S, G, R, dh = q.shape
    n_sel = sel_idx.shape[-1]
    n_slc = S // SLC_BLK
    kb = k.reshape(B, n_slc, SLC_BLK, G, dh).transpose(0, 3, 1, 2, 4)
    vb = v.reshape(B, n_slc, SLC_BLK, G, dh).transpose(0, 3, 1, 2, 4)
    table_g = rel_table.astype(jnp.float32).reshape(REL_BUCKETS, G, R).transpose(1, 0, 2)
    g_ix = jnp.arange(G)[:, None, None]
    n_q = S // B_QCHUNK
    n_keys = n_sel * SLC_BLK
    scale = dh ** -0.5

    def chunk(i):
        b, c = i // n_q, i % n_q
        start = c * B_QCHUNK
        q_c = lax.dynamic_slice_in_dim(q[b], start, B_QCHUNK, axis=0)
        idx = lax.dynamic_slice_in_dim(sel_idx[b], start, B_QCHUNK, axis=1)
        k_sel = kb[b][g_ix, idx].reshape(G, B_QCHUNK, n_keys, dh)
        v_sel = vb[b][g_ix, idx].reshape(G, B_QCHUNK, n_keys, dh)
        pos = (idx[..., None] * SLC_BLK + jnp.arange(SLC_BLK)).reshape(G, B_QCHUNK, n_keys)
        t = start + jnp.arange(B_QCHUNK)
        dist = t[None, :, None] - pos
        bias = table_g[g_ix, rel_bucket(dist)].transpose(0, 3, 1, 2)
        s = jnp.einsum("qgrd,gqkd->grqk", q_c, k_sel).astype(jnp.float32) * scale + bias
        p = masked_softmax(s, (dist >= 0)[:, None])
        o = jnp.einsum("grqk,gqkd->qgrd", p.astype(v.dtype), v_sel)
        return o.reshape(B_QCHUNK, G * R, dh)

    out = lax.map(chunk, jnp.arange(B * n_q))
    return out.reshape(B, S, G * R, dh)

def nsa_attention(h, w_in, w_out, cmp_pos, cmp_w1, cmp_w2, rel_table):
    B, S, _ = h.shape
    G, R, dh = B_KV_GROUPS, N_HEADS // B_KV_GROUPS, HEAD_DIM
    kvw = G * dh
    splits = np.cumsum([N_HEADS * dh] + [kvw] * 6).tolist()
    q, kc, vc, ks, vs, kw, vw, gate = jnp.split(h @ w_in, splits, axis=-1)
    q = q.reshape(B, S, G, R, dh)
    to_kv = lambda a: a.reshape(B, S, G, dh)
    scale = dh ** -0.5
    t = jnp.arange(S)

    kc_b = compress_kv(to_kv(kc), cmp_pos[0], cmp_w1[0], cmp_w2[0])
    vc_b = compress_kv(to_kv(vc), cmp_pos[1], cmp_w1[1], cmp_w2[1])
    n_cmp = kc_b.shape[1]
    cmp_end = jnp.arange(n_cmp) * CMP_STRIDE + CMP_LEN - 1
    s_cmp = jnp.einsum("bsgrd,bngd->bgrsn", q, kc_b).astype(jnp.float32) * scale
    p_cmp = masked_softmax(s_cmp, cmp_end[None, :] <= t[:, None])
    o_cmp = jnp.einsum("bgrsn,bngd->bsgrd", p_cmp.astype(vc_b.dtype), vc_b)

    n_slc = S // SLC_BLK
    n_sel = min(SLC_TOPK, n_slc)
    c_start = np.arange(n_cmp)[:, None] * CMP_STRIDE
    s_start = np.arange(n_slc)[None, :] * SLC_BLK
    overlap = ((c_start < s_start + SLC_BLK) & (c_start + CMP_LEN > s_start)).astype(np.float32)
    imp = jnp.einsum("bgrsn,nj->bgsj", p_cmp, jnp.asarray(overlap))
    cur = (t // SLC_BLK)[:, None]
    j = jnp.arange(n_slc)[None, :]
    forced = (j == 0) | (j == cur) | (j == cur - 1)
    imp = jnp.where(j > cur, NEG, jnp.where(forced, -NEG, imp))
    _, sel_idx = lax.top_k(imp, n_sel)
    o_slc = selected_block_attention(q, to_kv(ks), to_kv(vs), sel_idx, rel_table)

    o_win = banded_attention(q.reshape(B, S, N_HEADS, dh), to_kv(kw), to_kv(vw),
                             rel_table, B_WINDOW)

    g = jax.nn.sigmoid(gate.astype(jnp.float32)).reshape(B, S, N_HEADS, 3).astype(o_win.dtype)
    o = (g[..., 0:1] * o_cmp.reshape(B, S, N_HEADS, dh)
         + g[..., 1:2] * o_slc + g[..., 2:3] * o_win)
    return o.reshape(B, S, -1) @ w_out

def moba_attention(h, w_in, w_out, rel_table):
    B, S, _ = h.shape
    H, dh = N_HEADS, HEAD_DIM
    q, k, v = jnp.split(h @ w_in, 3, axis=-1)
    q = q.reshape(B, S, H, dh)
    k = k.reshape(B, S, H, dh)
    v = v.reshape(B, S, H, dh)
    n_blk = -(-S // MOBA_BLK)
    s_pad = n_blk * MOBA_BLK
    kb = jnp.pad(k, ((0, 0), (0, s_pad - S), (0, 0), (0, 0))).reshape(B, n_blk, MOBA_BLK, H, dh)
    vb = jnp.pad(v, ((0, 0), (0, s_pad - S), (0, 0), (0, 0))).reshape(B, n_blk, MOBA_BLK, H, dh)
    n_top = min(MOBA_TOPK, n_blk - 1)
    table = rel_table.astype(jnp.float32)
    table_h = table.T
    scale = dh ** -0.5
    t = jnp.arange(S)
    if n_top > 0:
        k_mean = jnp.mean(kb.astype(jnp.float32), axis=2).astype(q.dtype)
        gate = jnp.einsum("bshd,bnhd->bhsn", q, k_mean).astype(jnp.float32)
        past = jnp.arange(n_blk)[None, :] < (t // MOBA_BLK)[:, None]
        _, sel = lax.top_k(jnp.where(past, gate, NEG), n_top)
        kbh = kb.transpose(0, 3, 1, 2, 4)
        vbh = vb.transpose(0, 3, 1, 2, 4)
    h_ix = jnp.arange(H)[:, None, None]
    n_q = S // MOBA_QCHUNK

    def chunk(i):
        b, c = i // n_q, i % n_q
        start = c * MOBA_QCHUNK
        q_c = lax.dynamic_slice_in_dim(q[b], start, MOBA_QCHUNK, axis=0)
        tq = start + jnp.arange(MOBA_QCHUNK)
        own = start // MOBA_BLK
        k_own = lax.dynamic_index_in_dim(kb[b], own, axis=0, keepdims=False)
        v_own = lax.dynamic_index_in_dim(vb[b], own, axis=0, keepdims=False)
        d_own = tq[:, None] - (own * MOBA_BLK + jnp.arange(MOBA_BLK))[None, :]
        s_own = (jnp.einsum("qhd,khd->hqk", q_c, k_own).astype(jnp.float32) * scale
                 + table[rel_bucket(d_own)].transpose(2, 0, 1))
        ok_own = jnp.broadcast_to(d_own >= 0, s_own.shape)
        if n_top == 0:
            p = masked_softmax(s_own, ok_own)
            return jnp.einsum("hqk,khd->qhd", p.astype(v.dtype), v_own)
        idx = lax.dynamic_slice_in_dim(sel[b], start, MOBA_QCHUNK, axis=1)
        n_keys = n_top * MOBA_BLK
        k_sel = kbh[b][h_ix, idx].reshape(H, MOBA_QCHUNK, n_keys, dh)
        v_sel = vbh[b][h_ix, idx].reshape(H, MOBA_QCHUNK, n_keys, dh)
        pos = (idx[..., None] * MOBA_BLK + jnp.arange(MOBA_BLK)).reshape(H, MOBA_QCHUNK, n_keys)
        d_sel = tq[None, :, None] - pos
        s_sel = (jnp.einsum("qhd,hqkd->hqk", q_c, k_sel).astype(jnp.float32) * scale
                 + table_h[h_ix, rel_bucket(d_sel)])
        ok_sel = jnp.broadcast_to((idx < own)[..., None],
                                  (H, MOBA_QCHUNK, n_top, MOBA_BLK)).reshape(H, MOBA_QCHUNK, n_keys)
        p = masked_softmax(jnp.concatenate([s_own, s_sel], axis=-1),
                           jnp.concatenate([ok_own, ok_sel], axis=-1)).astype(v.dtype)
        return (jnp.einsum("hqk,khd->qhd", p[..., :MOBA_BLK], v_own)
                + jnp.einsum("hqk,hqkd->qhd", p[..., MOBA_BLK:], v_sel))

    out = lax.map(chunk, jnp.arange(B * n_q))
    return out.reshape(B, S, H * dh) @ w_out

def second_inputs(seed: int = 0) -> dict:
    key = jax.random.key(seed)
    ks = jax.random.split(key, 16)
    f32 = jnp.float32
    hd = N_HEADS * HEAD_DIM

    def nrm(k, shape, fan_in):
        return jax.random.normal(k, shape, f32) * fan_in ** -0.5

    return {
        "x": jax.random.normal(ks[0], (BATCH, SEQ, D_MODEL), f32),
        "rel_bias": 0.5 * jax.random.normal(ks[1], (REL_BUCKETS, N_HEADS), f32),
        "norm_g": 1.0 + 0.05 * jax.random.normal(ks[2], (DEPTH_2, 6, D_MODEL), f32),
        "ffn_w_in": nrm(ks[3], (DEPTH_2, 2, D_MODEL, 2 * D_FF), D_MODEL),
        "ffn_w_out": nrm(ks[4], (DEPTH_2, 2, D_FF, D_MODEL), D_FF),
        "a_w_in": nrm(ks[5], (N_A_LAYERS, D_MODEL, A_IN), D_MODEL),
        "a_w_out": nrm(ks[6], (N_A_LAYERS, hd, D_MODEL), hd),
        "a_sinks": jax.random.normal(ks[7], (N_A_LAYERS, N_HEADS), f32),
        "b_w_in": nrm(ks[8], (N_B_LAYERS, D_MODEL, B_IN), D_MODEL),
        "b_w_out": nrm(ks[9], (N_B_LAYERS, hd, D_MODEL), hd),
        "b_cmp_pos": 0.5 * jax.random.normal(ks[10], (N_B_LAYERS, 2, CMP_LEN, HEAD_DIM), f32),
        "b_cmp_w1": nrm(ks[11], (N_B_LAYERS, 2, CMP_LEN * HEAD_DIM, CMP_HIDDEN), CMP_LEN * HEAD_DIM),
        "b_cmp_w2": nrm(ks[12], (N_B_LAYERS, 2, CMP_HIDDEN, HEAD_DIM), CMP_HIDDEN),
        "c_w_in": nrm(ks[13], (N_C_LAYERS, D_MODEL, C_IN), D_MODEL),
        "c_w_out": nrm(ks[14], (N_C_LAYERS, hd, D_MODEL), hd),
    }

def second_block(x, rel_bias, norm_g, ffn_w_in, ffn_w_out, a_w_in, a_w_out, a_sinks,
              b_w_in, b_w_out, b_cmp_pos, b_cmp_w1, b_cmp_w2, c_w_in, c_w_out):
    for i in range(DEPTH_2):
        g = norm_g[i]
        x = x + 0.5 * rms_norm(swiglu_2(rms_norm(x, g[0]), ffn_w_in[i, 0], ffn_w_out[i, 0]), g[1])
        hm = rms_norm(x, g[2])
        kind, j = i % N_MIXERS, i // N_MIXERS
        if kind == 0:
            m = sliding_sink_attention(hm, a_w_in[j], a_w_out[j], a_sinks[j], rel_bias)
        elif kind == 1:
            m = nsa_attention(hm, b_w_in[j], b_w_out[j], b_cmp_pos[j], b_cmp_w1[j],
                              b_cmp_w2[j], rel_bias)
        else:
            m = moba_attention(hm, c_w_in[j], c_w_out[j], rel_bias)
        x = x + rms_norm(m, g[3])
        x = x + 0.5 * rms_norm(swiglu_2(rms_norm(x, g[4]), ffn_w_in[i, 1], ffn_w_out[i, 1]), g[5])
    return x


def setup_inputs(seed=0):
    out = dict(first_inputs(seed))
    for name, value in second_inputs(seed + 1).items():
        if name != "x":
            out[name + "_2"] = value
    return out


def reference(
    x, positions, norm_mix, w_in, conv_w, conv_b, dt_bias, a_log, d_skip, ssm_norm, w_out,
    norm_ffn, w_gate, w_up, w_down, final_norm, rel_bias_2, norm_g_2, ffn_w_in_2, ffn_w_out_2,
    a_w_in_2, a_w_out_2, a_sinks_2, b_w_in_2, b_w_out_2, b_cmp_pos_2, b_cmp_w1_2, b_cmp_w2_2,
    c_w_in_2, c_w_out_2,
):
    x = first_block(
        x, positions, norm_mix, w_in, conv_w, conv_b, dt_bias, a_log, d_skip, ssm_norm, w_out,
        norm_ffn, w_gate, w_up, w_down, final_norm,
    )
    return second_block(
        x, rel_bias_2, norm_g_2, ffn_w_in_2, ffn_w_out_2, a_w_in_2, a_w_out_2, a_sinks_2,
        b_w_in_2, b_w_out_2, b_cmp_pos_2, b_cmp_w1_2, b_cmp_w2_2, c_w_in_2, c_w_out_2,
    )


_drawn_inputs = setup_inputs


def setup_inputs(seed=0):
    import zlib

    import numpy as np

    out = dict(_drawn_inputs(seed))
    spreads = {}
    factors = {}
    for name, (base, spread) in spreads.items():
        noise = np.random.default_rng([zlib.crc32(name.encode()), seed]).standard_normal(out[name].shape)
        drawn = base * np.exp(spread * noise) if base else spread * noise
        out[name] = __import__('jax').numpy.asarray(drawn.astype(out[name].dtype))
    for name, factor in factors.items():
        out[name] = (out[name] * factor).astype(out[name].dtype)
    return out
```

```python
import math
from contextlib import ExitStack

import numpy as np

import concourse.bass as bass
from concourse import mybir

F32 = mybir.dt.float32
F32R = mybir.dt.float32r
I32 = mybir.dt.int32
ALU = mybir.AluOpType
ACT = mybir.ActivationFunctionType
AX_X = mybir.AxisListType.X

P = 128
SEQ = 256
NT = SEQ // P
D = 1024
KT = D // P
HD = 64
FF = 2816
FT = FF // P
NEG = -1e30
TINY = 1e-30

H1, KV1 = 8, 2
SSM_INNER, SSM_HEADS, SSM_GROUPS, STATE, CONV_W = 1024, 16, 2, 128, 4
CONV_CH = SSM_INNER + 2 * SSM_GROUPS * STATE
CT = CONV_CH // P
EPG = SSM_HEADS // SSM_GROUPS
C_K = H1 * HD
C_Z = C_K + 2 * KV1 * HD
C_XBC = C_Z + SSM_INNER
C_DT = C_XBC + CONV_CH
ROPE_DIM, ROPE_THETA = HD // 4, 500000.0
EPS1 = 1e-5

NH = 16
EPS2 = 1e-6
BG = 4
CMP_LEN, CMP_STRIDE, CMP_HIDDEN = 32, 16, 256
NCMP = (SEQ - CMP_LEN) // CMP_STRIDE + 1
CJ = CMP_LEN * HD // P
NBUCKET, MAX_DIST = 32, 1024
A_WINDOW = 128

SLOT = 2048
SMALL = 1152
SLOT_B = 1024

CC = {}
_at = 0
for _name, _width in (("ident", 128), ("flip", 128), ("triu", 128), ("negtri", 128), ("rot", 128),
                      ("dilated", 384), ("window", 128), ("invf", 1), ("pad", 1), ("cmpbias", 32),
                      ("cmpok", 32), ("bucket", 384), ("future", 384)):
    CC[_name] = (_at, _at + _width)
    _at += _width
CONST_COLS = _at
KEPT_COLS = CC["bucket"][0]


def constants():
    c = np.zeros((P, CONST_COLS), np.float32)

    def put(name, value):
        a, b = CC[name]
        c[: value.shape[0], a:b] = value

    r = np.arange(P)
    put("ident", np.eye(P))
    put("flip", np.eye(P)[::-1])
    put("triu", (r[:, None] <= r[None, :]).astype(np.float32))
    put("negtri", np.where(r[:, None] <= r[None, :], 0.0, NEG))
    rot = np.zeros((P, P))
    half = ROPE_DIM // 2
    for m in range(P):
        if m % HD < half:
            rot[m + half, m] = -1.0
        elif m % HD < ROPE_DIM:
            rot[m - half, m] = 1.0
    put("rot", rot)
    blocks = []
    for t0, s0 in ((0, 0), (P, 0), (P, P)):
        d = (t0 + r[:, None]) - (s0 + r[None, :])
        n = ((d >= 0) & (d <= 128)).astype(int)
        n += (d >= 0) & (d % 4 == 0)
        n += (d >= 0) & (d % 16 == 0)
        blocks.append(np.where(n > 0, np.log(np.maximum(n, 1)), NEG))
    put("dilated", np.concatenate(blocks, axis=1))
    put("window", np.where(P + r[:, None] - r[None, :] < A_WINDOW, 0.0, NEG))
    f = (np.float32(ROPE_THETA) ** (-np.arange(0, ROPE_DIM, 2, dtype=np.float32) / np.float32(ROPE_DIM)))
    put("invf", np.array([f[p % HD % half] if p % HD < ROPE_DIM else 0.0 for p in range(P)])[:, None])
    end = np.arange(16) * CMP_STRIDE + CMP_LEN - 1
    ok = np.stack([(end[None, :] <= (t * P + r)[:, None]) & (np.arange(16) < NCMP) for t in range(NT)], axis=1)
    put("cmpok", ok.reshape(P, 32).astype(np.float32))
    put("cmpbias", np.where(ok, 0.0, NEG).reshape(P, 32))
    dist = 255 - np.arange(384)
    d = np.maximum(dist, 1).astype(np.float32)
    exact = NBUCKET // 2
    logb = exact + (np.log(d / np.float32(exact)) / np.float32(math.log(MAX_DIST / exact))
                    * np.float32(NBUCKET - exact)).astype(np.int32)
    bucket = np.where(dist < exact, dist, np.minimum(logb, NBUCKET - 1))
    hot = (np.arange(NBUCKET)[:, None] == bucket[None, :]) & (dist >= 0)[None, :]
    put("bucket", hot.astype(np.float32))
    put("future", np.broadcast_to(np.where(dist >= 0, 0.0, NEG), (P, 384)))
    return c


class Stage:

    def __init__(self, kind, block=0, layer=0, half=0, j=0):
        self.kind, self.block, self.layer, self.half, self.j = kind, block, layer, half, j


def plan_stages():
    st = []
    for l in range(2):
        st.append(Stage("hybrid", layer=l))
        st.append(Stage("ffn", block=1, layer=l, half=0))
    st.append(Stage("final"))
    for i in range(4):
        st.append(Stage("ffn", block=2, layer=i, half=0))
        st.append(Stage("ABCA"[i], layer=i, j=i // 3))
        st.append(Stage("ffn", block=2, layer=i, half=1))
    return st


KINDS = {
    "hybrid": (14, 20, 4, 4, 2, 2),
    "A": (5, 9, 8, 8, 1, 2),
    "B": (11, 19, 16, 8, 1, 2),
    "C": (12, 16, 8, 8, 1, 2),
}


DUPS = {"hybrid": 2, "A": 2, "B": 8, "C": 0}
OUT_SLOTS = {"hybrid": 6, "A": 4, "B": 4, "C": 4}


def build_block(nc, T, out, stages):
    a = b = units = pairs = turns = rms = proj = gains = dups = outs = 0
    for k, s in enumerate(stages):
        s.k = k
        s.a0, s.b0, s.unit0, s.pair0, s.turn0, s.rms0, s.proj0 = a, b, units, pairs, turns, rms, proj
        s.gain0, s.dup0, s.out0 = gains, dups, outs
        outs += s.kind != "final"
        if s.kind == "ffn":
            a, b, turns, rms = a + FT, b + FT, turns + 1, rms + 1 + (s.block == 2)
            gains += s.block == 2
        elif s.kind == "final":
            rms, gains = rms + 1, gains + 1
        else:
            n = KINDS[s.kind]
            proj, a, units, pairs, turns, rms = proj + n[0], a + n[1], units + n[2], pairs + n[3], turns + n[4], rms + n[5]
            gains += s.kind != "hybrid"
            dups += DUPS[s.kind]
    A_TOTAL, B_TOTAL = a, b

    ctx = ExitStack()
    with ctx:
        def sb(name, shape, dt=F32):
            return ctx.enter_context(nc.sbuf_tensor(name, shape, dt))

        def sem(name):
            return ctx.enter_context(nc.semaphore(name))

        x = sb("x", [P, NT, D])
        xT_hi, xT_lo = sb("xT_hi", [P, KT, SEQ], F32R), sb("xT_lo", [P, KT, SEQ], F32R)
        oT_hi, oT_lo = sb("oT_hi", [P, 12, SEQ], F32R), sb("oT_lo", [P, 12, SEQ], F32R)
        raw_a = sb("raw_a", [P, 2, SLOT])
        hi_a, lo_a = sb("hi_a", [P, 2, SLOT], F32R), sb("lo_a", [P, 2, SLOT], F32R)
        raw_b = sb("raw_b", [P, 2, SLOT_B])
        hi_b, lo_b = sb("hi_b", [P, 2, SLOT_B], F32R), sb("lo_b", [P, 2, SLOT_B], F32R)
        h_hi, h_lo = sb("h_hi", [P, 2, SEQ], F32R), sb("h_lo", [P, 2, SEQ], F32R)
        const = sb("const", [P, KEPT_COLS])
        cols = sb("cols", [P, 4, P])
        small = sb("small", [P, SMALL])
        arena = sb("arena", [P, 18432])

        def C(name, rows=P):
            lo, hi = CC[name]
            if lo >= KEPT_COLS:
                return setup_const[0:rows, lo - KEPT_COLS:hi - KEPT_COLS]
            return const[0:rows, lo:hi]

        ident = C("ident")
        n_small = [0]

        def sm(width):
            n_small[0] += width
            assert n_small[0] <= SMALL
            return small[:, n_small[0] - width:n_small[0]]

        def ar(at, width):
            assert at + width <= 18432
            return arena[:, at:at + width]

        xn = ar(6144, 2048).rearrange("p (t d) -> p t d", t=NT)
        gain_b = ar(8192, 1024)
        bias = ar(0, 6144).rearrange("p (h c) -> p h c", h=NH)
        qT2 = ar(9216, 2048).rearrange("p (u t) -> p u t", u=8)
        kT2 = ar(11264, 2048).rearrange("p (u t) -> p u t", u=8)
        v2 = ar(13312, 2048).rearrange("p (t d) -> p t d", t=NT)
        probs = [ar(at, 768).rearrange("p (h c) -> p h c", h=2) for at in (15360, 16128, 6144)]
        probT = ar(16896, 1536).rearrange("p (b c) -> p b c", b=2)
        junk = ar(16896, 1024)
        sg = ar(15360, 512).rearrange("p (b t) -> p b t", b=2)
        hh32 = ar(15872, 512).rearrange("p (b t) -> p b t", b=2)
        v2b = ar(13312, 1024).rearrange("p (t d) -> p t d", t=NT)
        w2dup = ar(14336, 512).rearrange("p (m e d) -> p m e d", m=2, e=2)
        kcT = ar(14848, 64).rearrange("p (g n) -> p g n", g=BG)
        vcb = ar(14912, 256).rearrange("p (g d) -> p g d", g=BG)
        gates = ar(15168, 96).rearrange("p (t c) -> p t c", t=NT)
        craw = ar(15360, 1024).rearrange("p (m u t) -> p m u t", m=2, u=2)
        zsh = ar(16896, 4 * 272).rearrange("p (g t) -> p g t", g=BG)
        zpos = ar(6144, 1024)
        hid = ar(7168, 512)
        hidr = ar(7168, 1024)
        pc = ar(6144, 1024)
        pcT = ar(7168, 1024).rearrange("p (g t) -> p g t", g=BG)
        zsil = ar(0, 2048).rearrange("p (t d) -> p t d", t=NT)
        upad = ar(2048, CT * 260).rearrange("p (c t) -> p c t", c=CT)
        cos = ar(5168, 256)
        sin = ar(5424, 256)
        conv = ar(8192, CT * SEQ).rearrange("p (c t) -> p c t", c=CT)
        qT1 = ar(11264, 1024).rearrange("p (u t) -> p u t", u=4)
        kraw1 = ar(12288, 256)
        kT1 = ar(12544, 512).rearrange("p (u t) -> p u t", u=2)
        v1 = ar(13056, 256).rearrange("p (t d) -> p t d", t=NT)
        xs = ar(13312, 2048).rearrange("p (t d) -> p t d", t=NT)
        ropet = ar(15360, 1024).rearrange("p (a c) -> p a c", a=2)
        mT = ar(2048, 2048).rearrange("p (h l) -> p h l", h=SSM_HEADS)
        cbT = ar(4096, 512).rearrange("p (c g l) -> p c g l", c=NT, g=SSM_GROUPS)
        btok = ar(4608, 256).rearrange("p (g n) -> p g n", g=SSM_GROUPS)
        xdt = ar(15360, 2048).rearrange("p (t d) -> p t d", t=NT)
        st0 = ar(17408, 1024)
        xdec = ar(11264, 1024)
        y = xn
        rows = ar(0, 512).rearrange("p (k c) -> p k c", k=4)
        posb = ar(512, 256)
        setup_const = ar(11264, CONST_COLS - KEPT_COLS)
        setup_t = ar(1024, 1536).rearrange("p (k c) -> p k c", k=6)
        bias_rev = ar(9216, 16 * 256).rearrange("p (h c) -> p h c", h=NH)
        bias_row = ar(15360, 384)

        ss = sm(8)
        ms = sm(8)
        rstd = sm(8)
        mhalf = sm(8)
        ssg = sm(4)
        nmax = sm(8).rearrange("p (b c) -> p b c", b=2)
        den = sm(8).rearrange("p (b c) -> p b c", b=2)
        rden = sm(8).rearrange("p (b c) -> p b c", b=2)
        esink = sm(8).rearrange("p (b c) -> p b c", b=2)
        sarg = sm(8).rearrange("p (b c) -> p b c", b=2)
        sinks = sm(32).rearrange("p (j h) -> p j h", j=2)
        nsinks = sm(32).rearrange("p (j h) -> p j h", j=2)
        dtb, alog, dskip = (sm(32).rearrange("p (l h) -> p l h", l=2) for _ in range(3))
        apos = sm(32).rearrange("p (l h) -> p l h", l=2)
        dt_raw, dt_x, dt_u, dt_w, dt_ln, dt_e, dt_d, dt, da = (sm(32) for _ in range(9))
        cs = sm(48)
        csd = sm(16)
        ecs1, dec0 = sm(16), sm(16)
        ones = sm(128)
        hid2 = sm(128)
        cmx, cden = sm(32), sm(32)
        rtab = sm(16)
        gexp = sm(96)

        acc = ctx.enter_context(nc.psum_tensor("acc", [P, 4, 512], F32))
        gu = ctx.enter_context(nc.psum_tensor("gu", [P, 2, 512], F32))
        tp = ctx.enter_context(nc.psum_tensor("tp", [P, 2, 512], F32))
        accx = acc[:, :, :].rearrange("p (t h) n -> p t (h n)", t=NT)

        a_full = [sem("a_full0"), sem("a_full1")]
        b_full = [sem("b_full0"), sem("b_full1")]
        a_hi, a_lo, a_used = sem("a_hi"), sem("a_lo"), sem("a_used")
        b_hi, b_lo, b_used = sem("b_hi"), sem("b_lo"), sem("b_used")
        x_ready = sem("x_ready")
        loaded, cols_ps, rows_ps = sem("loaded"), sem("cols_ps"), sem("rows_ps")
        angles, setup_dve, setup_act, bias_row_ready = sem("angles"), sem("setup_dve"), sem("setup_act"), sem("bias_row_ready")
        scratch_out, scratch_in = sem("scratch_out"), sem("scratch_in")
        out_half = sem("out_half")
        sq_act, ms_ready, rstd_ready = sem("sq_act"), sem("ms_ready"), sem("rstd_ready")
        xn_ready, turned, turn_hi, turn_lo = sem("xn_ready"), sem("turned"), sem("turn_hi"), sem("turn_lo")
        hid_gate, hid_ready, hid_hi, hid_lo = sem("hid_gate"), sem("hid_ready"), sem("hid_hi"), sem("hid_lo")
        gain_full, post_sq = sem("gain_full"), sem("post_sq")
        proj_ready, proj_out = sem("proj_ready"), sem("proj_out")
        k_dup = sem("k_dup")
        score_ready, soft_ready, exp_ready, prob_ready = sem("score_ready"), sem("soft_ready"), sem("exp_ready"), sem("prob_ready")
        pt_ready, pt_act, pt_dve = sem("pt_ready"), sem("pt_act"), sem("pt_dve")
        o_ready, o_hi, o_lo = sem("o_ready"), sem("o_hi"), sem("o_lo")
        rope_pe, rope_dve = sem("rope_pe"), sem("rope_dve")
        conved, silued = sem("conved"), sem("silued")
        x_turned, xs_act, xs_dve, bc_ps, bc_out = sem("x_turned"), sem("xs_act"), sem("xs_dve"), sem("bc_ps"), sem("bc_out")
        dt_neg, dt_exp, dt_one, dt_log, dt_done = sem("dt_neg"), sem("dt_exp"), sem("dt_one"), sem("dt_log"), sem("dt_done")
        cs_ps, cs_out, decays, xdec_ready = sem("cs_ps"), sem("cs_out"), sem("decays"), sem("xdec_ready")
        row_ps, seg_ready, seg_exp, m_ready = sem("row_ps"), sem("seg_ready"), sem("seg_exp"), sem("m_ready")
        state_ps, state_out, ydiag_ps, yoff_ps = sem("state_ps"), sem("state_out"), sem("ydiag_ps"), sem("yoff_ps")
        skip_ready, y_ready = sem("skip_ready"), sem("y_ready")
        zsh_clear, zsh_full, w2_full = sem("zsh_clear"), sem("zsh_full"), sem("w2_full")
        z_ready, z_hi, z_lo = sem("z_ready"), sem("z_hi"), sem("z_lo")
        cmp_hid, hid_rep, cmp_kv, ckv_out = sem("cmp_hid"), sem("hid_rep"), sem("cmp_kv"), sem("ckv_out")
        cmp_s, cmp_sub, cmp_exp, cmp_p = sem("cmp_s"), sem("cmp_sub"), sem("cmp_exp"), sem("cmp_p")
        cmp_pt, cmp_pt_out = sem("cmp_pt"), sem("cmp_pt_out")
        flip_ready, flip_act = sem("flip_ready"), sem("flip_act")
        stored = sem("stored")

        scratch = nc.dram_tensor("bias_rows", (NH, 384), F32).ap()

        def slot_sources(s, i):
            w_in = {"hybrid": "w_in", "A": "a_w_in_2", "B": "b_w_in_2", "C": "c_w_in_2"}[s.kind]
            w_out = {"hybrid": "w_out", "A": "a_w_out_2", "B": "b_w_out_2", "C": "c_w_out_2"}[s.kind]
            l = s.layer if s.kind == "hybrid" else s.j if s.kind == "A" else 0
            n_proj = KINDS[s.kind][0]
            n_all = KINDS[s.kind][1]
            n_out = OUT_SLOTS[s.kind]
            if i < n_proj:
                c0, width = proj_columns(s, i)
                src = T[w_in][l].rearrange("(k p) n -> p k n", p=P)[:, :, c0:c0 + width]
                return [(k0, width, src[:, k0:k0 + 4, :]) for k0 in (0, 4)]
            if i < n_all - n_out:
                m, half = (i - n_proj) // 2, (i - n_proj) % 2
                src = T["b_cmp_w1_2"][0, m].rearrange("(k p) n -> p k n", p=P)[:, half * 8:half * 8 + 8, :]
                return [(k0, 256, src[:, k0:k0 + 4, :]) for k0 in (0, 4)]
            r = 2 * (i - (n_all - n_out))
            src = T[w_out][l].rearrange("(k p) n -> p k n", p=P)
            return [(4 * e, 256, src[:, r + e, :].rearrange("p (k n) -> p k n", k=4)) for e in range(2)]

        def proj_columns(s, i):
            if s.kind == "hybrid":
                if i < 3:
                    return 256 * i, 256
                if i < 9:
                    return C_XBC + 256 * (i - 3), 256
                if i < 13:
                    return C_Z + 256 * (i - 9), 256
                return C_DT, SSM_HEADS
            if s.kind == "B" and i == 10:
                return 2560, 48
            if s.kind == "A":
                return 256 * (0, 4, 1, 2, 3)[i], 256
            return 256 * i, 256

        def slot_words(s, i):
            return proj_columns(s, i)[1] if i < KINDS[s.kind][0] else 256

        def a_view(buf, n):
            return buf[:, n % 2, :].rearrange("p (k n) -> p k n", k=8)

        def stage_slot(n):
            for s in stages:
                if s.kind != "final" and s.a0 <= n < s.a0 + (FT if s.kind == "ffn" else KINDS[s.kind][1]):
                    return s, n - s.a0
            return None, 0

        def hi_slot_a(act, n, width=256, par=None):
            par = n % 2 if par is None else par
            act.wait_ge(a_full[par], fills(n, par, 32))
            if not isinstance(n, int) or n >= 2:
                act.wait_ge(a_used, n - 1)
            nc.scalar.activation(a_view(hi_a, par)[:, :, 0:width], a_view(raw_a, par)[:, :, 0:width],
                                 ACT.Copy).then_inc(a_hi, 1)

        def fills(n, par, per):
            if isinstance(n, int):
                return per * (n // 2 + 1)
            return n * (per // 2) + (2 - par) * (per // 2)

        def lo_slot_a(dve, n, width=256, par=None):
            par = n % 2 if par is None else par
            dve.wait_ge(a_hi, n + 1)
            nc.vector.tensor_tensor(a_view(lo_a, par)[:, :, 0:width], a_view(raw_a, par)[:, :, 0:width],
                                    a_view(hi_a, par)[:, :, 0:width].bitcast(F32), ALU.subtract).then_inc(a_lo, 1)

        def hi_slot_b(act, m, par):
            act.wait_ge(b_full[par], fills(m, par, 16))
            if not isinstance(m, int) or m >= 2:
                act.wait_ge(b_used, m - 1)
            nc.scalar.activation(hi_b[:, par, :], raw_b[:, par, :], ACT.Copy).then_inc(b_hi, 1)

        def lo_slot_b(dve, m, par):
            dve.wait_ge(b_hi, m + 1)
            nc.vector.tensor_tensor(lo_b[:, par, :], raw_b[:, par, :], hi_b[:, par, :].bitcast(F32),
                                    ALU.subtract).then_inc(b_lo, 1)

        def ahead_a(split, eng, n):
            s, i = stage_slot(n)
            if s is not None:
                split(eng, n, 256 if s.kind == "ffn" else slot_words(s, i))

        def rms_sum_act(act, e, t, src, scale):
            act.drain()
            o = 2 * (e % 2) + t
            nc.scalar.activation(junk, src, ACT.Square, scale=scale, accum_out=ss[:, o:o + 1]).then_inc(sq_act, 1)

        def rms_pow_pool(pool, e, eps):
            for t in range(NT):
                pool.wait_ge(sq_act, 2 * e + t + 1)
                o = 2 * (e % 2) + t
                nc.gpsimd.tensor_scalar(ms[:, o:o + 1], ss[:, o:o + 1], eps, None, ALU.add)
                pool.drain()
                nc.gpsimd.tensor_tensor(rstd[:, o:o + 1], ms[:, o:o + 1], mhalf[:, 0:1], ALU.pow).then_inc(rstd_ready, 1)

        def turn_pe(pe, t, src):
            for tt in range(NT):
                pe.wait_ge(xn_ready, 2 * t + tt + 1)
                for kt in range(KT):
                    mm = nc.tensor.transpose(acc[:, kt // 2, (kt % 2) * 256 + tt * P:(kt % 2) * 256 + (tt + 1) * P],
                                             src[:, tt, kt * P:(kt + 1) * P], ident)
                    if tt and kt % 2:
                        mm.then_inc(turned, 1)

        def turn_act(act, t, dst, k0, col):
            for q in range(4):
                g = 4 * t + q
                act.wait_ge(turned, g + 1)
                for e in range(2):
                    kt = 2 * q + e
                    ins = nc.scalar.activation(dst[:, k0 + kt, :], acc[:, q, e * 256:(e + 1) * 256],
                                               ACT.Copy, scale=col(kt))
                ins.then_inc(turn_hi, 1)

        def turn_dve(dve, t, hi, lo, k0, col):
            for q in range(4):
                g = 4 * t + q
                dve.wait_ge(turn_hi, g + 1)
                for e in range(2):
                    kt = 2 * q + e
                    ins = nc.vector.scalar_tensor_tensor(lo[:, k0 + kt, :], acc[:, q, e * 256:(e + 1) * 256],
                                                         col(kt), hi[:, k0 + kt, :].bitcast(F32), ALU.mult, ALU.subtract)
                ins.then_inc(turn_lo, 1)

        def col(k, r):
            return cols[:, k, r:r + 1]

        def pre_col(s):
            if s.kind == "hybrid":
                return lambda kt: col(1, 8 * s.layer + kt)
            if s.kind == "ffn" and s.block == 1:
                return lambda kt: col(1, 16 + 8 * s.layer + kt)
            which = 2 if s.kind != "ffn" else 4 * s.half
            r = (s.layer % 2) * 48 + which * 8
            return lambda kt: col(2 + s.layer // 2, r + kt)

        def eps_of(s):
            return EPS1 if s.kind == "hybrid" or (s.kind == "ffn" and s.block == 1) or s.kind == "final" else EPS2

        def post_gain(s):
            return T["norm_g_2"][s.layer, 3 if s.kind != "ffn" else 1 + 4 * s.half]

        def stage_start(eng, s, t):
            if s.k:
                eng.wait_ge(x_ready, 2 * s.k - 1 + t)
            elif t == 0:
                eng.wait_ge(loaded, 16 * LOADS)
                eng.wait_ge(setup_dve, 1)
                eng.wait_ge(setup_act, 1)

        def pre_act(act, s):
            for t in range(NT):
                stage_start(act, s, t)
                rms_sum_act(act, s.rms0, t, x[:, t, :], D ** -0.5)
            turn_act(act, s.turn0, xT_hi, 0, pre_col(s))

        def pre_dve(dve, s):
            for t in range(NT):
                dve.wait_ge(rstd_ready, 2 * s.rms0 + t + 1)
                o = 2 * (s.rms0 % 2) + t
                nc.vector.tensor_scalar(xn[:, t, :], x[:, t, :], rstd[:, o:o + 1], None, ALU.mult).then_inc(xn_ready, 1)
            turn_dve(dve, s.turn0, xT_hi, xT_lo, 0, pre_col(s))

        def pre_pe(pe, s):
            if s.k:
                pe.wait_ge(x_ready, 2 * s.k)
            turn_pe(pe, s.turn0, xn)

        def added_norm(s):
            return not (s.kind == "hybrid" or (s.kind == "ffn" and s.block == 1))

        def post_act(act, s, done):
            if not added_norm(s):
                return
            for t in range(NT):
                if t == 0:
                    act.wait_ge(out_half, s.out0 + 1)
                else:
                    done()
                rms_sum_act(act, s.rms0 + 1, t, accx[:, t, :], D ** -0.5 * (2 if s.kind == "ffn" else 1))

        def post_dve(dve, s, done):
            if not added_norm(s):
                for t in range(NT):
                    if t == 0:
                        dve.wait_ge(out_half, s.out0 + 1)
                    else:
                        done()
                    nc.vector.tensor_tensor(x[:, t, :], accx[:, t, :], x[:, t, :], ALU.add).then_inc(x_ready, 1)
                return
            e = s.rms0 + 1
            dve.wait_ge(gain_full, 16 * (s.gain0 + 1))
            for t in range(NT):
                o = 2 * (e % 2) + t
                dve.wait_ge(sq_act, 2 * e + 1 + t)
                nc.vector.tensor_tensor(xn[:, t, :], accx[:, t, :], gain_b, ALU.mult)
                dve.drain()
                dve.wait_ge(rstd_ready, 2 * e + 1 + t)
                nc.vector.scalar_tensor_tensor(x[:, t, :], xn[:, t, :], rstd[:, o:o + 1], x[:, t, :],
                                               ALU.mult, ALU.add).then_inc(x_ready, 1)

        def first_products(pe, s, bank, w_hi, w_lo):
            for q in range(4):
                for part in range(3):
                    if part < 2:
                        pe.wait_ge((turn_hi, turn_lo)[part], 4 * s.turn0 + q + 1)
                    for e in range(2):
                        o = bank[:, e * 256:(e + 1) * 256]
                        for kt in (2 * q, 2 * q + 1):
                            w = (w_lo if part == 2 else w_hi)[:, kt, e * P:(e + 1) * P]
                            mm = nc.tensor.matmul(o, w, (xT_lo if part == 1 else xT_hi)[:, kt, :], start=(part == 0 and e == 0 and kt == 0),
                                                  stop=(part == 2 and e == 1 and kt == KT - 1))
            return mm

        def ffn_in_pe(pe, s, n, m, pa, pm, first=False):
            pe.wait_ge(a_hi, n + 1)
            if not isinstance(m, int) or m >= 2:
                pe.wait_ge(hid_ready, m - 1)
            w_hi, w_lo = a_view(hi_a, pa), a_view(lo_a, pa)
            if first:
                pe.wait_ge(a_lo, n + 1)
                first_products(pe, s, gu[:, pm, :], w_hi, w_lo).then_inc(a_used, 1)
                return
            for e in range(2):
                o = gu[:, pm, e * 256:(e + 1) * 256]
                for kt in range(KT):
                    w = w_hi[:, kt, e * P:(e + 1) * P]
                    nc.tensor.matmul(o, w, xT_hi[:, kt, :], start=(kt == 0), stop=False)
                    nc.tensor.matmul(o, w, xT_lo[:, kt, :], start=False, stop=False)
                if e == 0:
                    pe.wait_ge(a_lo, n + 1)
                for kt in range(KT):
                    mm = nc.tensor.matmul(o, w_lo[:, kt, e * P:(e + 1) * P], xT_hi[:, kt, :], start=False, stop=(kt == KT - 1))
            mm.then_inc(a_used, 1)

        def down_pe(lhs_hi, lhs_lo, w_hi, w_lo, start, stop):
            for t in range(NT):
                for i, (l, w) in enumerate(((lhs_hi, w_hi), (lhs_hi, w_lo), (lhs_lo, w_hi))):
                    for c in range(2):
                        mm = nc.tensor.matmul(acc[:, 2 * t + c, :], l[:, t * P:(t + 1) * P], w[:, c * 512:(c + 1) * 512],
                                              start=(start and i == 0), stop=(stop and i == 2))
                if stop and t == 0:
                    mm.then_inc(out_half, 1)
            return mm

        def ffn_out_pe(pe, m, pm, start=False, stop=False):
            pe.wait_ge(hid_lo, m + 1)
            pe.wait_ge(b_lo, m + 1)
            down_pe(h_hi[:, pm, :], h_lo[:, pm, :], hi_b[:, pm, :], lo_b[:, pm, :], start, stop).then_inc(b_used, 1)

        def ffn_pe(pe, s):
            pre_pe(pe, s)
            ffn_in_pe(pe, s, s.a0, s.b0, s.a0 % 2, 0, first=True)
            ffn_in_pe(pe, s, s.a0 + 1, s.b0 + 1, (s.a0 + 1) % 2, 1)
            ffn_out_pe(pe, s.b0, 0, start=True)
            with pe.Fori(1, FT // 2) as i:
                for e in range(2):
                    ffn_in_pe(pe, s, 2 * i + (s.a0 + e), 2 * i + (s.b0 + e), (s.a0 + e) % 2, e)
                    ffn_out_pe(pe, 2 * i + (s.b0 + e - 1), 1 - e)
            ffn_out_pe(pe, s.b0 + FT - 1, 1, stop=True)

        def ffn_tile_act(act, n, m, pa, pm, more_a, more_b):
            act.wait_ge(a_used, n + 1)
            if not isinstance(m, int) or m >= 2:
                act.wait_ge(hid_ready, m - 1)
            nc.scalar.activation(sg[:, pm, :], gu[:, pm, 0:256], ACT.Silu).then_inc(hid_gate, 1)
            if more_a:
                hi_slot_a(act, n + 2, par=pa)
            act.wait_ge(hid_ready, m + 1)
            if not isinstance(m, int) or m >= 2:
                act.wait_ge(b_used, m - 1)
            nc.scalar.activation(h_hi[:, pm, :], hh32[:, pm, :], ACT.Copy).then_inc(hid_hi, 1)
            if more_b:
                hi_slot_b(act, m + 1, 1 - pm)

        def ffn_tile_dve(dve, n, m, pa, pm, more_a, more_b):
            dve.wait_ge(hid_gate, m + 1)
            if not isinstance(m, int) or m >= 2:
                dve.wait_ge(hid_lo, m - 1)
                dve.wait_ge(hid_hi, m - 1)
            nc.vector.tensor_tensor(hh32[:, pm, :], sg[:, pm, :], gu[:, pm, 256:512], ALU.mult).then_inc(hid_ready, 1)
            if more_a:
                lo_slot_a(dve, n + 2, par=pa)
            dve.wait_ge(hid_hi, m + 1)
            nc.vector.tensor_tensor(h_lo[:, pm, :], hh32[:, pm, :], h_hi[:, pm, :].bitcast(F32), ALU.subtract)\
                .then_inc(hid_lo, 1)
            if more_b:
                lo_slot_b(dve, m + 1, 1 - pm)

        def ffn_tiles(eng, s, split_b, tile):
            split_b(eng, s.b0, 0)

            def pair(i, more_a, end):
                for e in range(2):
                    tile(eng, 2 * i + (s.a0 + e), 2 * i + (s.b0 + e), (s.a0 + e) % 2, e, more_a, not (end and e))

            pair(0, True, False)
            with eng.Fori(1, FT // 2 - 1) as i:
                pair(i, True, False)
            pair(FT // 2 - 1, s.a0 + FT < A_TOTAL, True)

        def ffn_act(act, s):
            pre_act(act, s)
            ffn_tiles(act, s, hi_slot_b, ffn_tile_act)
            post_act(act, s, lambda: act.wait_ge(b_used, s.b0 + FT))

        def ffn_dve(dve, s):
            pre_dve(dve, s)
            ffn_tiles(dve, s, lo_slot_b, ffn_tile_dve)
            post_dve(dve, s, lambda: dve.wait_ge(b_used, s.b0 + FT))

        def ffn_sync(sp, s):
            if s.block == 1:
                gate, up, down = T["w_gate"][s.layer], T["w_up"][s.layer], T["w_down"][s.layer]
                up0 = 0
            else:
                gate = up = T["ffn_w_in_2"][s.layer, s.half]
                down, up0 = T["ffn_w_out_2"][s.layer, s.half], FF
            gate = gate.rearrange("(k p) n -> p k n", p=P)
            up = up.rearrange("(k p) n -> p k n", p=P)

            def tile(n, m, j, pa, pm):
                dst = a_view(raw_a, pa)
                if not isinstance(n, int) or n >= 2:
                    sp.wait_ge(a_lo, n - 1)
                sp.dma_start(dst[:, :, 0:P], gate[:, :, bass.ds(j * P, P)]).then_inc(a_full[pa], 16)
                sp.dma_start(dst[:, :, P:2 * P], up[:, :, bass.ds(j * P + up0, P)]).then_inc(a_full[pa], 16)
                if not isinstance(m, int) or m >= 2:
                    sp.wait_ge(b_lo, m - 1)
                sp.dma_start(raw_b[:, pm, :], down[bass.ds(j * P, P), :]).then_inc(b_full[pm], 16)

            for e in range(2):
                tile(s.a0 + e, s.b0 + e, e, (s.a0 + e) % 2, e)
            with sp.Fori(1, FT // 2) as i:
                for e in range(2):
                    tile(2 * i + (s.a0 + e), 2 * i + (s.b0 + e), 2 * i + e, (s.a0 + e) % 2, e)
            if s.block == 2:
                load_gain(sp, s, post_gain(s))

        def load_gain(sp, s, row):
            sp.wait_ge(x_ready, 2 * (s.k - (s.kind == "final")))
            sp.dma_start(gain_b, row.partition_broadcast(P)).then_inc(gain_full, 16)

        def mixer_sync(sp, s):
            if s.kind == "B":
                for m in range(2):
                    for c in (0, HD):
                        sp.dma_start(w2dup[:, m, :, c:c + HD], T["b_cmp_w2_2"][0, m].rearrange("(e p) d -> p e d", p=P))\
                            .then_inc(w2_full, 16)
            for i in range(KINDS[s.kind][1]):
                n = s.a0 + i
                if n >= 2:
                    sp.wait_ge(a_lo, n - 1)
                for k0, width, src in slot_sources(s, i):
                    sp.dma_start(a_view(raw_a, n)[:, k0:k0 + 4, 0:width], src).then_inc(a_full[n % 2], 16)
            if s.kind != "hybrid":
                load_gain(sp, s, post_gain(s))

        def proj_modes(s):
            return {"hybrid": "ffm" + "f" * 6 + "t" * 5, "A": "fmfff",
                    "B": "ffff" + "ff" + "f" + "t" + "f" + "t" + "t", "C": "ffff" + "ffff" + "tttt"}[s.kind]

        def proj_pe(pe, s, i):
            n, p, mode, width = s.a0 + i, s.proj0 + i, proj_modes(s)[i], slot_words(s, i)
            bank = gu[:, p % 2, :]
            w_hi, w_lo = a_view(hi_a, n), a_view(lo_a, n)
            jobs = []
            if mode == "f":
                jobs = [("f", e * 256, e * P, P) for e in range(2)]
            elif mode == "m":
                jobs = [("f", 0, 0, P)] + [("t", 256 + t * P, P, P, t) for t in range(NT)]
            else:
                jobs = [("t", t * 256, 0, width, t) for t in range(NT)]
            pe.wait_ge(a_lo, n + 1)
            if p >= 2:
                pe.wait_ge(proj_out, p - 1)
            if i == 0:
                first_products(pe, s, bank, w_hi, w_lo).then_inc(a_used, 1)
                return
            for job in jobs:
                o0, c0, w = job[1:4]
                for kt in range(KT):
                    wh, wl = w_hi[:, kt, c0:c0 + w], w_lo[:, kt, c0:c0 + w]
                    first, last = kt == 0, kt == KT - 1
                    if job[0] == "f":
                        o = bank[:, o0:o0 + 256]
                        nc.tensor.matmul(o, wh, xT_hi[:, kt, :], start=first, stop=False)
                        nc.tensor.matmul(o, wh, xT_lo[:, kt, :], start=False, stop=False)
                        mm = nc.tensor.matmul(o, wl, xT_hi[:, kt, :], start=False, stop=last)
                    else:
                        o, t = bank[:, o0:o0 + w], job[4]
                        xh, xl = xT_hi[:, kt, t * P:(t + 1) * P], xT_lo[:, kt, t * P:(t + 1) * P]
                        nc.tensor.matmul(o, xh, wh, start=first, stop=False)
                        nc.tensor.matmul(o, xh, wl, start=False, stop=False)
                        mm = nc.tensor.matmul(o, xl, wh, start=False, stop=last)
            mm.then_inc(a_used, 1)

        def proj_act(act, s, i, evacuate):
            n, p = s.a0 + i, s.proj0 + i
            act.wait_ge(a_used, n + 1)
            evacuate(gu[:, p % 2, :]).then_inc(proj_out, 1)
            ahead_a(hi_slot_a, act, n + 2)

        def out_pe(pe, s):
            n_out = OUT_SLOTS[s.kind]
            first = s.a0 + KINDS[s.kind][1] - n_out
            for r in range(n_out):
                n = first + r
                pe.wait_ge(a_lo, n + 1)
                for e in range(2):
                    k = 2 * r + e
                    mm = down_pe(oT_hi[:, k, :], oT_lo[:, k, :], hi_a[:, n % 2, e * D:(e + 1) * D],
                                 lo_a[:, n % 2, e * D:(e + 1) * D], k == 0, k == 2 * n_out - 1)
                mm.then_inc(a_used, 1)

        def out_split(split, eng, s):
            n_out = OUT_SLOTS[s.kind]
            first = s.a0 + KINDS[s.kind][1] - n_out
            for r in range(n_out):
                ahead_a(split, eng, first + r + 2)

        def unit(s, w):
            if s.kind == "hybrid":
                g = 2 * w // (H1 // KV1)
                return w, 0, kT1[:, g, :], (v1, g * HD, g * HD), C("dilated").unsqueeze(1).broadcast_to([P, 2, 384])
            if s.kind == "A":
                g = 2 * w // 8
                return w, 0, kT2[:, g, :], (v2, g * HD, g * HD), bias[:, 2 * w:2 * w + 2, :]
            if s.kind == "B":
                u, br = w // 2, w % 2
                g = 2 * u // 4
                return u, br, kT2[:, 4 * br + g, :], (v2b, 256 * br + g * HD, 256 * br + g * HD), bias[:, 2 * u:2 * u + 2, :]
            return w, 0, kT2[:, w, :], (v2, 2 * w * HD, (2 * w + 1) * HD), bias[:, 2 * w:2 * w + 2, :]

        def branches(s):
            return 2 if s.kind == "B" else 1

        def n_units(s):
            return KINDS[s.kind][2]

        def scores_pe(pe, s, w):
            g = s.unit0 + w
            u, _, kt, _, _ = unit(s, w)
            q = qT1 if s.kind == "hybrid" else qT2
            if g >= 2:
                pe.wait_ge(soft_ready, g - 1)
            for hh in range(2):
                r = slice(64 * hh, 64 * hh + 64)
                bank = acc[:, 2 * (g % 2) + hh, :]
                nc.tensor.matmul(bank[:, 0:128], q[r, u, 0:128], kt[r, 0:128], start=True, stop=True)
                mm = nc.tensor.matmul(bank[:, 128:384], q[r, u, 128:256], kt[r, 0:256], start=True, stop=True)
            mm.then_inc(score_ready, 1)

        def turn_probs_pe(pe, s, w):
            g = s.unit0 + w
            pe.wait_ge(prob_ready, g + 1)
            if g >= 1:
                pe.wait_ge(pt_act, g)
            for hh in range(2):
                for t in range(NT):
                    mm = nc.tensor.transpose(gu[:, 0, hh * 256 + t * P:hh * 256 + (t + 1) * P],
                                             probs[g % 3][:, hh, t * P:(t + 1) * P], ident)
            mm.then_inc(pt_ready, 1)
            if g >= 1:
                pe.wait_ge(pt_dve, g)
            for hh in range(2):
                mm = nc.tensor.transpose(gu[:, 1, hh * P:(hh + 1) * P], probs[g % 3][:, hh, 256:384], ident)
            mm.then_inc(pt_ready, 1)

        def values_pe(pe, s, w):
            g = s.unit0 + w
            u, br, _, (v, c0, c1), _ = unit(s, w)
            o = s.pair0 + u
            nb = branches(s)
            pe.wait_ge(pt_act, g + 1)
            pe.wait_ge(pt_dve, g + 1)
            if br == 0 and o >= 2:
                pe.wait_ge(o_lo, o - 1)
            for hh, c in ((0, c0), (1, c1)):
                r = slice(64 * hh, 64 * hh + 64)
                bank = tp[r, o % 2, :]
                last = br == nb - 1
                cmp_too = s.kind == "B" and last
                nc.tensor.matmul(bank[:, 0:256], v[:, 0, c:c + HD], probT[:, g % 2, hh * 256:(hh + 1) * 256],
                                 start=(br == 0), stop=False)
                mm = nc.tensor.matmul(bank[:, 128:256], v[:, 1, c:c + HD], probT[:, g % 2, 512 + hh * P:512 + (hh + 1) * P],
                                      start=False, stop=(last and not cmp_too))
                if cmp_too:
                    head = 2 * u + hh
                    q = slice(32 * (head % 4), 32 * (head % 4) + 32)
                    mm = nc.tensor.matmul(bank[:, 0:256], vcb[q, head // 4, :], pcT[q, head // 4, :], start=False, stop=True)
            if br == nb - 1:
                mm.then_inc(o_ready, 1)

        def attention_steps(s):
            return range(n_units(s) + 3)

        def first_scores_pe(pe, s):
            last = KINDS[s.kind][0] - (s.kind != "B")
            pe.wait_ge(proj_out, s.proj0 + last)
            if DUPS[s.kind]:
                pe.wait_ge(k_dup, 16 * (s.dup0 + DUPS[s.kind]))
            scores_pe(pe, s, 0)

        def attention_pe(pe, s):
            W = n_units(s)
            for k in attention_steps(s):
                if 0 <= k - 2 < W:
                    turn_probs_pe(pe, s, k - 2)
                if k + 1 < W:
                    scores_pe(pe, s, k + 1)
                if k == 0:
                    pe.wait_ge(proj_out, s.proj0 + KINDS[s.kind][0])
                if 0 <= k - 2 < W:
                    values_pe(pe, s, k - 2)

        def attention_act(act, s, steps):
            W, nb = n_units(s), branches(s)
            for k in steps:
                if 0 <= k - 2 < W:
                    g = s.unit0 + k - 2
                    act.wait_ge(pt_ready, 2 * g + 1)
                    nc.scalar.activation(probT[:, g % 2, 0:512], gu[:, 0, :], ACT.Copy).then_inc(pt_act, 1)
                if k < W:
                    g = s.unit0 + k
                    b, prob = g % 2, probs[g % 3]
                    act.wait_ge(soft_ready, g + 1)
                    for hh in range(2):
                        nc.scalar.activation(prob[:, hh, 0:128], prob[:, hh, 0:128], ACT.Exp,
                                             bias=nmax[:, b, 2 * hh:2 * hh + 1], accum_out=den[:, b, 2 * hh:2 * hh + 1])
                        ins = nc.scalar.activation(prob[:, hh, 128:384], prob[:, hh, 128:384], ACT.Exp,
                                                   bias=nmax[:, b, 2 * hh + 1:2 * hh + 2], accum_out=den[:, b, 2 * hh + 1:2 * hh + 2])
                    if s.kind == "A":
                        ins = nc.scalar.activation(esink[:, b, :], sarg[:, b, :], ACT.Exp)
                    ins.then_inc(exp_ready, 1)
                if 0 <= k - 2 < W and (k - 2) % nb == nb - 1:
                    u = (k - 2) // nb
                    o = s.pair0 + u
                    act.wait_ge(o_ready, o + 1)
                    nc.scalar.activation(oT_hi[:, u, :], tp[:, o % 2, 0:256], ACT.Copy).then_inc(o_hi, 1)

        def soft_dve(dve, s, k):
            g = s.unit0 + k
            b, prob = g % 2, probs[g % 3]
            dve.wait_ge(score_ready, g + 1)
            nc.vector.scalar_tensor_tensor(prob, acc[:, 2 * b:2 * b + 2, 0:384], HD ** -0.5, unit(s, k)[4],
                                           ALU.mult, ALU.add)
            dve.drain()
            if s.kind == "A":
                nc.vector.tensor_tensor(prob[:, :, 128:256], prob[:, :, 128:256],
                                        C("window").unsqueeze(1).broadcast_to([P, 2, P]), ALU.add)
                dve.drain()
            n4 = nmax[:, b, :].rearrange("p (h t) -> p h t", h=2)
            for t, (c0, c1) in enumerate(((0, 128), (128, 384))):
                ins = nc.vector.tensor_reduce(n4[:, :, t:t + 1], prob[:, :, c0:c1], AX_X, ALU.max, negate=True)
            if s.kind == "A":
                dve.drain()
                sk = sinks[:, s.j, 2 * k:2 * k + 2].unsqueeze(2).broadcast_to([P, 2, 2])
                nk = nsinks[:, s.j, 2 * k:2 * k + 2].unsqueeze(2).broadcast_to([P, 2, 2])
                nc.vector.tensor_tensor(n4, n4, nk, ALU.min)
                dve.drain()
                ins = nc.vector.tensor_tensor(sarg[:, b, :].rearrange("p (h t) -> p h t", h=2), n4, sk, ALU.add)
            ins.then_inc(soft_ready, 1)

        def normalise_dve(dve, s, w):
            g = s.unit0 + w
            b, prob = g % 2, probs[g % 3]
            dve.wait_ge(exp_ready, g + 1)
            if s.kind == "A":
                nc.vector.tensor_tensor(den[:, b, :], den[:, b, :], esink[:, b, :], ALU.add)
                dve.drain()
            nc.vector.reciprocal(rden[:, b, :], den[:, b, :])
            dve.drain()
            r4 = rden[:, b, :].rearrange("p (h t) -> p h t", h=2)
            if s.kind == "B":
                u, br = w // 2, w % 2
                gt = gates.rearrange("p t (h c) -> p h t c", c=3)[:, 2 * u:2 * u + 2, :, 1 + br]
                nc.vector.tensor_tensor(r4, r4, gt, ALU.mult)
                dve.drain()
            for t, (c0, c1) in enumerate(((0, 128), (128, 384))):
                ins = nc.vector.tensor_tensor(prob[:, :, c0:c1], prob[:, :, c0:c1],
                                              r4[:, :, t:t + 1].broadcast_to([P, 2, c1 - c0]), ALU.mult)
            ins.then_inc(prob_ready, 1)

        def attention_dve(dve, s, steps):
            W, nb = n_units(s), branches(s)
            for k in steps:
                if k < W:
                    soft_dve(dve, s, k)
                if 0 <= k - 2 < W:
                    g = s.unit0 + k - 2
                    dve.wait_ge(pt_ready, 2 * g + 2)
                    nc.vector.tensor_copy(probT[:, g % 2, 512:768], gu[:, 1, 0:256]).then_inc(pt_dve, 1)
                if 0 <= k - 3 < W and (k - 3) % nb == nb - 1:
                    u = (k - 3) // nb
                    o = s.pair0 + u
                    dve.wait_ge(o_hi, o + 1)
                    nc.vector.tensor_tensor(oT_lo[:, u, :], tp[:, o % 2, 0:256], oT_hi[:, u, :].bitcast(F32),
                                            ALU.subtract).then_inc(o_lo, 1)
                if 0 <= k - 1 < W:
                    normalise_dve(dve, s, k - 1)

        def dup_keys(act, kt, tiles):
            for c in tiles:
                src, dst = (slice(0, 64), slice(64, 128)) if c % 2 == 0 else (slice(64, 128), slice(0, 64))
                act.dma_start(kt[dst, c, :], kt[src, c, :]).then_inc(k_dup, 16)

        def half_keys(kt, c, bank):
            nc.scalar.activation(kt[0:64, c, :], bank[0:64, 0:256], ACT.Copy)
            return nc.scalar.activation(kt[64:128, c + 1, :], bank[64:128, 0:256], ACT.Copy)

        def evac_A(i):
            c = max(i - 1, 0)

            def q(bank):
                return nc.scalar.activation(qT2[:, 2 * c:2 * c + 2, :], bank.rearrange("p (u t) -> p u t", u=2), ACT.Copy)

            def kv(bank):
                half_keys(kT2, 0, bank)
                return nc.scalar.activation(v2[:, :, 0:128], bank[:, 256:512].rearrange("p (t d) -> p t d", t=2), ACT.Copy)
            return kv if i == 1 else q

        def evac_C(i):
            def qk(bank):
                dst = qT2 if i < 4 else kT2
                return nc.scalar.activation(dst[:, 2 * (i % 4):2 * (i % 4) + 2, :], bank.rearrange("p (u t) -> p u t", u=2), ACT.Copy)

            def v(bank):
                c = 256 * (i - 8)
                return nc.scalar.activation(v2[:, :, c:c + 256], bank.rearrange("p (t d) -> p t d", t=2), ACT.Copy)
            return qk if i < 8 else v

        def ac_pe(pe, s):
            pre_pe(pe, s)
            for i in range(KINDS[s.kind][0]):
                if i == KINDS[s.kind][0] - 1:
                    first_scores_pe(pe, s)
                proj_pe(pe, s, i)
            attention_pe(pe, s)
            pe.wait_ge(o_lo, s.pair0 + 8)
            out_pe(pe, s)

        def ac_act(act, s):
            pre_act(act, s)
            for i in range(KINDS[s.kind][0]):
                if i == KINDS[s.kind][0] - 1:
                    attention_act(act, s, attention_steps(s)[:1])
                proj_act(act, s, i, (evac_A if s.kind == "A" else evac_C)(i))
                if s.kind == "A" and i == 1:
                    act.wait_ge(proj_out, s.proj0 + 2)
                    dup_keys(act, kT2, (0, 1))
            attention_act(act, s, attention_steps(s)[1:])
            out_split(hi_slot_a, act, s)
            post_act(act, s, lambda: act.wait_ge(a_used, s.a0 + KINDS[s.kind][1]))

        def ac_dve(dve, s):
            pre_dve(dve, s)
            for i in range(KINDS[s.kind][0]):
                if i == KINDS[s.kind][0] - 1:
                    attention_dve(dve, s, attention_steps(s)[:1])
                ahead_a(lo_slot_a, dve, s.a0 + i + 2)
            attention_dve(dve, s, attention_steps(s)[1:])
            out_split(lo_slot_a, dve, s)
            post_dve(dve, s, None)

        def evac_B(i):
            def q(bank):
                return nc.scalar.activation(qT2[:, 2 * i:2 * i + 2, :], bank.rearrange("p (u t) -> p u t", u=2), ACT.Copy)

            def c(bank):
                return nc.scalar.activation(craw[:, i - 4, :, :], bank.rearrange("p (u t) -> p u t", u=2), ACT.Copy)

            def k(bank):
                br = (i - 6) // 2
                half_keys(kT2, 4 * br, bank[:, 0:256])
                return half_keys(kT2, 4 * br + 2, bank[:, 256:512])

            def v(bank):
                br = (i - 7) // 2
                return nc.scalar.activation(v2b[:, :, 256 * br:256 * br + 256], bank.rearrange("p (t d) -> p t d", t=2), ACT.Copy)

            def g(bank):
                return nc.scalar.activation(gexp.rearrange("p (t c) -> p t c", t=2),
                                            bank.rearrange("p (t d) -> p t d", t=2)[:, :, 0:48], ACT.Exp, scale=-1.0)
            return q if i < 4 else c if i < 6 else g if i == 10 else (k, v)[i % 2]

        def shift_rows(act, m):
            for g in range(BG):
                src = craw[64 * (g % 2):64 * (g % 2) + 64, m, g // 2, :]
                act.dma_start(zsh[0:64, g, 0:256], src).then_inc(zsh_full, 16)
                act.dma_start(zsh[64:128, g, 0:255], src[:, 1:256]).then_inc(zsh_full, 16)

        def b_pe(pe, s):
            pre_pe(pe, s)
            for i in range(11):
                proj_pe(pe, s, i)
            pe.wait_ge(proj_out, s.proj0 + 11)
            for m in range(2):
                pe.wait_ge(z_lo, m + 1)
                for q in range(2):
                    n = s.a0 + 11 + 2 * m + q
                    pe.wait_ge(a_lo, n + 1)
                    w_hi, w_lo = a_view(hi_a, n), a_view(lo_a, n)
                    for e in range(2):
                        o = gu[:, e, 0:64]
                        for kk in range(8):
                            j = 8 * q + kk
                            c = slice(64 * (j % 4), 64 * (j % 4) + 64)
                            xh, xl = oT_hi[:, j // 4, c], oT_lo[:, j // 4, c]
                            wh, wl = w_hi[:, kk, e * P:(e + 1) * P], w_lo[:, kk, e * P:(e + 1) * P]
                            nc.tensor.matmul(o, wh, xh, start=(j == 0), stop=False)
                            nc.tensor.matmul(o, wh, xl, start=False, stop=False)
                            mm = nc.tensor.matmul(o, wl, xh, start=False, stop=(j == CJ - 1))
                    mm.then_inc(a_used, 1)
                pe.wait_ge(cmp_hid, m + 1)
                if m == 0:
                    pe.wait_ge(w2_full, 64)
                    for e in range(2):
                        mm = nc.tensor.matmul(tp[:, 0, 0:64], w2dup[:, 0, e, :], hid[:, 64 * e:64 * e + 64],
                                              start=(e == 0), stop=(e == 1))
                else:
                    pe.wait_ge(hid_rep, 1)
                    hr = hidr.rearrange("p (e g c) -> p e g c", e=2, g=BG)
                    for g in range(BG):
                        for e in range(2):
                            mm = nc.tensor.matmul(tp[:, 1, g * HD:(g + 1) * HD], hr[:, e, g, :], w2dup[:, 1, e, 0:HD],
                                                  start=(e == 0), stop=(e == 1))
                mm.then_inc(cmp_kv, 1)
            pe.wait_ge(ckv_out, 2)
            for t in range(NT):
                for h in range(NH):
                    r = slice(64 * (h % 2), 64 * (h % 2) + 64)
                    mm = nc.tensor.matmul(acc[:, 2 * t + h % 2, 16 * (h // 2):16 * (h // 2) + 16], qT2[r, h // 2, t * P:(t + 1) * P], kcT[r, h // 4, :],
                                          start=True, stop=True)
            mm.then_inc(cmp_s, 1)
            pe.wait_ge(cmp_p, 1)
            for g in range(BG):
                for t in range(NT):
                    mm = nc.tensor.transpose(acc[:, 2 + g // 2, 256 * (g % 2) + t * P:256 * (g % 2) + (t + 1) * P],
                                             pc.rearrange("p (t g c) -> p t g c", t=2, g=BG)[:, t, g, :], ident)
                if g % 2:
                    mm.then_inc(cmp_pt, 1)
            pe.wait_ge(cmp_pt_out, 2)
            first_scores_pe(pe, s)
            attention_pe(pe, s)
            pe.wait_ge(o_lo, s.pair0 + 8)
            out_pe(pe, s)

        def b_act(act, s):
            pre_act(act, s)
            for i in range(11):
                proj_act(act, s, i, evac_B(i))
                if i == 5:
                    act.wait_ge(proj_out, s.proj0 + 6)
                    act.wait_ge(zsh_clear, 1)
                    shift_rows(act, 0)
                if i == 6 or i == 8:
                    act.wait_ge(proj_out, s.proj0 + i + 1)
                    dup_keys(act, kT2, range(2 * (i - 6), 2 * (i - 6) + 4))
            for m in range(2):
                act.wait_ge(z_ready, m + 1)
                if m == 1:
                    act.wait_ge(a_used, s.a0 + 13)
                nc.scalar.activation(oT_hi[:, 0:4, :], zpos.rearrange("p (k t) -> p k t", k=4), ACT.Copy).then_inc(z_hi, 1)
                if m == 0:
                    shift_rows(act, 1)
                for q in range(2):
                    ahead_a(hi_slot_a, act, s.a0 + 11 + 2 * m + q + 2)
                act.wait_ge(a_used, s.a0 + 13 + 2 * m)
                h = hid if m == 0 else hid2
                for e in range(2):
                    ins = nc.scalar.activation(h[:, 64 * e:64 * e + 64], gu[:, e, 0:64], ACT.Gelu_apprx_tanh)
                ins.then_inc(cmp_hid, 1)
                act.wait_ge(cmp_kv, m + 1)
                dst = (kcT, vcb)[m]
                nc.scalar.activation(dst, tp[:, m, 0:(64, 256)[m]].rearrange("p (g n) -> p g n", g=BG), ACT.Copy)\
                    .then_inc(ckv_out, 1)
            act.wait_ge(cmp_sub, 1)
            pv = pc.rearrange("p (a c) -> p a c", c=32)[:, :, 0:16]
            nc.scalar.activation(pv, pv, ACT.Exp).then_inc(cmp_exp, 1)
            for q in range(2):
                act.wait_ge(cmp_pt, q + 1)
                nc.scalar.activation(pcT[:, 2 * q:2 * q + 2, :], acc[:, 2 + q, :].rearrange("p (g t) -> p g t", g=2),
                                     ACT.Copy).then_inc(cmp_pt_out, 1)
            attention_act(act, s, attention_steps(s))
            out_split(hi_slot_a, act, s)
            post_act(act, s, lambda: act.wait_ge(a_used, s.a0 + KINDS[s.kind][1]))

        def b_dve(dve, s):
            pre_dve(dve, s)
            nc.vector.memset(zsh, 0.0).then_inc(zsh_clear, 1)
            for i in range(11):
                ahead_a(lo_slot_a, dve, s.a0 + i + 2)
            dve.wait_ge(proj_out, s.proj0 + 11)
            nc.vector.tensor_scalar(gexp, gexp, 1.0, None, ALU.add)
            dve.drain()
            nc.vector.reciprocal(gates, gexp.rearrange("p (t c) -> p t c", t=2))
            z4 = zpos.rearrange("p (j g n) -> p j g n", j=CJ, g=BG)
            for m in range(2):
                dve.wait_ge(zsh_full, 16 * (8 + 8 * m))
                if m == 1:
                    dve.wait_ge(z_hi, 1)
                    dve.drain()
                for g in range(BG):
                    src = zsh[:, g, :].rearrange("p (n c) -> p c n", c=CMP_STRIDE)
                    for half in range(2):
                        pos = cols[:, 1, 48 + 16 * m + 8 * half:48 + 16 * m + 8 * half + 8].unsqueeze(2).broadcast_to([P, 8, 16])
                        ins = nc.vector.tensor_tensor(z4[:, 8 * half:8 * half + 8, g, :], src[:, 0:16:2, half:half + 16],
                                                      pos, ALU.add)
                ins.then_inc(z_ready, 1)
                dve.wait_ge(z_hi, m + 1)
                nc.vector.tensor_tensor(oT_lo[:, 0:4, :], zpos.rearrange("p (k t) -> p k t", k=4),
                                        oT_hi[:, 0:4, :].bitcast(F32), ALU.subtract).then_inc(z_lo, 1)
                for q in range(2):
                    ahead_a(lo_slot_a, dve, s.a0 + 11 + 2 * m + q + 2)
            dve.wait_ge(cmp_hid, 2)
            dve.wait_ge(cmp_kv, 1)
            nc.vector.memset(hidr, 0.0)
            dve.drain()
            hr = hidr.rearrange("p (e g h n) -> p e g h n", e=2, g=BG, h=4)
            for e in range(2):
                for g in range(BG):
                    c = 64 * e + 16 * g
                    ins = nc.vector.tensor_copy(hr[:, e, g, :, 0:16], hid2[:, c:c + 16].unsqueeze(1).broadcast_to([P, 4, 16]))
            ins.then_inc(hid_rep, 1)
            nc.vector.memset(pc, 0.0)
            dve.drain()
            dve.wait_ge(cmp_s, 1)
            p4 = pc.rearrange("p (t h c) -> p t h c", t=2, h=NH)
            mx = cmx.rearrange("p (t h) -> p t h", t=2)
            dn = cden.rearrange("p (t h) -> p t h", t=2)
            for t in range(NT):
                for e in range(2):
                    nc.vector.scalar_tensor_tensor(p4[:, t, e:NH:2, 0:16],
                                                   acc[:, 2 * t + e, 0:128].rearrange("p (h c) -> p h c", h=8), HD ** -0.5,
                                                   C("cmpbias")[:, 16 * t:16 * t + 16].unsqueeze(1).broadcast_to([P, 8, 16]),
                                                   ALU.mult, ALU.add)
            dve.drain()
            for t in range(NT):
                nc.vector.tensor_reduce(mx[:, t, :].unsqueeze(2), p4[:, t, :, 0:16], AX_X, ALU.max)
            dve.drain()
            for t in range(NT):
                ins = nc.vector.tensor_tensor(p4[:, t, :, 0:16], p4[:, t, :, 0:16],
                                              mx[:, t, :].unsqueeze(2).broadcast_to([P, NH, 16]), ALU.subtract)
            ins.then_inc(cmp_sub, 1)
            dve.wait_ge(cmp_exp, 1)
            for t in range(NT):
                nc.vector.tensor_tensor(p4[:, t, :, 0:16], p4[:, t, :, 0:16],
                                        C("cmpok")[:, 16 * t:16 * t + 16].unsqueeze(1).broadcast_to([P, NH, 16]), ALU.mult)
            dve.drain()
            for t in range(NT):
                nc.vector.tensor_reduce(dn[:, t, :].unsqueeze(2), p4[:, t, :, 0:16], AX_X, ALU.add)
            dve.drain()
            nc.vector.tensor_scalar(cden, cden, TINY, None, ALU.max)
            dve.drain()
            nc.vector.reciprocal(cden, cden)
            dve.drain()
            nc.vector.tensor_tensor(dn, dn, gates.rearrange("p t (h c) -> p t h c", c=3)[:, :, :, 0], ALU.mult)
            dve.drain()
            for t in range(NT):
                ins = nc.vector.tensor_tensor(p4[:, t, :, 0:16], p4[:, t, :, 0:16],
                                              dn[:, t, :].unsqueeze(2).broadcast_to([P, NH, 16]), ALU.mult)
            ins.then_inc(cmp_p, 1)
            attention_dve(dve, s, attention_steps(s))
            out_split(lo_slot_a, dve, s)
            post_dve(dve, s, None)

        def hybrid_pe(pe, s):
            L = s.layer
            pre_pe(pe, s)
            for i in range(14):
                if i == 13:
                    pe.wait_ge(rope_dve, 3 * L + 3)
                    first_scores_pe(pe, s)
                proj_pe(pe, s, i)
                if i == 3:
                    for r in range(3):
                        pe.wait_ge(proj_out, s.proj0 + r + 1)
                        if r == 2:
                            pe.wait_ge(rope_dve, 3 * L + 1)
                        src = qT1[:, 2 * r:2 * r + 2, :] if r < 2 else kraw1
                        nc.tensor.matmul(tp[:, r % 2, 0:(512 if r < 2 else 256)], C("rot"), src,
                                         start=True, stop=True).then_inc(rope_pe, 1)
            attention_pe(pe, s)
            ssd_pe(pe, s)
            turn_pe(pe, s.turn0 + 1, y)
            pe.wait_ge(turn_lo, 4 * s.turn0 + 8)
            out_pe(pe, s)

        def ssd_pe(pe, s):
            L = s.layer
            pe.wait_ge(silued, 6 * L + 6)
            pe.wait_ge(o_lo, s.pair0 + 4)
            for c in range(NT):
                for k in range(8):
                    mm = nc.tensor.transpose(acc[:, 2 * c + k // 4, (k % 4) * P:(k % 4 + 1) * P],
                                             conv[:, k, c * P:(c + 1) * P], ident)
                mm.then_inc(x_turned, 1)
            for g in range(SSM_GROUPS):
                nc.tensor.transpose(tp[:, 0, g * P:(g + 1) * P], conv[:, 8 + g, 0:P], ident)
            for c in range(NT):
                for g in range(SSM_GROUPS):
                    mm = nc.tensor.matmul(gu[:, 0, (2 * c + g) * P:(2 * c + g + 1) * P], conv[:, 8 + g, c * P:(c + 1) * P],
                                          conv[:, 10 + g, c * P:(c + 1) * P], start=True, stop=True)
            mm.then_inc(bc_ps, 1)
            pe.wait_ge(dt_done, L + 1)
            for c in range(NT):
                nc.tensor.matmul(tp[:, 1, 16 * c:16 * c + 16], C("triu"), da[:, 16 * c:16 * c + 16], start=True, stop=True)
            nc.tensor.matmul(tp[:, 1, 32:48], ones, da[:, 0:16], start=True, stop=True).then_inc(cs_ps, 1)
            pe.wait_ge(xs_act, L + 1)
            pe.wait_ge(xs_dve, L + 1)
            for c in range(NT):
                for q in range(4):
                    if c == 1:
                        pe.wait_ge(seg_ready, 8 * L + q + 1)
                    for e in range(4):
                        a = 16 * c + 4 * q + e
                        mm = nc.tensor.matmul(acc[:, q, e * P:(e + 1) * P], da[:, a:a + 1].broadcast_to([P, P]), C("triu"),
                                              start=True, stop=True)
                    mm.then_inc(row_ps, 1)
                if c == 0:
                    pe.wait_ge(xdec_ready, L + 1)
                    pe.wait_ge(bc_out, L + 1)
                    for g in range(SSM_GROUPS):
                        mm = nc.tensor.matmul(gu[:, g, :], btok[:, g, :], xdec[:, g * 512:(g + 1) * 512], start=True, stop=True)
                    mm.then_inc(state_ps, 1)
                pe.wait_ge(m_ready, 4 * L + 2 * c + 2)
                if c == 1:
                    pe.wait_ge(y_ready, 2 * L + 1)
                for h in range(SSM_HEADS):
                    mm = nc.tensor.matmul(tp[:, h // 8, (h % 8) * HD:(h % 8 + 1) * HD], mT[:, h, :],
                                          xdt[:, c, h * HD:(h + 1) * HD], start=True, stop=True)
                mm.then_inc(ydiag_ps, 1)
            pe.wait_ge(state_out, L + 1)
            for g in range(SSM_GROUPS):
                mm = nc.tensor.matmul(gu[:, g, :], conv[:, 10 + g, P:2 * P], st0[:, g * 512:(g + 1) * 512], start=True, stop=True)
            mm.then_inc(yoff_ps, 1)

        def hybrid_act(act, s):
            L = s.layer
            pre_act(act, s)

            def q(i):
                return lambda bank: nc.scalar.activation(qT1[:, 2 * i:2 * i + 2, :], bank.rearrange("p (u t) -> p u t", u=2), ACT.Copy)

            def kv(bank):
                nc.scalar.activation(kraw1, bank[:, 0:256], ACT.Copy)
                return nc.scalar.activation(v1, bank[:, 256:512].rearrange("p (t d) -> p t d", t=2), ACT.Copy)

            def xbc(i):
                def f(bank):
                    for e in range(2):
                        k = 2 * i + e
                        nc.scalar.activation(conv[:, k, :], bank[:, e * 256:(e + 1) * 256], ACT.Identity,
                                             bias=col(0, 96 + CT * L + k), scale=col(0, 4 * CT * L + 3 * CT + k))
                    return nc.scalar.activation(upad[:, 2 * i:2 * i + 2, 3:259], bank.rearrange("p (u t) -> p u t", u=2), ACT.Copy)
                return f

            def z(i):
                return lambda bank: nc.scalar.activation(zsil[:, :, 256 * i:256 * i + 256],
                                                         bank.rearrange("p (t d) -> p t d", t=2), ACT.Silu)

            def dtr(bank):
                return nc.scalar.activation(dt_raw.rearrange("p (t h) -> p t h", t=2),
                                            bank.rearrange("p (t d) -> p t d", t=2)[:, :, 0:16], ACT.Copy)

            for i in range(14):
                f = q(i) if i < 2 else kv if i == 2 else xbc(i - 3) if i < 9 else z(i - 9) if i < 13 else dtr
                if i == 13:
                    attention_act(act, s, attention_steps(s)[:1])
                proj_act(act, s, i, f)
                if 4 <= i <= 9:
                    k = i - 4
                    act.wait_ge(conved, 6 * L + k + 1)
                    nc.scalar.activation(conv[:, 2 * k:2 * k + 2, :], conv[:, 2 * k:2 * k + 2, :], ACT.Silu).then_inc(silued, 1)
                if i == 5:
                    act.wait_ge(rope_dve, 3 * L + 3)
                    dup_keys(act, kT1, (0, 1))
            attention_act(act, s, attention_steps(s)[1:])
            act.wait_ge(dt_neg, L + 1)
            nc.scalar.activation(dt_u, dt_u, ACT.Exp).then_inc(dt_exp, 1)
            act.wait_ge(dt_one, L + 1)
            nc.scalar.activation(dt_ln, dt_w, ACT.Ln).then_inc(dt_log, 1)
            act.wait_ge(x_turned, 2 * L + 1)
            nc.scalar.activation(xs[:, 0, :], accx[:, 0, :], ACT.Copy).then_inc(xs_act, 1)
            act.wait_ge(bc_ps, L + 1)
            nc.scalar.activation(btok, tp[:, 0, 0:256].rearrange("p (g n) -> p g n", g=2), ACT.Copy)
            nc.scalar.activation(cbT, gu[:, 0, :].rearrange("p (c g l) -> p c g l", c=2, g=2), ACT.Copy).then_inc(bc_out, 1)
            act.wait_ge(cs_out, L + 1)
            nc.scalar.activation(ecs1, cs[:, 16:32], ACT.Exp)
            nc.scalar.activation(dec0, csd, ACT.Exp).then_inc(decays, 1)
            for c in range(NT):
                for q4 in range(4):
                    act.wait_ge(seg_ready, 8 * L + 4 * c + q4 + 1)
                    m = mT[:, 4 * q4:4 * q4 + 4, :]
                    nc.scalar.activation(m, m, ACT.Exp).then_inc(seg_exp, 1)
                if c == 0:
                    act.wait_ge(state_ps, L + 1)
                    nc.scalar.activation(st0, gu[:, :, :].rearrange("p g n -> p (g n)"), ACT.Copy).then_inc(state_out, 1)
            act.wait_ge(y_ready, 2 * L + 2)
            e = 2 * (s.rms0 + 1)
            for c in range(NT):
                for g in range(SSM_GROUPS):
                    ins = nc.scalar.activation(xdt[:, c, g * 512:(g + 1) * 512], y[:, c, g * 512:(g + 1) * 512], ACT.Square,
                                               accum_out=ssg[:, 2 * c + g:2 * c + g + 1])
                ins.then_inc(sq_act, 1)
            turn_act(act, s.turn0 + 1, oT_hi, 4, ssm_col(s))
            out_split(hi_slot_a, act, s)

        def ssm_col(s):
            return lambda kt: col(1, 32 + 8 * s.layer + kt)

        def hybrid_dve(dve, s):
            L = s.layer
            pre_dve(dve, s)
            nc.vector.memset(upad[:, :, 0:3], 0.0)
            dve.drain()

            def rope():
                for r in range(3):
                    dve.wait_ge(rope_pe, 3 * L + r + 1)
                    n = 2 if r < 2 else 1
                    raw = qT1[:, 2 * r:2 * r + 2, :] if r < 2 else kraw1.unsqueeze(1)
                    t1, t2 = (ropet[:, e, 0:256 * n].rearrange("p (u t) -> p u t", u=n) for e in range(2))
                    nc.vector.tensor_tensor(t1, raw, cos.unsqueeze(1).broadcast_to([P, n, SEQ]), ALU.mult)
                    nc.vector.tensor_tensor(t2, tp[:, r % 2, 0:256 * n].rearrange("p (u t) -> p u t", u=n),
                                            sin.unsqueeze(1).broadcast_to([P, n, SEQ]), ALU.mult)
                    dve.drain()
                    if r < 2:
                        ins = nc.vector.tensor_tensor(qT1[:, 2 * r:2 * r + 2, :], t1, t2, ALU.add)
                    else:
                        nc.vector.tensor_tensor(kT1[0:64, 0, :], t1[0:64, 0, :], t2[0:64, 0, :], ALU.add)
                        ins = nc.vector.tensor_tensor(kT1[64:128, 1, :], t1[64:128, 0, :], t2[64:128, 0, :], ALU.add)
                    ins.then_inc(rope_dve, 1)
                    dve.drain()

            def taps(i):
                dve.wait_ge(proj_out, s.proj0 + 3 + i + 1)
                for tap in range(3):
                    for e in range(2):
                        k = 2 * i + e
                        ins = nc.vector.scalar_tensor_tensor(conv[:, k, :], upad[:, k, tap:tap + 256],
                                                             col(0, 4 * CT * L + CT * tap + k), conv[:, k, :],
                                                             ALU.mult, ALU.add)
                    if tap < 2:
                        dve.drain()
                ins.then_inc(conved, 1)

            for i in range(14):
                if i == 13:
                    attention_dve(dve, s, attention_steps(s)[:1])
                ahead_a(lo_slot_a, dve, s.a0 + i + 2)
                if i == 3:
                    rope()
                if 3 <= i < 9:
                    taps(i - 3)
            attention_dve(dve, s, attention_steps(s)[1:])
            dve.wait_ge(proj_out, s.proj0 + 14)

            def th(v):
                return v.rearrange("p (t h) -> p t h", t=2)

            nc.vector.tensor_tensor(th(dt_x), th(dt_raw), dtb[:, L, :].unsqueeze(1).broadcast_to([P, 2, 16]), ALU.add)
            dve.drain()
            nc.vector.tensor_scalar(dt_u, dt_x, -1.0, None, ALU.mult)
            dve.drain()
            nc.vector.tensor_tensor(dt_u, dt_u, dt_x, ALU.min).then_inc(dt_neg, 1)
            dve.wait_ge(dt_exp, L + 1)
            nc.vector.tensor_scalar(dt_w, dt_u, 1.0, None, ALU.add).then_inc(dt_one, 1)
            dve.drain()
            nc.vector.tensor_scalar(dt_e, dt_w, 1.0, None, ALU.is_equal)
            nc.vector.tensor_scalar(dt_d, dt_w, -1.0, None, ALU.add)
            dve.drain()
            nc.vector.tensor_tensor(dt_d, dt_d, dt_e, ALU.add)
            dve.drain()
            nc.vector.reciprocal(dt_d, dt_d)
            dve.wait_ge(dt_log, L + 1)
            nc.vector.tensor_tensor(dt_e, dt_e, dt_ln, ALU.add)
            dve.drain()
            nc.vector.tensor_tensor(dt_e, dt_e, dt_d, ALU.mult)
            dve.drain()
            nc.vector.tensor_tensor(dt_e, dt_e, dt_u, ALU.mult)
            dve.drain()
            nc.vector.scalar_tensor_tensor(dt, dt_x, 0.0, dt_e, ALU.max, ALU.add)
            dve.drain()
            nc.vector.scalar_tensor_tensor(th(da), th(dt), -1.0, apos[:, L, :].unsqueeze(1).broadcast_to([P, 2, 16]),
                                           ALU.mult, ALU.mult).then_inc(dt_done, 1)
            dve.wait_ge(x_turned, 2 * L + 2)
            nc.vector.tensor_copy(xs[:, 1, :], accx[:, 1, :]).then_inc(xs_dve, 1)
            dve.wait_ge(cs_ps, L + 1)
            nc.vector.tensor_copy(cs, tp[:, 1, 0:48])
            dve.drain()
            nc.vector.tensor_tensor(csd, cs[:, 32:48], cs[:, 0:16], ALU.subtract).then_inc(cs_out, 1)

            def heads(v):
                return v.rearrange("p (h d) -> p h d", d=HD)

            def per_head(v):
                return v.unsqueeze(2).broadcast_to([P, SSM_HEADS, HD])

            dve.wait_ge(xs_act, L + 1)
            dve.wait_ge(decays, L + 1)
            for c in range(NT):
                nc.vector.tensor_tensor(heads(xdt[:, c, :]), heads(xs[:, c, :]), per_head(dt[:, 16 * c:16 * c + 16]), ALU.mult)
            dve.drain()
            nc.vector.tensor_tensor(heads(xdec), heads(xdt[:, 0, :]), per_head(dec0), ALU.mult).then_inc(xdec_ready, 1)
            for c in range(NT):
                if c == 1:
                    dve.wait_ge(ydiag_ps, 2 * L + 1)
                for q4 in range(4):
                    dve.wait_ge(row_ps, 8 * L + 4 * c + q4 + 1)
                    for e in range(4):
                        h = 4 * q4 + e
                        ins = nc.vector.scalar_tensor_tensor(mT[:, h, :], acc[:, q4, e * P:(e + 1) * P],
                                                             cs[:, 16 * c + h:16 * c + h + 1], C("negtri"),
                                                             ALU.subtract, ALU.add)
                    ins.then_inc(seg_ready, 1)
                for g in range(SSM_GROUPS):
                    dve.wait_ge(seg_exp, 8 * L + 4 * c + 2 * g + 2)
                    m = mT[:, 8 * g:8 * g + 8, :]
                    nc.vector.tensor_tensor(m, m, cbT[:, c, g, :].unsqueeze(1).broadcast_to([P, 8, P]), ALU.mult).then_inc(m_ready, 1)
                dve.wait_ge(skip_ready, 2 * L + c + 1)
                dve.wait_ge(ydiag_ps, 2 * L + c + 1)
                nc.vector.tensor_tensor(y[:, c, :], tp[:, :, :].rearrange("p g n -> p (g n)"), y[:, c, :], ALU.add)
                dve.drain()
                if c == 1:
                    dve.wait_ge(yoff_ps, L + 1)
                    nc.vector.tensor_tensor(heads(xs[:, 1, :]), heads(gu[:, :, :].rearrange("p g n -> p (g n)")),
                                            per_head(ecs1), ALU.mult)
                    dve.drain()
                    nc.vector.tensor_tensor(y[:, 1, :], y[:, 1, :], xs[:, 1, :], ALU.add)
                    dve.drain()
                nc.vector.tensor_tensor(y[:, c, :], y[:, c, :], zsil[:, c, :], ALU.mult).then_inc(y_ready, 1)
            dve.wait_ge(sq_act, 2 * (s.rms0 + 1) + 2)
            nc.vector.tensor_scalar(ms[:, 4:8], ssg, float(SSM_GROUPS) / SSM_INNER, EPS1, ALU.mult, ALU.add).then_inc(ms_ready, 1)
            dve.wait_ge(rstd_ready, 2 * s.rms0 + 4)
            for c in range(NT):
                for g in range(SSM_GROUPS):
                    yy = y[:, c, g * 512:(g + 1) * 512]
                    ins = nc.vector.tensor_scalar(yy, yy, rstd[:, 4 + 2 * c + g:5 + 2 * c + g], None, ALU.mult)
                ins.then_inc(xn_ready, 1)
            turn_dve(dve, s.turn0 + 1, oT_hi, oT_lo, 4, ssm_col(s))
            out_split(lo_slot_a, dve, s)
            post_dve(dve, s, lambda: dve.wait_ge(a_used, s.a0 + 20))

        def skip_pool(pool, s):
            L = s.layer
            pool.wait_ge(xs_act, L + 1)
            pool.wait_ge(xs_dve, L + 1)
            for c in range(NT):
                nc.gpsimd.tensor_tensor(y[:, c, :].rearrange("p (h d) -> p h d", d=HD), xs[:, c, :].rearrange("p (h d) -> p h d", d=HD),
                                        dskip[:, L, :].unsqueeze(2).broadcast_to([P, SSM_HEADS, HD]), ALU.mult)\
                    .then_inc(skip_ready, 1)

        def flip_banks():
            return [acc[:, 0, :], acc[:, 1, :], acc[:, 2, :], acc[:, 3, :], gu[:, 0, :], gu[:, 1, :], tp[:, 0, :], tp[:, 1, :]]

        def final_sync(sp, s):
            load_gain(sp, s, T["final_norm"])
            sp.wait_ge(scratch_out, 16)
            src = bass.AP(scratch.tensor, 0, [[1, P], [384, NH], [1, 256]])
            sp.dma_start(bias_rev, src).then_inc(scratch_in, 16)

        def final_pe(pe, s):
            pe.wait_ge(x_ready, 2 * s.k)
            pe.wait_ge(scratch_in, 16)
            for b, bank in enumerate(flip_banks()):
                nc.tensor.matmul(bank, C("flip"), bias_rev[:, 2 * b:2 * b + 2, :], start=True, stop=True).then_inc(flip_ready, 1)

        def flip_out(copy, b):
            bank = flip_banks()[b].rearrange("p (h c) -> p h c", h=2)
            for c0, src in ((0, P), (P, 0), (2 * P, P)):
                ins = copy(bias[:, 2 * b:2 * b + 2, c0:c0 + P], bank[:, :, src:src + P])
            return ins

        def final_act(act, s):
            for t in range(NT):
                stage_start(act, s, t)
                rms_sum_act(act, s.rms0, t, x[:, t, :], D ** -0.5)
            for b in range(4, 8):
                act.wait_ge(flip_ready, b + 1)
                flip_out(lambda o, i: nc.scalar.activation(o, i, ACT.Copy), b).then_inc(flip_act, 1)

        def final_dve(dve, s):
            dve.wait_ge(gain_full, 16 * (s.gain0 + 1))
            for b in range(4):
                dve.wait_ge(flip_ready, b + 1)
                flip_out(nc.vector.tensor_copy, b)
            dve.wait_ge(flip_act, 4)
            for t in range(NT):
                dve.wait_ge(rstd_ready, 2 * s.rms0 + t + 1)
                o = 2 * (s.rms0 % 2) + t
                nc.vector.scalar_tensor_tensor(x[:, t, :], x[:, t, :], rstd[:, o:o + 1], gain_b, ALU.mult, ALU.mult)\
                    .then_inc(x_ready, 1)

        def setup_loads():
            yield const[:, :], T["constants"][:, 0:KEPT_COLS]
            yield setup_const, T["constants"][:, KEPT_COLS:CONST_COLS]
            yield x[:, :, :], T["x"][0].rearrange("(t p) d -> p t d", p=P)
            yield rows[0:96, 0, :], T["conv_w"].rearrange("l t (k c) -> (l t k) c", c=P)
            yield rows[96:120, 0, :], T["conv_b"].rearrange("l (k c) -> (l k) c", c=P)
            yield rows[0:16, 1, :], T["norm_mix"].rearrange("l (k c) -> (l k) c", c=P)
            yield rows[16:32, 1, :], T["norm_ffn"].rearrange("l (k c) -> (l k) c", c=P)
            yield rows[32:48, 1, :], T["ssm_norm"].rearrange("l (k c) -> (l k) c", c=P)
            yield rows[48:80, 1, :], T["b_cmp_pos_2"][0].rearrange("m (j l) d -> (m j) (l d)", l=2)
            for i in range(2):
                yield rows[0:96, 2 + i, :], T["norm_g_2"][2 * i:2 * i + 2].rearrange("l g (k c) -> (l g k) c", c=P)
            yield posb.bitcast(I32), T["positions"][0].partition_broadcast(P)
            for dst, name in ((dtb, "dt_bias"), (alog, "a_log"), (dskip, "d_skip"), (sinks, "a_sinks_2")):
                yield dst, T[name].partition_broadcast(P)
            yield rtab[0:NBUCKET, :], T["rel_bias_2"]

        LOADS = 17
        ROWS = (120, 80, 96, 96)

        def setup_pe(pe):
            pe.wait_ge(loaded, 16 * LOADS)
            for k, r in enumerate(ROWS):
                mm = nc.tensor.transpose(tp[:, 0, k * P:k * P + r], rows[0:r, k, :], ident[0:r, 0:r])
            mm.then_inc(cols_ps, 1)
            nc.tensor.matmul(tp[0:NH, 1, 0:384], rtab[0:NBUCKET, :], C("bucket", NBUCKET), start=True, stop=True).then_inc(rows_ps, 1)

        def setup_dve_(dve):
            nc.vector.memset(mhalf, -0.5)
            nc.vector.memset(ones, 1.0)
            dve.wait_ge(loaded, 16 * LOADS)
            posf, ang = setup_t[:, 0, :], setup_t[:, 1, :]
            nc.vector.tensor_copy(posf, posb.bitcast(I32))
            dve.drain()
            nc.vector.tensor_scalar(ang, posf, C("invf"), None, ALU.mult)
            dve.drain()
            two_pi = (6.28125, 0.0019340515136719, 1.2556659146e-6)
            nc.vector.tensor_scalar(setup_t[:, 3, :], ang, math.pi / 2, None, ALU.add)
            nc.vector.tensor_copy(setup_t[:, 2, :], ang)
            dve.drain()
            arg, turns_ = setup_t[:, 2:4, :], setup_t[:, 4:6, :]
            magic = 1.5 * 2.0 ** 23
            nc.vector.tensor_scalar(turns_, arg, 1.0 / (2 * math.pi), magic, ALU.mult, ALU.add)
            dve.drain()
            nc.vector.tensor_scalar(turns_, turns_, magic, None, ALU.subtract)
            dve.drain()
            for part in two_pi:
                nc.vector.scalar_tensor_tensor(arg, turns_, -part, arg, ALU.mult, ALU.add)
                dve.drain()
            nc.vector.tensor_scalar(arg, arg, 3.1415925, -3.1415925, ALU.min, ALU.max).then_inc(angles, 1)
            dve.wait_ge(cols_ps, 1)
            for k, r in enumerate(ROWS):
                nc.vector.tensor_copy(cols[:, k, 0:r], tp[:, 0, k * P:k * P + r])
            nc.vector.tensor_scalar(nsinks, sinks, -1.0, None, ALU.mult).then_inc(setup_dve, 1)
            dve.wait_ge(rows_ps, 1)
            nc.vector.tensor_tensor(bias_row[0:NH, :], tp[0:NH, 1, 0:384], C("future", NH), ALU.add).then_inc(bias_row_ready, 1)
            for n in range(2):
                lo_slot_a(dve, n)

        def setup_act_(act):
            act.wait_ge(loaded, 16 * LOADS)
            nc.scalar.activation(apos, alog, ACT.Exp)
            act.wait_ge(angles, 1)
            nc.scalar.activation(sin, setup_t[:, 2, :], ACT.Sin)
            nc.scalar.activation(cos, setup_t[:, 3, :], ACT.Sin).then_inc(setup_act, 1)
            for n in range(2):
                hi_slot_a(act, n)

        block = ctx.enter_context(nc.Block())

        @block.sync
        def _(sp):
            for dst, src in setup_loads():
                sp.dma_start(dst, src).then_inc(loaded, 16)
            for s in stages:
                {"ffn": ffn_sync, "final": final_sync}.get(s.kind, mixer_sync)(sp, s)
            sp.wait_ge(x_ready, 2 * len(stages))
            sp.dma_start(out[0].rearrange("(t p) d -> p t d", p=P), x[:, :, :]).then_inc(stored, 16)
            sp.wait_ge(stored, 16)

        @block.gpsimd
        def _(pool):
            if any(s.kind == "final" for s in stages):
                pool.wait_ge(bias_row_ready, 1)
                pool.dma_start(scratch, bias_row[0:NH, :]).then_inc(scratch_out, 16)
                pool.wait_ge(scratch_out, 16)
            for s in stages:
                rms_pow_pool(pool, s.rms0, eps_of(s))
                if s.kind == "hybrid":
                    skip_pool(pool, s)
                    pool.wait_ge(ms_ready, s.layer + 1)
                    nc.gpsimd.tensor_tensor(rstd[:, 4:8], ms[:, 4:8], mhalf[:, 0:4], ALU.pow).then_inc(rstd_ready, 2)
                elif s.kind != "final" and added_norm(s):
                    rms_pow_pool(pool, s.rms0 + 1, (4 if s.kind == "ffn" else 1) * EPS2)

        @block.scalar
        def _(act):
            setup_act_(act)
            for s in stages:
                {"ffn": ffn_act, "final": final_act, "hybrid": hybrid_act, "B": b_act}.get(s.kind, ac_act)(act, s)

        @block.vector
        def _(dve):
            setup_dve_(dve)
            for s in stages:
                {"ffn": ffn_dve, "final": final_dve, "hybrid": hybrid_dve, "B": b_dve}.get(s.kind, ac_dve)(dve, s)

        @block.tensor
        def _(pe):
            setup_pe(pe)
            for s in stages:
                {"ffn": ffn_pe, "final": final_pe, "hybrid": hybrid_pe, "B": b_pe}.get(s.kind, ac_pe)(pe, s)


NAMES = ("x", "positions", "norm_mix", "w_in", "conv_w", "conv_b", "dt_bias", "a_log", "d_skip", "ssm_norm", "w_out",
         "norm_ffn", "w_gate", "w_up", "w_down", "final_norm", "rel_bias_2", "norm_g_2", "ffn_w_in_2", "ffn_w_out_2",
         "a_w_in_2", "a_w_out_2", "a_sinks_2", "b_w_in_2", "b_w_out_2", "b_cmp_pos_2", "b_cmp_w1_2", "b_cmp_w2_2",
         "c_w_in_2", "c_w_out_2")


def kernel(**inputs):
    import concourse.bacc as bacc
    from concourse.bass_utils import run_bass_kernel_spmd

    nc = bacc.Bacc("TRN2", target_bir_lowering=False, num_devices=1)
    arrays = {f"in_{n}": np.ascontiguousarray(inputs[n]) for n in NAMES}
    arrays["in_constants"] = constants()
    T = {n[3:]: nc.dram_tensor(n, a.shape, mybir.dt.from_np(a.dtype), kind="ExternalInput").ap() for n, a in arrays.items()}
    out = nc.dram_tensor("out", (1, SEQ, D), F32, kind="ExternalOutput").ap()
    build_block(nc, T, out, plan_stages())
    return run_bass_kernel_spmd(nc, [arrays], core_ids=[0]).results[0]["out"]
```

```python
import math
from contextlib import ExitStack

import numpy as np

import concourse.bass as bass
from concourse import mybir

F32 = mybir.dt.float32
F32R = mybir.dt.float32r
I32 = mybir.dt.int32
ALU = mybir.AluOpType
ACT = mybir.ActivationFunctionType
AX_X = mybir.AxisListType.X

P = 128
SEQ = 256
NT = SEQ // P
D = 1024
KT = D // P
HD = 64
WARM_CMP = WARM_ATT = 12
FF = 2816
FT = FF // P
NEG = -1e30
TINY = 1e-30

H1, KV1 = 8, 2
SSM_INNER, SSM_HEADS, SSM_GROUPS, STATE, CONV_W = 1024, 16, 2, 128, 4
CONV_CH = SSM_INNER + 2 * SSM_GROUPS * STATE
CT = CONV_CH // P
EPG = SSM_HEADS // SSM_GROUPS
C_K = H1 * HD
C_Z = C_K + 2 * KV1 * HD
C_XBC = C_Z + SSM_INNER
C_DT = C_XBC + CONV_CH
ROPE_DIM, ROPE_THETA = HD // 4, 500000.0
EPS1 = 1e-5

NH = 16
EPS2 = 1e-6
BG = 4
CMP_LEN, CMP_STRIDE, CMP_HIDDEN = 32, 16, 256
NCMP = (SEQ - CMP_LEN) // CMP_STRIDE + 1
CJ = CMP_LEN * HD // P
NBUCKET, MAX_DIST = 32, 1024
A_WINDOW = 128

SLOT = 2048
SMALL = 1152
SLOT_B = 1024

CC = {}
_at = 0
for _name, _width in (("ident", 128), ("flip", 128), ("triu", 128), ("negtri", 128), ("rot", 128),
                      ("dilated", 384), ("window", 128), ("invf", 1), ("pad", 1), ("cmpbias", 32),
                      ("cmpok", 32), ("bucket", 384), ("future", 384)):
    CC[_name] = (_at, _at + _width)
    _at += _width
CONST_COLS = _at
KEPT_COLS = CC["bucket"][0]


def constants():
    c = np.zeros((P, CONST_COLS), np.float32)

    def put(name, value):
        a, b = CC[name]
        c[: value.shape[0], a:b] = value

    r = np.arange(P)
    put("ident", np.eye(P))
    put("flip", np.eye(P)[::-1])
    put("triu", (r[:, None] <= r[None, :]).astype(np.float32))
    put("negtri", np.where(r[:, None] <= r[None, :], 0.0, NEG))
    rot = np.zeros((P, P))
    half = ROPE_DIM // 2
    for m in range(P):
        if m % HD < half:
            rot[m + half, m] = -1.0
        elif m % HD < ROPE_DIM:
            rot[m - half, m] = 1.0
    put("rot", rot)
    blocks = []
    for t0, s0 in ((0, 0), (P, 0), (P, P)):
        d = (t0 + r[:, None]) - (s0 + r[None, :])
        n = ((d >= 0) & (d <= 128)).astype(int)
        n += (d >= 0) & (d % 4 == 0)
        n += (d >= 0) & (d % 16 == 0)
        blocks.append(np.where(n > 0, np.log(np.maximum(n, 1)), NEG))
    put("dilated", np.concatenate(blocks, axis=1))
    put("window", np.where(P + r[:, None] - r[None, :] < A_WINDOW, 0.0, NEG))
    f = (np.float32(ROPE_THETA) ** (-np.arange(0, ROPE_DIM, 2, dtype=np.float32) / np.float32(ROPE_DIM)))
    put("invf", np.array([f[p % HD % half] if p % HD < ROPE_DIM else 0.0 for p in range(P)])[:, None])
    end = np.arange(16) * CMP_STRIDE + CMP_LEN - 1
    ok = np.stack([(end[None, :] <= (t * P + r)[:, None]) & (np.arange(16) < NCMP) for t in range(NT)], axis=1)
    put("cmpok", ok.reshape(P, 32).astype(np.float32))
    put("cmpbias", np.where(ok, 0.0, NEG).reshape(P, 32))
    dist = 255 - np.arange(384)
    d = np.maximum(dist, 1).astype(np.float32)
    exact = NBUCKET // 2
    logb = exact + (np.log(d / np.float32(exact)) / np.float32(math.log(MAX_DIST / exact))
                    * np.float32(NBUCKET - exact)).astype(np.int32)
    bucket = np.where(dist < exact, dist, np.minimum(logb, NBUCKET - 1))
    hot = (np.arange(NBUCKET)[:, None] == bucket[None, :]) & (dist >= 0)[None, :]
    put("bucket", hot.astype(np.float32))
    put("future", np.broadcast_to(np.where(dist >= 0, 0.0, NEG), (P, 384)))
    return c


class Stage:

    def __init__(self, kind, block=0, layer=0, half=0, j=0):
        self.kind, self.block, self.layer, self.half, self.j = kind, block, layer, half, j


def plan_stages():
    st = []
    for l in range(2):
        st.append(Stage("hybrid", layer=l))
        st.append(Stage("ffn", block=1, layer=l, half=0))
    st.append(Stage("final"))
    for i in range(4):
        st.append(Stage("ffn", block=2, layer=i, half=0))
        st.append(Stage("ABCA"[i], layer=i, j=i // 3))
        st.append(Stage("ffn", block=2, layer=i, half=1))
    return st


KINDS = {
    "hybrid": (14, 20, 4, 4, 2, 2),
    "A": (5, 9, 8, 8, 1, 2),
    "B": (11, 19, 16, 8, 1, 2),
    "C": (12, 16, 8, 8, 1, 2),
}


DUPS = {"hybrid": 2, "A": 2, "B": 8, "C": 0}
HY_SLOTS = (("q", 0), ("q", 1), ("kv", 0), ("xbc", 0), ("z", 0), ("xbc", 1), ("z", 1), ("xbc", 2), ("xbc", 3), ("z", 2),
            ("xbc", 4), ("xbc", 5), ("dt", 0), ("z", 3))
HY_ROPES = {4: (0, 3), 6: (1, 5), 9: (2, 8)}
OUT_SLOTS = {"hybrid": 6, "A": 4, "B": 4, "C": 4}


def build_block(nc, T, out, stages):
    a = b = units = pairs = turns = rms = proj = gains = dups = outs = 0
    for k, s in enumerate(stages):
        s.k = k
        s.a0, s.b0, s.unit0, s.pair0, s.turn0, s.rms0, s.proj0 = a, b, units, pairs, turns, rms, proj
        s.gain0, s.dup0, s.out0 = gains, dups, outs
        outs += s.kind != "final"
        if s.kind == "ffn":
            a, b, turns, rms = a + FT, b + FT, turns + 1, rms + 1 + (s.block == 2)
            gains += s.block == 2
        elif s.kind == "final":
            rms, gains = rms + 1, gains + 1
        else:
            n = KINDS[s.kind]
            proj, a, units, pairs, turns, rms = proj + n[0], a + n[1], units + n[2], pairs + n[3], turns + n[4], rms + n[5]
            gains += s.kind != "hybrid"
            dups += DUPS[s.kind]
    A_TOTAL, B_TOTAL = a, b

    ctx = ExitStack()
    with ctx:
        def sb(name, shape, dt=F32):
            return ctx.enter_context(nc.sbuf_tensor(name, shape, dt))

        def sem(name):
            return ctx.enter_context(nc.semaphore(name))

        x = sb("x", [P, NT, D])
        xT_hi, xT_lo = sb("xT_hi", [P, KT, SEQ], F32R), sb("xT_lo", [P, KT, SEQ], F32R)
        oT_hi, oT_lo = sb("oT_hi", [P, 12, SEQ], F32R), sb("oT_lo", [P, 12, SEQ], F32R)
        raw_a = sb("raw_a", [P, 2, SLOT])
        hi_a, lo_a = sb("hi_a", [P, 2, SLOT], F32R), sb("lo_a", [P, 2, SLOT], F32R)
        raw_b = sb("raw_b", [P, 2, SLOT_B])
        hi_b, lo_b = sb("hi_b", [P, 2, SLOT_B], F32R), sb("lo_b", [P, 2, SLOT_B], F32R)
        h_hi, h_lo = sb("h_hi", [P, 2, SEQ], F32R), sb("h_lo", [P, 2, SEQ], F32R)
        const = sb("const", [P, KEPT_COLS])
        cols = sb("cols", [P, 4, P])
        small = sb("small", [P, SMALL])
        arena = sb("arena", [P, 18432])

        def C(name, rows=P):
            lo, hi = CC[name]
            if lo >= KEPT_COLS:
                return setup_const[0:rows, lo - KEPT_COLS:hi - KEPT_COLS]
            return const[0:rows, lo:hi]

        ident = C("ident")
        n_small = [0]

        def sm(width):
            n_small[0] += width
            assert n_small[0] <= SMALL
            return small[:, n_small[0] - width:n_small[0]]

        def ar(at, width):
            assert at + width <= 18432
            return arena[:, at:at + width]

        xn = ar(6144, 2048).rearrange("p (t d) -> p t d", t=NT)
        gain_b = ar(8192, 1024)
        bias = ar(0, 6144).rearrange("p (h c) -> p h c", h=NH)
        qT2 = ar(9216, 2048).rearrange("p (u t) -> p u t", u=8)
        kT2 = ar(11264, 2048).rearrange("p (u t) -> p u t", u=8)
        v2 = ar(13312, 2048).rearrange("p (t d) -> p t d", t=NT)
        probs = [ar(at, 768).rearrange("p (h c) -> p h c", h=2) for at in (15360, 16128, 6144)]
        probT = ar(16896, 1536).rearrange("p (b c) -> p b c", b=2)
        junk = ar(16896, 1024)
        sg = ar(15360, 512).rearrange("p (b t) -> p b t", b=2)
        hh32 = ar(15872, 512).rearrange("p (b t) -> p b t", b=2)
        v2b = ar(13312, 1024).rearrange("p (t d) -> p t d", t=NT)
        w2dup = ar(14336, 512).rearrange("p (m e d) -> p m e d", m=2, e=2)
        kcd = ar(16384, 128).rearrange("p (g h n) -> p g h n", g=BG, h=2)
        vcb = ar(14912, 256).rearrange("p (g d) -> p g d", g=BG)
        gates = ar(15168, 96).rearrange("p (t c) -> p t c", t=NT)
        craw = ar(15360, 1024).rearrange("p (m u t) -> p m u t", m=2, u=2)
        zsh = ar(16896, 4 * 272).rearrange("p (g t) -> p g t", g=BG)
        zpos = [ar(6144, 1024), ar(7168, 1024)]
        hidt = ar(15360, 512).rearrange("p (m c) -> p m c", m=2)
        hidr = ar(7168, 1024)
        pc = ar(6144, 1024)
        pcT = ar(7168, 1024).rearrange("p (g t) -> p g t", g=BG)
        zsil = ar(0, 2048).rearrange("p (t d) -> p t d", t=NT)
        upad = ar(2048, CT * 260).rearrange("p (c t) -> p c t", c=CT)
        cos = ar(5168, 256)
        sin = ar(5424, 256)
        conv = ar(8192, CT * SEQ).rearrange("p (c t) -> p c t", c=CT)
        qT1 = ar(11264, 1024).rearrange("p (u t) -> p u t", u=4)
        kraw1 = ar(12288, 256)
        kT1 = ar(12544, 512).rearrange("p (u t) -> p u t", u=2)
        v1 = ar(13056, 256).rearrange("p (t d) -> p t d", t=NT)
        xs = ar(13312, 2048).rearrange("p (t d) -> p t d", t=NT)
        ropet = ar(15360, 1024).rearrange("p (a c) -> p a c", a=2)
        mTs = [ar(at, 2048).rearrange("p (h l) -> p h l", h=SSM_HEADS) for at in (2048, 8192)]
        cbT = ar(4096, 512).rearrange("p (c g l) -> p c g l", c=NT, g=SSM_GROUPS)
        btok = ar(4608, 256).rearrange("p (g n) -> p g n", g=SSM_GROUPS)
        xdt = ar(15360, 2048).rearrange("p (t d) -> p t d", t=NT)
        st0 = ar(17408, 1024)
        xdec = ar(11264, 1024)
        y = xn
        rows = ar(0, 512).rearrange("p (k c) -> p k c", k=4)
        posb = ar(512, 256)
        setup_const = ar(11264, CONST_COLS - KEPT_COLS)
        setup_t = ar(1024, 1536).rearrange("p (k c) -> p k c", k=6)
        bias_rev = ar(9216, 16 * 256).rearrange("p (h c) -> p h c", h=NH)
        bias_row = ar(15360, 384)

        ss = sm(8)
        ms = sm(8)
        rstd = sm(8)
        mhalf = sm(8)
        ssg = sm(4)
        nmax = sm(8).rearrange("p (b c) -> p b c", b=2)
        den = sm(8).rearrange("p (b c) -> p b c", b=2)
        rden = sm(8).rearrange("p (b c) -> p b c", b=2)
        esink = sm(8).rearrange("p (b c) -> p b c", b=2)
        sarg = sm(8).rearrange("p (b c) -> p b c", b=2)
        sinks = sm(32).rearrange("p (j h) -> p j h", j=2)
        nsinks = sm(32).rearrange("p (j h) -> p j h", j=2)
        dtb, alog, dskip = (sm(32).rearrange("p (l h) -> p l h", l=2) for _ in range(3))
        apos = sm(32).rearrange("p (l h) -> p l h", l=2)
        dt_raw, dt_x, dt_u, dt_w, dt_ln, dt_e, dt_d, dt, da = (sm(32) for _ in range(9))
        cs = sm(48)
        csd = sm(16)
        ecs1, dec0 = sm(16), sm(16)
        ones = sm(128)
        hid2 = sm(128)
        cmx, cden = sm(32), sm(32)
        rtab = sm(16)
        gexp = sm(96)

        acc = ctx.enter_context(nc.psum_tensor("acc", [P, 4, 512], F32))
        gu = ctx.enter_context(nc.psum_tensor("gu", [P, 2, 512], F32))
        tp = ctx.enter_context(nc.psum_tensor("tp", [P, 2, 512], F32))
        accx = acc[:, :, :].rearrange("p (t h) n -> p t (h n)", t=NT)

        a_full = [sem("a_full0"), sem("a_full1")]
        b_full = [sem("b_full0"), sem("b_full1")]
        a_hi, a_lo, a_used = sem("a_hi"), sem("a_lo"), sem("a_used")
        b_hi, b_lo, b_used = sem("b_hi"), sem("b_lo"), sem("b_used")
        x_ready = sem("x_ready")
        loaded, cols_ps, rows_ps = sem("loaded"), sem("cols_ps"), sem("rows_ps")
        angles, setup_dve, setup_act, bias_row_ready = sem("angles"), sem("setup_dve"), sem("setup_act"), sem("bias_row_ready")
        scratch_out, scratch_in = sem("scratch_out"), sem("scratch_in")
        out_half = sem("out_half")
        sq_act, rstd_ready = sem("sq_act"), sem("rstd_ready")
        xn_ready, turned, turn_hi, turn_lo = sem("xn_ready"), sem("turned"), sem("turn_hi"), sem("turn_lo")
        hid_gate, hid_ready, hid_hi, hid_lo = sem("hid_gate"), sem("hid_ready"), sem("hid_hi"), sem("hid_lo")
        gain_full = sem("gain_full")
        proj_ready, proj_out = sem("proj_ready"), sem("proj_out")
        k_dup = sem("k_dup")
        score_ready, soft_ready, exp_ready, rden_ready, prob_ready = sem("score_ready"), sem("soft_ready"), sem("exp_ready"), sem("rden_ready"), sem("prob_ready")
        pt_ready, pt_act, pt_dve = sem("pt_ready"), sem("pt_act"), sem("pt_dve")
        o_ready, o_hi, o_lo = sem("o_ready"), sem("o_hi"), sem("o_lo")
        rope_pe, rope_dve = sem("rope_pe"), sem("rope_dve")
        conved, silued = sem("conved"), sem("silued")
        x_turned, xs_act, xs_dve, bc_half, bc_out = sem("x_turned"), sem("xs_act"), sem("xs_dve"), sem("bc_half"), sem("bc_out")
        dt_neg, dt_exp, dt_one, dt_log, dt_done = sem("dt_neg"), sem("dt_exp"), sem("dt_one"), sem("dt_log"), sem("dt_done")
        cs_ps, cs_out, decays, xdec_ready = sem("cs_ps"), sem("cs_out"), sem("decays"), sem("xdec_ready")
        row_ps, seg_ready, seg_exp, m_ready = sem("row_ps"), sem("seg_ready"), sem("seg_exp"), sem("m_ready")
        state_ps, state_out, ydiag_ps, yoff_ps = sem("state_ps"), sem("state_out"), sem("ydiag_ps"), sem("yoff_ps")
        skip_ready, y_ready = sem("skip_ready"), sem("y_ready")
        zsh_clear, zsh_full, w2_full = sem("zsh_clear"), sem("zsh_full"), sem("w2_full")
        z_ready, z_hi, z_lo = sem("z_ready"), sem("z_hi"), sem("z_lo")
        cmp_hid, hid_turned, hid_out, hid_rep = sem("cmp_hid"), sem("hid_turned"), sem("hid_out"), sem("hid_rep")
        cmp_kv, ckv_out = sem("cmp_kv"), sem("ckv_out")
        cmp_s, cmp_sub, cmp_exp, cmp_p = sem("cmp_s"), sem("cmp_sub"), sem("cmp_exp"), sem("cmp_p")
        cmp_pt, cmp_pt_out = sem("cmp_pt"), sem("cmp_pt_out")
        flip_ready, flip_act = sem("flip_ready"), sem("flip_act")
        stored = sem("stored")

        scratch = nc.dram_tensor("bias_rows", (NH, 384), F32).ap()

        def slot_sources(s, i):
            w_in = {"hybrid": "w_in", "A": "a_w_in_2", "B": "b_w_in_2", "C": "c_w_in_2"}[s.kind]
            w_out = {"hybrid": "w_out", "A": "a_w_out_2", "B": "b_w_out_2", "C": "c_w_out_2"}[s.kind]
            l = s.layer if s.kind == "hybrid" else s.j if s.kind == "A" else 0
            n_proj = KINDS[s.kind][0]
            n_all = KINDS[s.kind][1]
            n_out = OUT_SLOTS[s.kind]
            if i < n_proj:
                c0, width = proj_columns(s, i)
                src = T[w_in][l].rearrange("(k p) n -> p k n", p=P)[:, :, c0:c0 + width]
                return [(k0, width, src[:, k0:k0 + 4, :]) for k0 in (0, 4)]
            if i < n_all - n_out:
                m, half = (i - n_proj) // 2, (i - n_proj) % 2
                src = T["b_cmp_w1_2"][0, m].rearrange("(k p) n -> p k n", p=P)[:, half * 8:half * 8 + 8, :]
                return [(k0, 256, src[:, k0:k0 + 4, :]) for k0 in (0, 4)]
            r = 2 * (i - (n_all - n_out))
            src = T[w_out][l].rearrange("(k p) n -> p k n", p=P)
            return [(4 * e, 256, src[:, r + e, :].rearrange("p (k n) -> p k n", k=4)) for e in range(2)]

        def proj_columns(s, i):
            if s.kind == "hybrid":
                kind, r = HY_SLOTS[i]
                first = {"q": 0, "kv": C_K, "xbc": C_XBC, "z": C_Z, "dt": C_DT}[kind]
                return first + 256 * r, SSM_HEADS if kind == "dt" else 256
            if s.kind == "B" and i == 10:
                return 2560, 48
            if s.kind == "B" and i < 6:
                return 256 * (4, 5, 0, 1, 2, 3)[i], 256
            if s.kind == "A":
                return 256 * (0, 4, 1, 2, 3)[i], 256
            return 256 * i, 256

        def slot_words(s, i):
            return proj_columns(s, i)[1] if i < KINDS[s.kind][0] else 256

        def a_view(buf, n):
            return buf[:, n % 2, :].rearrange("p (k n) -> p k n", k=8)

        def stage_slot(n):
            for s in stages:
                if s.kind != "final" and s.a0 <= n < s.a0 + (FT if s.kind == "ffn" else KINDS[s.kind][1]):
                    return s, n - s.a0
            return None, 0

        def hi_slot_a(act, n, width=256, par=None):
            par = n % 2 if par is None else par
            act.wait_ge(a_full[par], fills(n, par, 32))
            if not isinstance(n, int) or n >= 2:
                act.wait_ge(a_used, n - 1)
            nc.scalar.activation(a_view(hi_a, par)[:, :, 0:width], a_view(raw_a, par)[:, :, 0:width],
                                 ACT.Copy).then_inc(a_hi, 1)

        def fills(n, par, per):
            if isinstance(n, int):
                return per * (n // 2 + 1)
            return n * (per // 2) + (2 - par) * (per // 2)

        def lo_slot_a(dve, n, width=256, par=None):
            par = n % 2 if par is None else par
            dve.wait_ge(a_hi, n + 1)
            nc.vector.tensor_tensor(a_view(lo_a, par)[:, :, 0:width], a_view(raw_a, par)[:, :, 0:width],
                                    a_view(hi_a, par)[:, :, 0:width].bitcast(F32), ALU.subtract).then_inc(a_lo, 1)

        def hi_slot_b(act, m, par):
            act.wait_ge(b_full[par], fills(m, par, 16))
            if not isinstance(m, int) or m >= 2:
                act.wait_ge(b_used, m - 1)
            nc.scalar.activation(hi_b[:, par, :], raw_b[:, par, :], ACT.Copy).then_inc(b_hi, 1)

        def lo_slot_b(dve, m, par):
            dve.wait_ge(b_hi, m + 1)
            nc.vector.tensor_tensor(lo_b[:, par, :], raw_b[:, par, :], hi_b[:, par, :].bitcast(F32),
                                    ALU.subtract).then_inc(b_lo, 1)

        def ahead_a(split, eng, n):
            s, i = stage_slot(n)
            if s is not None:
                split(eng, n, 256 if s.kind == "ffn" else slot_words(s, i))

        def rms_sum_act(act, e, t, src, scale):
            act.drain()
            o = 2 * (e % 2) + t
            nc.scalar.activation(junk, src, ACT.Square, scale=scale, accum_out=ss[:, o:o + 1]).then_inc(sq_act, 1)

        def rms_pow_pool(pool, e, eps):
            for t in range(NT):
                pool.wait_ge(sq_act, 2 * e + t + 1)
                o = 2 * (e % 2) + t
                nc.gpsimd.tensor_scalar(ms[:, o:o + 1], ss[:, o:o + 1], eps, None, ALU.add)
                pool.drain()
                nc.gpsimd.tensor_tensor(rstd[:, o:o + 1], ms[:, o:o + 1], mhalf[:, 0:1], ALU.pow).then_inc(rstd_ready, 1)

        turn_acc = [acc[:, q, :] for q in range(4)]
        turn_others = [gu[:, 0, :], gu[:, 1, :], tp[:, 0, :], tp[:, 1, :]]

        def turn_pe(pe, t, src, banks=turn_acc):
            for tt in range(NT):
                pe.wait_ge(xn_ready, 2 * t + tt + 1)
                for kt in range(KT):
                    mm = nc.tensor.transpose(banks[kt // 2][:, (kt % 2) * 256 + tt * P:(kt % 2) * 256 + (tt + 1) * P],
                                             src[:, tt, kt * P:(kt + 1) * P], ident)
                    if tt and kt % 2:
                        mm.then_inc(turned, 1)

        def turn_act(act, t, dst, k0, col, banks=turn_acc):
            for q in range(4):
                g = 4 * t + q
                act.wait_ge(turned, g + 1)
                for e in range(2):
                    kt = 2 * q + e
                    ins = nc.scalar.activation(dst[:, k0 + kt, :], banks[q][:, e * 256:(e + 1) * 256],
                                               ACT.Copy, scale=col(kt))
                ins.then_inc(turn_hi, 1)

        def turn_dve(dve, t, hi, lo, k0, col, banks=turn_acc):
            for q in range(4):
                g = 4 * t + q
                dve.wait_ge(turn_hi, g + 1)
                for e in range(2):
                    kt = 2 * q + e
                    ins = nc.vector.scalar_tensor_tensor(lo[:, k0 + kt, :], banks[q][:, e * 256:(e + 1) * 256],
                                                         col(kt), hi[:, k0 + kt, :].bitcast(F32), ALU.mult, ALU.subtract)
                ins.then_inc(turn_lo, 1)

        def col(k, r):
            return cols[:, k, r:r + 1]

        def pre_col(s):
            if s.kind == "hybrid":
                return lambda kt: col(1, 8 * s.layer + kt)
            if s.kind == "ffn" and s.block == 1:
                return lambda kt: col(1, 16 + 8 * s.layer + kt)
            which = 2 if s.kind != "ffn" else 4 * s.half
            r = (s.layer % 2) * 48 + which * 8
            return lambda kt: col(2 + s.layer // 2, r + kt)

        def eps_of(s):
            return EPS1 if s.kind == "hybrid" or (s.kind == "ffn" and s.block == 1) or s.kind == "final" else EPS2

        def post_gain(s):
            return T["norm_g_2"][s.layer, 3 if s.kind != "ffn" else 1 + 4 * s.half]

        def stage_start(eng, s, t):
            if s.k:
                eng.wait_ge(x_ready, 2 * s.k - 1 + t)
            elif t == 0:
                eng.wait_ge(loaded, 16 * LOADS)
                eng.wait_ge(setup_dve, 1)
                eng.wait_ge(setup_act, 1)

        def pre_act(act, s):
            for t in range(NT):
                stage_start(act, s, t)
                rms_sum_act(act, s.rms0, t, x[:, t, :], D ** -0.5)
            turn_act(act, s.turn0, xT_hi, 0, pre_col(s))

        def pre_dve(dve, s):
            for t in range(NT):
                dve.wait_ge(rstd_ready, 2 * s.rms0 + t + 1)
                o = 2 * (s.rms0 % 2) + t
                nc.vector.tensor_scalar(xn[:, t, :], x[:, t, :], rstd[:, o:o + 1], None, ALU.mult).then_inc(xn_ready, 1)
            turn_dve(dve, s.turn0, xT_hi, xT_lo, 0, pre_col(s))

        def keep_warm(n):
            for _ in range(n):
                nc.tensor.matmul(tp[:, 0, 0:P], ident, C("flip"), start=True, stop=True)

        def pre_pe(pe, s):
            if s.k:
                if stages[s.k - 1].kind != "final":
                    keep_warm(20)
                pe.wait_ge(x_ready, 2 * s.k)
            turn_pe(pe, s.turn0, xn)

        def added_norm(s):
            return not (s.kind == "hybrid" or (s.kind == "ffn" and s.block == 1))

        def post_act(act, s, done):
            if not added_norm(s):
                return
            for t in range(NT):
                if t == 0:
                    act.wait_ge(out_half, s.out0 + 1)
                else:
                    done()
                rms_sum_act(act, s.rms0 + 1, t, accx[:, t, :], D ** -0.5 * (2 if s.kind == "ffn" else 1))

        def post_dve(dve, s, done):
            if not added_norm(s):
                for t in range(NT):
                    if t == 0:
                        dve.wait_ge(out_half, s.out0 + 1)
                    else:
                        done()
                    nc.vector.tensor_tensor(x[:, t, :], accx[:, t, :], x[:, t, :], ALU.add).then_inc(x_ready, 1)
                return
            e = s.rms0 + 1
            dve.wait_ge(gain_full, 16 * (s.gain0 + 1))
            for t in range(NT):
                o = 2 * (e % 2) + t
                dve.wait_ge(sq_act, 2 * e + 1 + t)
                nc.vector.tensor_tensor(xn[:, t, :], accx[:, t, :], gain_b, ALU.mult)
                dve.drain()
                dve.wait_ge(rstd_ready, 2 * e + 1 + t)
                nc.vector.scalar_tensor_tensor(x[:, t, :], xn[:, t, :], rstd[:, o:o + 1], x[:, t, :],
                                               ALU.mult, ALU.add).then_inc(x_ready, 1)

        def first_products(pe, s, bank, w_hi, w_lo):
            for q in range(4):
                for part in range(3):
                    if part < 2:
                        pe.wait_ge((turn_hi, turn_lo)[part], 4 * s.turn0 + q + 1)
                    for e in range(2):
                        o = bank[:, e * 256:(e + 1) * 256]
                        for kt in (2 * q, 2 * q + 1):
                            w = (w_lo if part == 2 else w_hi)[:, kt, e * P:(e + 1) * P]
                            mm = nc.tensor.matmul(o, w, (xT_lo if part == 1 else xT_hi)[:, kt, :], start=(part == 0 and e == 0 and kt == 0),
                                                  stop=(part == 2 and e == 1 and kt == KT - 1))
            return mm

        def ffn_in_pe(pe, s, n, m, pa, pm, first=False):
            pe.wait_ge(a_hi, n + 1)
            if not isinstance(m, int) or m >= 2:
                pe.wait_ge(hid_ready, m - 1)
            w_hi, w_lo = a_view(hi_a, pa), a_view(lo_a, pa)
            if first:
                pe.wait_ge(a_lo, n + 1)
                first_products(pe, s, gu[:, pm, :], w_hi, w_lo).then_inc(a_used, 1)
                return
            for e in range(2):
                o = gu[:, pm, e * 256:(e + 1) * 256]
                for kt in range(KT):
                    w = w_hi[:, kt, e * P:(e + 1) * P]
                    nc.tensor.matmul(o, w, xT_hi[:, kt, :], start=(kt == 0), stop=False)
                    nc.tensor.matmul(o, w, xT_lo[:, kt, :], start=False, stop=False)
                if e == 0:
                    pe.wait_ge(a_lo, n + 1)
                for kt in range(KT):
                    mm = nc.tensor.matmul(o, w_lo[:, kt, e * P:(e + 1) * P], xT_hi[:, kt, :], start=False, stop=(kt == KT - 1))
            mm.then_inc(a_used, 1)

        def down_pe(lhs_hi, lhs_lo, w_hi, w_lo, start, stop):
            for t in range(NT):
                for i, (l, w) in enumerate(((lhs_hi, w_hi), (lhs_hi, w_lo), (lhs_lo, w_hi))):
                    for c in range(2):
                        mm = nc.tensor.matmul(acc[:, 2 * t + c, :], l[:, t * P:(t + 1) * P], w[:, c * 512:(c + 1) * 512],
                                              start=(start and i == 0), stop=(stop and i == 2))
                if stop and t == 0:
                    mm.then_inc(out_half, 1)
            return mm

        def ffn_out_pe(pe, m, pm, start=False, stop=False):
            pe.wait_ge(hid_lo, m + 1)
            pe.wait_ge(b_lo, m + 1)
            down_pe(h_hi[:, pm, :], h_lo[:, pm, :], hi_b[:, pm, :], lo_b[:, pm, :], start, stop).then_inc(b_used, 1)

        def ffn_pe(pe, s):
            pre_pe(pe, s)
            ffn_in_pe(pe, s, s.a0, s.b0, s.a0 % 2, 0, first=True)
            ffn_in_pe(pe, s, s.a0 + 1, s.b0 + 1, (s.a0 + 1) % 2, 1)
            ffn_out_pe(pe, s.b0, 0, start=True)
            with pe.Fori(1, FT // 2) as i:
                for e in range(2):
                    ffn_in_pe(pe, s, 2 * i + (s.a0 + e), 2 * i + (s.b0 + e), (s.a0 + e) % 2, e)
                    ffn_out_pe(pe, 2 * i + (s.b0 + e - 1), 1 - e)
            ffn_out_pe(pe, s.b0 + FT - 1, 1, stop=True)

        def ffn_tile_act(act, n, m, pa, pm, more_a, more_b):
            act.wait_ge(a_used, n + 1)
            if not isinstance(m, int) or m >= 2:
                act.wait_ge(hid_ready, m - 1)
            nc.scalar.activation(sg[:, pm, :], gu[:, pm, 0:256], ACT.Silu).then_inc(hid_gate, 1)
            if more_a and more_b:
                hi_slot_a(act, n + 2, par=pa)
            act.wait_ge(hid_ready, m + 1)
            if not isinstance(m, int) or m >= 2:
                act.wait_ge(b_used, m - 1)
            nc.scalar.activation(h_hi[:, pm, :], hh32[:, pm, :], ACT.Copy).then_inc(hid_hi, 1)
            if more_b:
                hi_slot_b(act, m + 1, 1 - pm)
            elif more_a:
                hi_slot_a(act, n + 2, par=pa)

        def ffn_tile_dve(dve, n, m, pa, pm, more_a, more_b):
            dve.wait_ge(hid_gate, m + 1)
            if not isinstance(m, int) or m >= 2:
                dve.wait_ge(hid_lo, m - 1)
                dve.wait_ge(hid_hi, m - 1)
            nc.vector.tensor_tensor(hh32[:, pm, :], sg[:, pm, :], gu[:, pm, 256:512], ALU.mult).then_inc(hid_ready, 1)
            if more_a and more_b:
                lo_slot_a(dve, n + 2, par=pa)
            dve.wait_ge(hid_hi, m + 1)
            nc.vector.tensor_tensor(h_lo[:, pm, :], hh32[:, pm, :], h_hi[:, pm, :].bitcast(F32), ALU.subtract)\
                .then_inc(hid_lo, 1)
            if more_b:
                lo_slot_b(dve, m + 1, 1 - pm)
            elif more_a:
                lo_slot_a(dve, n + 2, par=pa)

        def ffn_tiles(eng, s, split_b, tile):
            split_b(eng, s.b0, 0)

            def pair(i, more_a, end):
                for e in range(2):
                    tile(eng, 2 * i + (s.a0 + e), 2 * i + (s.b0 + e), (s.a0 + e) % 2, e, more_a, not (end and e))

            pair(0, True, False)
            with eng.Fori(1, FT // 2 - 1) as i:
                pair(i, True, False)
            pair(FT // 2 - 1, s.a0 + FT < A_TOTAL, True)

        def ffn_act(act, s):
            pre_act(act, s)
            ffn_tiles(act, s, hi_slot_b, ffn_tile_act)
            post_act(act, s, lambda: act.wait_ge(b_used, s.b0 + FT))

        def ffn_dve(dve, s):
            pre_dve(dve, s)
            ffn_tiles(dve, s, lo_slot_b, ffn_tile_dve)
            post_dve(dve, s, lambda: dve.wait_ge(b_used, s.b0 + FT))

        def ffn_sync(sp, s):
            if s.block == 1:
                gate, up, down = T["w_gate"][s.layer], T["w_up"][s.layer], T["w_down"][s.layer]
                up0 = 0
            else:
                gate = up = T["ffn_w_in_2"][s.layer, s.half]
                down, up0 = T["ffn_w_out_2"][s.layer, s.half], FF
            gate = gate.rearrange("(k p) n -> p k n", p=P)
            up = up.rearrange("(k p) n -> p k n", p=P)

            def tile(n, m, j, pa, pm):
                dst = a_view(raw_a, pa)
                if not isinstance(n, int) or n >= 2:
                    sp.wait_ge(a_lo, n - 1)
                sp.dma_start(dst[:, :, 0:P], gate[:, :, bass.ds(j * P, P)]).then_inc(a_full[pa], 16)
                sp.dma_start(dst[:, :, P:2 * P], up[:, :, bass.ds(j * P + up0, P)]).then_inc(a_full[pa], 16)
                if not isinstance(m, int) or m >= 2:
                    sp.wait_ge(b_lo, m - 1)
                sp.dma_start(raw_b[:, pm, :], down[bass.ds(j * P, P), :]).then_inc(b_full[pm], 16)

            for e in range(2):
                tile(s.a0 + e, s.b0 + e, e, (s.a0 + e) % 2, e)
            with sp.Fori(1, FT // 2) as i:
                for e in range(2):
                    tile(2 * i + (s.a0 + e), 2 * i + (s.b0 + e), 2 * i + e, (s.a0 + e) % 2, e)
            if s.block == 2:
                load_gain(sp, s, post_gain(s))

        def load_gain(sp, s, row):
            sp.wait_ge(x_ready, 2 * (s.k - (s.kind == "final")))
            sp.dma_start(gain_b, row.partition_broadcast(P)).then_inc(gain_full, 16)

        def mixer_sync(sp, s):
            if s.kind == "B":
                for m in range(2):
                    for c in (0, HD):
                        sp.dma_start(w2dup[:, m, :, c:c + HD], T["b_cmp_w2_2"][0, m].rearrange("(e p) d -> p e d", p=P))\
                            .then_inc(w2_full, 16)
            for i in range(KINDS[s.kind][1]):
                n = s.a0 + i
                if n >= 2:
                    sp.wait_ge(a_lo, n - 1)
                for k0, width, src in slot_sources(s, i):
                    sp.dma_start(a_view(raw_a, n)[:, k0:k0 + 4, 0:width], src).then_inc(a_full[n % 2], 16)
            if s.kind != "hybrid":
                load_gain(sp, s, post_gain(s))

        def proj_modes(s):
            return {"hybrid": [{"q": "f", "kv": "m", "xbc": "f"}.get(kind, "t") for kind, _ in HY_SLOTS], "A": "fmfff",
                    "B": "ffff" + "ff" + "f" + "t" + "f" + "t" + "t", "C": "ffff" + "ffff" + "tttt"}[s.kind]

        def proj_pe(pe, s, i):
            n, p, mode, width = s.a0 + i, s.proj0 + i, proj_modes(s)[i], slot_words(s, i)
            bank = gu[:, p % 2, :]
            w_hi, w_lo = a_view(hi_a, n), a_view(lo_a, n)
            jobs = []
            if mode == "f":
                jobs = [("f", e * 256, e * P, P) for e in range(2)]
            elif mode == "m":
                jobs = [("f", 0, 0, P)] + [("t", 256 + t * P, P, P, t) for t in range(NT)]
            else:
                jobs = [("t", t * 256, 0, width, t) for t in range(NT)]
            pe.wait_ge(a_lo, n + 1)
            if p >= 2:
                pe.wait_ge(proj_out, p - 1)
            if i == 0:
                first_products(pe, s, bank, w_hi, w_lo).then_inc(a_used, 1)
                return
            for job in jobs:
                o0, c0, w = job[1:4]
                for kt in range(KT):
                    wh, wl = w_hi[:, kt, c0:c0 + w], w_lo[:, kt, c0:c0 + w]
                    first, last = kt == 0, kt == KT - 1
                    if job[0] == "f":
                        o = bank[:, o0:o0 + 256]
                        nc.tensor.matmul(o, wh, xT_hi[:, kt, :], start=first, stop=False)
                        nc.tensor.matmul(o, wh, xT_lo[:, kt, :], start=False, stop=False)
                        mm = nc.tensor.matmul(o, wl, xT_hi[:, kt, :], start=False, stop=last)
                    else:
                        o, t = bank[:, o0:o0 + w], job[4]
                        xh, xl = xT_hi[:, kt, t * P:(t + 1) * P], xT_lo[:, kt, t * P:(t + 1) * P]
                        nc.tensor.matmul(o, xh, wh, start=first, stop=False)
                        nc.tensor.matmul(o, xh, wl, start=False, stop=False)
                        mm = nc.tensor.matmul(o, xl, wh, start=False, stop=last)
            mm.then_inc(a_used, 1)

        def proj_act(act, s, i, evacuate):
            n, p = s.a0 + i, s.proj0 + i
            act.wait_ge(a_used, n + 1)
            evacuate(gu[:, p % 2, :]).then_inc(proj_out, 1)
            ahead_a(hi_slot_a, act, n + 2)

        def out_pe(pe, s, slots):
            n_out = OUT_SLOTS[s.kind]
            first = s.a0 + KINDS[s.kind][1] - n_out
            for r in slots:
                n = first + r
                if s.kind == "hybrid" and r >= 2:
                    pe.wait_ge(turn_lo, 4 * s.turn0 + r + 3)
                else:
                    pe.wait_ge(o_lo, s.pair0 + 2 * r + 2)
                pe.wait_ge(a_lo, n + 1)
                for e in range(2):
                    k = 2 * r + e
                    mm = down_pe(oT_hi[:, k, :], oT_lo[:, k, :], hi_a[:, n % 2, e * D:(e + 1) * D],
                                 lo_a[:, n % 2, e * D:(e + 1) * D], k == 0, k == 2 * n_out - 1)
                mm.then_inc(a_used, 1)

        def out_split(split, eng, s, slots=None):
            n_out = OUT_SLOTS[s.kind]
            first = s.a0 + KINDS[s.kind][1] - n_out
            for r in slots or range(0 if s.kind == "hybrid" else 2, n_out):
                ahead_a(split, eng, first + r + 2)

        def unit(s, w):
            if s.kind == "hybrid":
                g = 2 * w // (H1 // KV1)
                return w, 0, kT1[:, g, :], (v1, g * HD, g * HD), C("dilated").unsqueeze(1).broadcast_to([P, 2, 384])
            if s.kind == "A":
                g = 2 * w // 8
                return w, 0, kT2[:, g, :], (v2, g * HD, g * HD), bias[:, 2 * w:2 * w + 2, :]
            if s.kind == "B":
                u, br = w // 2, w % 2
                g = 2 * u // 4
                return u, br, kT2[:, 4 * br + g, :], (v2b, 256 * br + g * HD, 256 * br + g * HD), bias[:, 2 * u:2 * u + 2, :]
            return w, 0, kT2[:, w, :], (v2, 2 * w * HD, (2 * w + 1) * HD), bias[:, 2 * w:2 * w + 2, :]

        def branches(s):
            return 2 if s.kind == "B" else 1

        def n_units(s):
            return KINDS[s.kind][2]

        def scores_pe(pe, s, w):
            g = s.unit0 + w
            u, _, kt, _, _ = unit(s, w)
            q = qT1 if s.kind == "hybrid" else qT2
            if g >= 2:
                pe.wait_ge(soft_ready, g - 1)
            for hh in range(2):
                r = slice(64 * hh, 64 * hh + 64)
                bank = acc[:, 2 * (g % 2) + hh, :]
                nc.tensor.matmul(bank[:, 0:128], q[r, u, 0:128], kt[r, 0:128], start=True, stop=True)
                mm = nc.tensor.matmul(bank[:, 128:384], q[r, u, 128:256], kt[r, 0:256], start=True, stop=True)
            mm.then_inc(score_ready, 1)

        def turn_probs_pe(pe, s, w):
            g = s.unit0 + w
            pe.wait_ge(prob_ready, g + 1)
            if g >= 1:
                pe.wait_ge(pt_act, g)
            for hh in range(2):
                for t in range(NT):
                    mm = nc.tensor.transpose(gu[:, 0, hh * 256 + t * P:hh * 256 + (t + 1) * P],
                                             probs[g % 3][:, hh, t * P:(t + 1) * P], ident)
            mm.then_inc(pt_ready, 1)
            if g >= 1:
                pe.wait_ge(pt_dve, g)
            for hh in range(2):
                mm = nc.tensor.transpose(gu[:, 1, hh * P:(hh + 1) * P], probs[g % 3][:, hh, 256:384], ident)
            mm.then_inc(pt_ready, 1)

        def values_pe(pe, s, w):
            g = s.unit0 + w
            u, br, _, (v, c0, c1), _ = unit(s, w)
            o = s.pair0 + u
            nb = branches(s)
            pe.wait_ge(pt_act, g + 1)
            pe.wait_ge(pt_dve, g + 1)
            if br == 0 and o >= 2:
                pe.wait_ge(o_lo, o - 1)
            for hh, c in ((0, c0), (1, c1)):
                r = slice(64 * hh, 64 * hh + 64)
                bank = tp[r, o % 2, :]
                last = br == nb - 1
                cmp_too = s.kind == "B" and last
                nc.tensor.matmul(bank[:, 0:256], v[:, 0, c:c + HD], probT[:, g % 2, hh * 256:(hh + 1) * 256],
                                 start=(br == 0), stop=False)
                mm = nc.tensor.matmul(bank[:, 128:256], v[:, 1, c:c + HD], probT[:, g % 2, 512 + hh * P:512 + (hh + 1) * P],
                                      start=False, stop=(last and not cmp_too))
                if cmp_too:
                    head = 2 * u + hh
                    q = slice(32 * (head % 4), 32 * (head % 4) + 32)
                    mm = nc.tensor.matmul(bank[:, 0:256], vcb[q, head // 4, :], pcT[q, head // 4, :], start=False, stop=True)
            if br == nb - 1:
                mm.then_inc(o_ready, 1)

        def attention_steps(s):
            return range(n_units(s) + 3)

        def first_scores_pe(pe, s):
            last = KINDS[s.kind][0] - (s.kind != "B")
            pe.wait_ge(proj_out, s.proj0 + last)
            if DUPS[s.kind]:
                pe.wait_ge(k_dup, 16 * (s.dup0 + DUPS[s.kind]))
            scores_pe(pe, s, 0)

        def attention_pe(pe, s):
            W = n_units(s)
            for k in attention_steps(s):
                if 0 <= k - 2 < W:
                    turn_probs_pe(pe, s, k - 2)
                if k + 1 < W:
                    scores_pe(pe, s, k + 1)
                if k == 1:
                    if s.kind == "hybrid":
                        pe.wait_ge(bc_out, s.layer + 1)
                        pe.wait_ge(cs_out, s.layer + 1)
                    keep_warm(WARM_ATT)
                if k in (W, W + 1) and s.kind != "hybrid":
                    pe.wait_ge(soft_ready, s.unit0 + W)
                    out_pe(pe, s, (k - W,))
                if k == 0:
                    pe.wait_ge(proj_out, s.proj0 + KINDS[s.kind][0])
                if 0 <= k - 2 < W:
                    values_pe(pe, s, k - 2)

        def attention_act(act, s, steps):
            W, nb = n_units(s), branches(s)
            for k in steps:
                if 0 <= k - 2 < W:
                    g = s.unit0 + k - 2
                    act.wait_ge(pt_ready, 2 * g + 1)
                    nc.scalar.activation(probT[:, g % 2, 0:512], gu[:, 0, :], ACT.Copy).then_inc(pt_act, 1)
                if k < W:
                    g = s.unit0 + k
                    b, prob = g % 2, probs[g % 3]
                    act.wait_ge(soft_ready, g + 1)
                    for hh in range(2):
                        nc.scalar.activation(prob[:, hh, 0:128], prob[:, hh, 0:128], ACT.Exp,
                                             bias=nmax[:, b, 2 * hh:2 * hh + 1], accum_out=den[:, b, 2 * hh:2 * hh + 1])
                        ins = nc.scalar.activation(prob[:, hh, 128:384], prob[:, hh, 128:384], ACT.Exp,
                                                   bias=nmax[:, b, 2 * hh + 1:2 * hh + 2], accum_out=den[:, b, 2 * hh + 1:2 * hh + 2])
                    if s.kind == "A":
                        ins = nc.scalar.activation(esink[:, b, :], sarg[:, b, :], ACT.Exp)
                    ins.then_inc(exp_ready, 1)
                if k > W and s.kind != "hybrid":
                    out_split(hi_slot_a, act, s, (k - W - 1,))
                if 0 <= k - 2 < W and (k - 2) % nb == nb - 1:
                    u = (k - 2) // nb
                    o = s.pair0 + u
                    act.wait_ge(o_ready, o + 1)
                    nc.scalar.activation(oT_hi[:, u, :], tp[:, o % 2, 0:256], ACT.Copy).then_inc(o_hi, 1)

        def soft_dve(dve, s, k):
            g = s.unit0 + k
            b, prob = g % 2, probs[g % 3]
            dve.wait_ge(score_ready, g + 1)
            nc.vector.scalar_tensor_tensor(prob, acc[:, 2 * b:2 * b + 2, 0:384], HD ** -0.5, unit(s, k)[4],
                                           ALU.mult, ALU.add)
            dve.drain()
            if s.kind == "A":
                nc.vector.tensor_tensor(prob[:, :, 128:256], prob[:, :, 128:256],
                                        C("window").unsqueeze(1).broadcast_to([P, 2, P]), ALU.add)
                dve.drain()
            n4 = nmax[:, b, :].rearrange("p (h t) -> p h t", h=2)
            for t, (c0, c1) in enumerate(((0, 128), (128, 384))):
                ins = nc.vector.tensor_reduce(n4[:, :, t:t + 1], prob[:, :, c0:c1], AX_X, ALU.max, negate=True)
            if s.kind == "A":
                dve.drain()
                sk = sinks[:, s.j, 2 * k:2 * k + 2].unsqueeze(2).broadcast_to([P, 2, 2])
                nk = nsinks[:, s.j, 2 * k:2 * k + 2].unsqueeze(2).broadcast_to([P, 2, 2])
                nc.vector.tensor_tensor(n4, n4, nk, ALU.min)
                dve.drain()
                ins = nc.vector.tensor_tensor(sarg[:, b, :].rearrange("p (h t) -> p h t", h=2), n4, sk, ALU.add)
            ins.then_inc(soft_ready, 1)

        def rden_dve(dve, s, w):
            g = s.unit0 + w
            b = g % 2
            dve.wait_ge(exp_ready, g + 1)
            if s.kind == "A":
                nc.vector.tensor_tensor(den[:, b, :], den[:, b, :], esink[:, b, :], ALU.add)
                dve.drain()
            ins = nc.vector.reciprocal(rden[:, b, :], den[:, b, :])
            if s.kind == "B":
                dve.drain()
                r4 = rden[:, b, :].rearrange("p (h t) -> p h t", h=2)
                u, br = w // 2, w % 2
                gt = gates.rearrange("p t (h c) -> p h t c", c=3)[:, 2 * u:2 * u + 2, :, 1 + br]
                ins = nc.vector.tensor_tensor(r4, r4, gt, ALU.mult)
            ins.then_inc(rden_ready, 1)

        def normalise_pool(pool, s):
            for w in range(n_units(s)):
                g = s.unit0 + w
                pool.wait_ge(rden_ready, g + 1)
                prob, r4 = probs[g % 3], rden[:, g % 2, :].rearrange("p (h t) -> p h t", h=2)
                for t, (c0, c1) in enumerate(((0, 128), (128, 384))):
                    ins = nc.gpsimd.tensor_tensor(prob[:, :, c0:c1], prob[:, :, c0:c1],
                                                  r4[:, :, t:t + 1].broadcast_to([P, 2, c1 - c0]), ALU.mult)
                ins.then_inc(prob_ready, 1)

        def attention_dve(dve, s, steps):
            W, nb = n_units(s), branches(s)
            for k in steps:
                if k == 1:
                    rden_dve(dve, s, 0)
                if k < W:
                    soft_dve(dve, s, k)
                if 0 <= k - 2 < W:
                    g = s.unit0 + k - 2
                    dve.wait_ge(pt_ready, 2 * g + 2)
                    nc.vector.tensor_copy(probT[:, g % 2, 512:768], gu[:, 1, 0:256]).then_inc(pt_dve, 1)
                if 0 <= k - 3 < W and (k - 3) % nb == nb - 1:
                    u = (k - 3) // nb
                    o = s.pair0 + u
                    dve.wait_ge(o_hi, o + 1)
                    nc.vector.tensor_tensor(oT_lo[:, u, :], tp[:, o % 2, 0:256], oT_hi[:, u, :].bitcast(F32),
                                            ALU.subtract).then_inc(o_lo, 1)
                if 1 <= k - 1 < W:
                    rden_dve(dve, s, k - 1)
                if k > W and s.kind != "hybrid":
                    out_split(lo_slot_a, dve, s, (k - W - 1,))

        def dup_keys(act, kt, tiles):
            for c in tiles:
                src, dst = (slice(0, 64), slice(64, 128)) if c % 2 == 0 else (slice(64, 128), slice(0, 64))
                act.dma_start(kt[dst, c, :], kt[src, c, :]).then_inc(k_dup, 16)

        def half_keys(kt, c, bank):
            nc.scalar.activation(kt[0:64, c, :], bank[0:64, 0:256], ACT.Copy)
            return nc.scalar.activation(kt[64:128, c + 1, :], bank[64:128, 0:256], ACT.Copy)

        def evac_A(i):
            c = max(i - 1, 0)

            def q(bank):
                return nc.scalar.activation(qT2[:, 2 * c:2 * c + 2, :], bank.rearrange("p (u t) -> p u t", u=2), ACT.Copy)

            def kv(bank):
                half_keys(kT2, 0, bank)
                return nc.scalar.activation(v2[:, :, 0:128], bank[:, 256:512].rearrange("p (t d) -> p t d", t=2), ACT.Copy)
            return kv if i == 1 else q

        def evac_C(i):
            def qk(bank):
                dst = qT2 if i < 4 else kT2
                return nc.scalar.activation(dst[:, 2 * (i % 4):2 * (i % 4) + 2, :], bank.rearrange("p (u t) -> p u t", u=2), ACT.Copy)

            def v(bank):
                c = 256 * (i - 8)
                return nc.scalar.activation(v2[:, :, c:c + 256], bank.rearrange("p (t d) -> p t d", t=2), ACT.Copy)
            return qk if i < 8 else v

        def ac_pe(pe, s):
            pre_pe(pe, s)
            for i in range(KINDS[s.kind][0]):
                if i == KINDS[s.kind][0] - 1:
                    first_scores_pe(pe, s)
                proj_pe(pe, s, i)
            attention_pe(pe, s)
            out_pe(pe, s, (2, 3))

        def ac_act(act, s):
            pre_act(act, s)
            for i in range(KINDS[s.kind][0]):
                if i == KINDS[s.kind][0] - 1:
                    attention_act(act, s, attention_steps(s)[:1])
                proj_act(act, s, i, (evac_A if s.kind == "A" else evac_C)(i))
                if s.kind == "A" and i == 1:
                    act.wait_ge(proj_out, s.proj0 + 2)
                    dup_keys(act, kT2, (0, 1))
            attention_act(act, s, attention_steps(s)[1:])
            out_split(hi_slot_a, act, s)
            post_act(act, s, lambda: act.wait_ge(a_used, s.a0 + KINDS[s.kind][1]))

        def ac_dve(dve, s):
            pre_dve(dve, s)
            for i in range(KINDS[s.kind][0]):
                if i == KINDS[s.kind][0] - 1:
                    attention_dve(dve, s, attention_steps(s)[:2])
                ahead_a(lo_slot_a, dve, s.a0 + i + 2)
            attention_dve(dve, s, attention_steps(s)[2:])
            out_split(lo_slot_a, dve, s)
            post_dve(dve, s, None)

        def evac_B(i):
            def q(bank):
                return nc.scalar.activation(qT2[:, 2 * i - 4:2 * i - 2, :], bank.rearrange("p (u t) -> p u t", u=2), ACT.Copy)

            def c(bank):
                return nc.scalar.activation(craw[:, i, :, :], bank.rearrange("p (u t) -> p u t", u=2), ACT.Copy)

            def k(bank):
                br = (i - 6) // 2
                half_keys(kT2, 4 * br, bank[:, 0:256])
                return half_keys(kT2, 4 * br + 2, bank[:, 256:512])

            def v(bank):
                br = (i - 7) // 2
                return nc.scalar.activation(v2b[:, :, 256 * br:256 * br + 256], bank.rearrange("p (t d) -> p t d", t=2), ACT.Copy)

            def g(bank):
                return nc.scalar.activation(gexp.rearrange("p (t c) -> p t c", t=2),
                                            bank.rearrange("p (t d) -> p t d", t=2)[:, :, 0:48], ACT.Exp, scale=-1.0)
            return c if i < 2 else q if i < 6 else g if i == 10 else (k, v)[i % 2]

        def shift_rows(act, m):
            for g in range(BG):
                src = craw[64 * (g % 2):64 * (g % 2) + 64, m, g // 2, :]
                act.dma_start(zsh[0:64, g, 0:256], src).then_inc(zsh_full, 16)
                act.dma_start(zsh[64:128, g, 0:255], src[:, 1:256]).then_inc(zsh_full, 16)

        def b_pe(pe, s):
            pre_pe(pe, s)
            for i in range(11):
                proj_pe(pe, s, i)
            pe.wait_ge(proj_out, s.proj0 + 11)
            for m in range(2):
                pe.wait_ge(z_lo, m + 1)
                for q in range(2):
                    n = s.a0 + 11 + 2 * m + q
                    pe.wait_ge(a_lo, n + 1)
                    for kk in range(8):
                        j = 8 * q + kk
                        c = slice(64 * (j % 4), 64 * (j % 4) + 64)
                        xh, xl = oT_hi[:, 4 * m + j // 4, c], oT_lo[:, 4 * m + j // 4, c]
                        wh, wl = a_view(hi_a, n)[:, kk, :], a_view(lo_a, n)[:, kk, :]
                        for l, w in ((xh, wh), (xh, wl), (xl, wh)):
                            mm = nc.tensor.matmul(tp[0:64, m, 0:256], l, w, start=(j == 0 and l is xh and w is wh),
                                                  stop=(j == CJ - 1 and l is xl))
                    mm.then_inc(a_used, 1)
            for m in range(2):
                pe.wait_ge(cmp_hid, m + 1)
                for e in range(2):
                    mm = nc.tensor.transpose(acc[:, m, 64 * e:64 * e + 64], hidt[0:64, m, e * P:(e + 1) * P], ident[0:64, 0:64])
                mm.then_inc(hid_turned, 1)
            pe.wait_ge(w2_full, 64)
            pe.wait_ge(hid_out, 1)
            for e in range(2):
                mm = nc.tensor.matmul(gu[:, 0, 0:64], w2dup[:, 0, e, :], hid2[:, 64 * e:64 * e + 64],
                                      start=(e == 0), stop=(e == 1))
            mm.then_inc(cmp_kv, 1)
            pe.wait_ge(hid_rep, 1)
            hr = hidr.rearrange("p (e g c) -> p e g c", e=2, g=BG)
            for g in range(BG):
                for e in range(2):
                    mm = nc.tensor.matmul(gu[:, 1, g * HD:(g + 1) * HD], hr[:, e, g, :], w2dup[:, 1, e, 0:HD],
                                          start=(e == 0), stop=(e == 1))
            mm.then_inc(cmp_kv, 1)
            pe.wait_ge(ckv_out, 2)
            for t in range(NT):
                for u in range(8):
                    c = 256 * t + 32 * u
                    mm = nc.tensor.matmul(gu[:, 0, c:c + 32], qT2[:, u, t * P:(t + 1) * P], kcd[:, u // 2, :, :],
                                          start=True, stop=True)
            mm.then_inc(cmp_s, 1)
            first_scores_pe(pe, s)
            keep_warm(WARM_CMP)
            pe.wait_ge(cmp_p, 1)
            for g in range(BG):
                for t in range(NT):
                    mm = nc.tensor.transpose(tp[:, g // 2, 256 * (g % 2) + t * P:256 * (g % 2) + (t + 1) * P],
                                             pc.rearrange("p (t g c) -> p t g c", t=2, g=BG)[:, t, g, :], ident)
                if g % 2:
                    mm.then_inc(cmp_pt, 1)
            pe.wait_ge(cmp_pt_out, 2)
            attention_pe(pe, s)
            out_pe(pe, s, (2, 3))

        def b_act(act, s):
            pre_act(act, s)
            for i in range(11):
                proj_act(act, s, i, evac_B(i))
                if i == 1:
                    act.wait_ge(proj_out, s.proj0 + 2)
                    act.wait_ge(zsh_clear, 1)
                    shift_rows(act, 0)
                if i in (3, 5):
                    m = (i - 3) // 2
                    act.wait_ge(z_ready, m + 1)
                    nc.scalar.activation(oT_hi[:, 4 * m:4 * m + 4, :], zpos[m].rearrange("p (k t) -> p k t", k=4), ACT.Copy)\
                        .then_inc(z_hi, 1)
                    if m == 0:
                        shift_rows(act, 1)
                if i == 6 or i == 8:
                    act.wait_ge(proj_out, s.proj0 + i + 1)
                    dup_keys(act, kT2, range(2 * (i - 6), 2 * (i - 6) + 4))
            for m in range(2):
                for q in range(2):
                    ahead_a(hi_slot_a, act, s.a0 + 11 + 2 * m + q + 2)
                act.wait_ge(a_used, s.a0 + 13 + 2 * m)
                nc.scalar.activation(hidt[0:64, m, :], tp[0:64, m, 0:256], ACT.Gelu_apprx_tanh).then_inc(cmp_hid, 1)
            act.wait_ge(hid_turned, 1)
            nc.scalar.activation(hid2, acc[:, 0, 0:P], ACT.Copy).then_inc(hid_out, 1)
            act.wait_ge(cmp_kv, 1)
            for h in range(2):
                r = slice(64 * h, 64 * h + 64)
                ins = nc.scalar.activation(kcd[r, :, h, :], gu[r, 0, 0:64].rearrange("p (g n) -> p g n", g=BG), ACT.Copy)
            ins.then_inc(ckv_out, 1)
            act.wait_ge(cmp_kv, 2)
            nc.scalar.activation(vcb, gu[:, 1, 0:256].rearrange("p (g n) -> p g n", g=BG), ACT.Copy).then_inc(ckv_out, 1)
            act.wait_ge(cmp_sub, 1)
            pv = pc.rearrange("p (a c) -> p a c", c=32)[:, :, 0:16]
            nc.scalar.activation(pv, pv, ACT.Exp).then_inc(cmp_exp, 1)
            for q in range(2):
                act.wait_ge(cmp_pt, q + 1)
                nc.scalar.activation(pcT[:, 2 * q:2 * q + 2, :], tp[:, q, :].rearrange("p (g t) -> p g t", g=2),
                                     ACT.Copy).then_inc(cmp_pt_out, 1)
            attention_act(act, s, attention_steps(s))
            out_split(hi_slot_a, act, s)
            post_act(act, s, lambda: act.wait_ge(a_used, s.a0 + KINDS[s.kind][1]))

        def b_dve(dve, s):
            pre_dve(dve, s)
            nc.vector.memset(kcd, 0.0)
            nc.vector.memset(zsh, 0.0).then_inc(zsh_clear, 1)
            for i in range(11):
                ahead_a(lo_slot_a, dve, s.a0 + i + 2)
                if i in (2, 4):
                    m = (i - 2) // 2
                    dve.wait_ge(zsh_full, 16 * (8 + 8 * m))
                    z4 = zpos[m].rearrange("p (j g n) -> p j g n", j=CJ, g=BG)
                    for g in range(BG):
                        src = zsh[:, g, :].rearrange("p (n c) -> p c n", c=CMP_STRIDE)
                        for half in range(2):
                            pos = cols[:, 1, 48 + 16 * m + 8 * half:48 + 16 * m + 8 * half + 8].unsqueeze(2).broadcast_to([P, 8, 16])
                            ins = nc.vector.tensor_tensor(z4[:, 8 * half:8 * half + 8, g, :], src[:, 0:16:2, half:half + 16],
                                                          pos, ALU.add)
                    ins.then_inc(z_ready, 1)
                if i in (3, 5):
                    m = (i - 3) // 2
                    dve.wait_ge(z_hi, m + 1)
                    nc.vector.tensor_tensor(oT_lo[:, 4 * m:4 * m + 4, :], zpos[m].rearrange("p (k t) -> p k t", k=4),
                                            oT_hi[:, 4 * m:4 * m + 4, :].bitcast(F32), ALU.subtract).then_inc(z_lo, 1)
            nc.vector.memset(hidr, 0.0)
            nc.vector.memset(pc, 0.0)
            for m in range(2):
                for q in range(2):
                    ahead_a(lo_slot_a, dve, s.a0 + 11 + 2 * m + q + 2)
            dve.wait_ge(proj_out, s.proj0 + 11)
            nc.vector.tensor_scalar(gexp, gexp, 1.0, None, ALU.add)
            dve.drain()
            nc.vector.reciprocal(gates, gexp.rearrange("p (t c) -> p t c", t=2))
            dve.wait_ge(hid_turned, 2)
            hr = hidr.rearrange("p (e g h n) -> p e g h n", e=2, g=BG, h=4)
            for e in range(2):
                for g in range(BG):
                    c = 64 * e + 16 * g
                    ins = nc.vector.tensor_copy(hr[:, e, g, :, 0:16], acc[:, 1, c:c + 16].unsqueeze(1).broadcast_to([P, 4, 16]))
            ins.then_inc(hid_rep, 1)
            p4 = pc.rearrange("p (t h c) -> p t h c", t=2, h=NH)
            mx = cmx.rearrange("p (t h) -> p t h", t=2)
            dn = cden.rearrange("p (t h) -> p t h", t=2)
            dve.wait_ge(cmp_s, 1)
            for t in range(NT):
                nc.vector.scalar_tensor_tensor(p4[:, t, :, 0:16], gu[:, 0, 256 * t:256 * t + 256].rearrange("p (h c) -> p h c", h=NH),
                                               HD ** -0.5, C("cmpbias")[:, 16 * t:16 * t + 16].unsqueeze(1).broadcast_to([P, NH, 16]),
                                               ALU.mult, ALU.add)
            dve.drain()
            for t in range(NT):
                nc.vector.tensor_reduce(mx[:, t, :].unsqueeze(2), p4[:, t, :, 0:16], AX_X, ALU.max)
            dve.drain()
            for t in range(NT):
                ins = nc.vector.tensor_tensor(p4[:, t, :, 0:16], p4[:, t, :, 0:16],
                                              mx[:, t, :].unsqueeze(2).broadcast_to([P, NH, 16]), ALU.subtract)
            ins.then_inc(cmp_sub, 1)
            dve.wait_ge(cmp_exp, 1)
            for t in range(NT):
                nc.vector.tensor_tensor(p4[:, t, :, 0:16], p4[:, t, :, 0:16],
                                        C("cmpok")[:, 16 * t:16 * t + 16].unsqueeze(1).broadcast_to([P, NH, 16]), ALU.mult)
            dve.drain()
            for t in range(NT):
                nc.vector.tensor_reduce(dn[:, t, :].unsqueeze(2), p4[:, t, :, 0:16], AX_X, ALU.add)
            dve.drain()
            nc.vector.tensor_scalar(cden, cden, TINY, None, ALU.max)
            dve.drain()
            nc.vector.reciprocal(cden, cden)
            dve.drain()
            nc.vector.tensor_tensor(dn, dn, gates.rearrange("p t (h c) -> p t h c", c=3)[:, :, :, 0], ALU.mult)
            dve.drain()
            for t in range(NT):
                ins = nc.vector.tensor_tensor(p4[:, t, :, 0:16], p4[:, t, :, 0:16],
                                              dn[:, t, :].unsqueeze(2).broadcast_to([P, NH, 16]), ALU.mult)
            ins.then_inc(cmp_p, 1)
            attention_dve(dve, s, attention_steps(s))
            out_split(lo_slot_a, dve, s)
            post_dve(dve, s, None)

        def hybrid_pe(pe, s):
            L = s.layer
            pre_pe(pe, s)
            for i in range(14):
                if i == 13:
                    pe.wait_ge(rope_dve, 3 * L + 3)
                    first_scores_pe(pe, s)
                proj_pe(pe, s, i)
                for r, after in HY_ROPES.values():
                    if i == after:
                        pe.wait_ge(proj_out, s.proj0 + HY_SLOTS.index(("kv", 0)) + 1)
                        if r == 2:
                            pe.wait_ge(rope_dve, 3 * L + 1)
                        src = qT1[:, 2 * r - 2:2 * r, :] if r else kraw1
                        nc.tensor.matmul(tp[:, r % 2, 0:(512 if r else 256)], C("rot"), src,
                                         start=True, stop=True).then_inc(rope_pe, 1)
            ssd_early_pe(pe, s)
            attention_pe(pe, s)
            ssd_pe(pe, s)
            pe.wait_ge(y_ready, 2 * L + 2)
            out_pe(pe, s, (0,))
            turn_pe(pe, s.turn0 + 1, y, turn_others)
            out_pe(pe, s, (1, 2, 3, 4, 5))

        def ssd_early_pe(pe, s):
            L = s.layer
            pe.wait_ge(silued, 6 * L + 6)
            for g in range(SSM_GROUPS):
                nc.tensor.transpose(tp[:, 0, g * P:(g + 1) * P], conv[:, 8 + g, 0:P], ident)
            for c in range(NT):
                for g in range(SSM_GROUPS):
                    nc.tensor.matmul(tp[:, 1, (2 * c + g) * P:(2 * c + g + 1) * P], conv[:, 8 + g, c * P:(c + 1) * P],
                                     conv[:, 10 + g, c * P:(c + 1) * P], start=True, stop=True)
            pe.wait_ge(dt_done, L + 1)
            for c in range(NT):
                nc.tensor.matmul(tp[:, 0, 256 + 16 * c:272 + 16 * c], C("triu"), da[:, 16 * c:16 * c + 16], start=True, stop=True)
            nc.tensor.matmul(tp[:, 0, 288:304], ones, da[:, 0:16], start=True, stop=True).then_inc(cs_ps, 1)

        def ssd_pe(pe, s):
            L = s.layer

            def turn_x(c, banks):
                for k in range(8):
                    mm = nc.tensor.transpose(banks[:, k // 4, (k % 4) * P:(k % 4 + 1) * P],
                                             conv[:, k, c * P:(c + 1) * P], ident)
                mm.then_inc(x_turned, 1)

            def decay_rows(c):
                for q in range(4):
                    if c == 1:
                        pe.wait_ge(seg_ready, 8 * L + q + 1)
                    for e in range(4):
                        a = 16 * c + 4 * q + e
                        mm = nc.tensor.matmul(acc[:, q, e * P:(e + 1) * P], da[:, a:a + 1].broadcast_to([P, P]), C("triu"),
                                              start=True, stop=True)
                    mm.then_inc(row_ps, 1)

            def within_chunk(c, banks):
                pe.wait_ge(m_ready, 4 * L + 2 * c + 2)
                for h in range(SSM_HEADS):
                    mm = nc.tensor.matmul(banks[:, h // 8, (h % 8) * HD:(h % 8 + 1) * HD], mTs[c][:, h, :],
                                          xdt[:, c, h * HD:(h + 1) * HD], start=True, stop=True)
                mm.then_inc(ydiag_ps, 1)

            turn_x(0, gu)
            decay_rows(0)
            pe.wait_ge(o_lo, s.pair0 + 4)
            turn_x(1, tp)
            decay_rows(1)
            pe.wait_ge(xs_act, L + 1)
            pe.wait_ge(xdec_ready, L + 1)
            for g in range(SSM_GROUPS):
                mm = nc.tensor.matmul(gu[:, g, :], btok[:, g, :], xdec[:, g * 512:(g + 1) * 512], start=True, stop=True)
            mm.then_inc(state_ps, 1)
            pe.wait_ge(xs_dve, L + 1)
            within_chunk(0, tp)
            pe.wait_ge(state_out, L + 1)
            for g in range(SSM_GROUPS):
                mm = nc.tensor.matmul(gu[:, g, :], conv[:, 10 + g, P:2 * P], st0[:, g * 512:(g + 1) * 512], start=True, stop=True)
            mm.then_inc(yoff_ps, 1)
            within_chunk(1, acc[:, 0:2, :])

        def hybrid_act(act, s):
            L = s.layer
            pre_act(act, s)

            def q(i):
                return lambda bank: nc.scalar.activation(qT1[:, 2 * i:2 * i + 2, :], bank.rearrange("p (u t) -> p u t", u=2), ACT.Copy)

            def kv(bank):
                nc.scalar.activation(kraw1, bank[:, 0:256], ACT.Copy)
                return nc.scalar.activation(v1, bank[:, 256:512].rearrange("p (t d) -> p t d", t=2), ACT.Copy)

            def xbc(i):
                def f(bank):
                    for e in range(2):
                        k = 2 * i + e
                        nc.scalar.activation(conv[:, k, :], bank[:, e * 256:(e + 1) * 256], ACT.Identity,
                                             bias=col(0, 96 + CT * L + k), scale=col(0, 4 * CT * L + 3 * CT + k))
                    return nc.scalar.activation(upad[:, 2 * i:2 * i + 2, 3:259], bank.rearrange("p (u t) -> p u t", u=2), ACT.Copy)
                return f

            def z(i):
                return lambda bank: nc.scalar.activation(zsil[:, :, 256 * i:256 * i + 256],
                                                         bank.rearrange("p (t d) -> p t d", t=2), ACT.Silu)

            def dtr(bank):
                return nc.scalar.activation(dt_raw.rearrange("p (t h) -> p t h", t=2),
                                            bank.rearrange("p (t d) -> p t d", t=2)[:, :, 0:16], ACT.Copy)

            for i in range(14):
                kind, r = HY_SLOTS[i]
                f = kv if kind == "kv" else dtr if kind == "dt" else {"q": q, "xbc": xbc, "z": z}[kind](r)
                if i == 13:
                    attention_act(act, s, attention_steps(s)[:1])
                proj_act(act, s, i, f)
                if HY_SLOTS[i - 1][0] == "xbc":
                    k = HY_SLOTS[i - 1][1]
                    act.wait_ge(conved, 6 * L + k + 1)
                    nc.scalar.activation(conv[:, 2 * k:2 * k + 2, :], conv[:, 2 * k:2 * k + 2, :], ACT.Silu).then_inc(silued, 1)
                if i == min(HY_ROPES) + 1:
                    act.wait_ge(rope_dve, 3 * L + 1)
                    dup_keys(act, kT1, (0, 1))
                if kind == "dt":
                    act.wait_ge(dt_neg, L + 1)
                    nc.scalar.activation(dt_u, dt_u, ACT.Exp).then_inc(dt_exp, 1)
                    act.wait_ge(dt_one, L + 1)
                    nc.scalar.activation(dt_ln, dt_w, ACT.Ln).then_inc(dt_log, 1)
            act.wait_ge(cs_ps, L + 1)
            nc.scalar.activation(btok, tp[:, 0, 0:256].rearrange("p (g n) -> p g n", g=2), ACT.Copy).then_inc(bc_half, 1)
            nc.scalar.activation(cbT, tp[:, 1, :].rearrange("p (c g l) -> p c g l", c=2, g=2), ACT.Copy).then_inc(bc_out, 1)
            act.wait_ge(cs_out, L + 1)
            nc.scalar.activation(ecs1, cs[:, 16:32], ACT.Exp)
            nc.scalar.activation(dec0, csd, ACT.Exp).then_inc(decays, 1)
            attention_act(act, s, attention_steps(s)[1:])
            act.wait_ge(x_turned, 2 * L + 1)
            nc.scalar.activation(xs[:, 0, :], gu[:, :, :].rearrange("p g n -> p (g n)"), ACT.Copy).then_inc(xs_act, 1)
            for c in range(NT):
                for q4 in range(4):
                    act.wait_ge(seg_ready, 8 * L + 4 * c + q4 + 1)
                    m = mTs[c][:, 4 * q4:4 * q4 + 4, :]
                    nc.scalar.activation(m, m, ACT.Exp).then_inc(seg_exp, 1)
                if c == 0:
                    act.wait_ge(state_ps, L + 1)
                    nc.scalar.activation(st0, gu[:, :, :].rearrange("p g n -> p (g n)"), ACT.Copy).then_inc(state_out, 1)
            for c in range(NT):
                act.wait_ge(y_ready, 2 * L + c + 1)
                for g in range(SSM_GROUPS):
                    ins = nc.scalar.activation(xdt[:, c, g * 512:(g + 1) * 512], y[:, c, g * 512:(g + 1) * 512], ACT.Square,
                                               accum_out=ssg[:, 2 * c + g:2 * c + g + 1])
                ins.then_inc(sq_act, 1)
            turn_act(act, s.turn0 + 1, oT_hi, 4, ssm_col(s), turn_others)
            out_split(hi_slot_a, act, s)

        def ssm_col(s):
            return lambda kt: col(1, 32 + 8 * s.layer + kt)

        def hybrid_dve(dve, s):
            L = s.layer
            pre_dve(dve, s)
            nc.vector.memset(upad[:, :, 0:3], 0.0)
            dve.drain()

            def rope(r):
                dve.wait_ge(rope_pe, 3 * L + r + 1)
                n = 2 if r else 1
                raw = qT1[:, 2 * r - 2:2 * r, :] if r else kraw1.unsqueeze(1)
                t1, t2 = (ropet[:, e, 0:256 * n].rearrange("p (u t) -> p u t", u=n) for e in range(2))
                nc.vector.tensor_tensor(t1, raw, cos.unsqueeze(1).broadcast_to([P, n, SEQ]), ALU.mult)
                nc.vector.tensor_tensor(t2, tp[:, r % 2, 0:256 * n].rearrange("p (u t) -> p u t", u=n),
                                        sin.unsqueeze(1).broadcast_to([P, n, SEQ]), ALU.mult)
                dve.drain()
                if r:
                    ins = nc.vector.tensor_tensor(raw, t1, t2, ALU.add)
                else:
                    nc.vector.tensor_tensor(kT1[0:64, 0, :], t1[0:64, 0, :], t2[0:64, 0, :], ALU.add)
                    ins = nc.vector.tensor_tensor(kT1[64:128, 1, :], t1[64:128, 0, :], t2[64:128, 0, :], ALU.add)
                ins.then_inc(rope_dve, 1)
                dve.drain()

            def taps(slot, i):
                dve.wait_ge(proj_out, s.proj0 + slot + 1)
                for tap in range(3):
                    for e in range(2):
                        k = 2 * i + e
                        ins = nc.vector.scalar_tensor_tensor(conv[:, k, :], upad[:, k, tap:tap + 256],
                                                             col(0, 4 * CT * L + CT * tap + k), conv[:, k, :],
                                                             ALU.mult, ALU.add)
                    if tap < 2:
                        dve.drain()
                ins.then_inc(conved, 1)

            def th(v):
                return v.rearrange("p (t h) -> p t h", t=2)

            def softplus():
                dve.wait_ge(proj_out, s.proj0 + HY_SLOTS.index(("dt", 0)) + 1)
                nc.vector.tensor_tensor(th(dt_x), th(dt_raw), dtb[:, L, :].unsqueeze(1).broadcast_to([P, 2, 16]), ALU.add)
                dve.drain()
                nc.vector.tensor_scalar(dt_u, dt_x, -1.0, None, ALU.mult)
                dve.drain()
                nc.vector.tensor_tensor(dt_u, dt_u, dt_x, ALU.min).then_inc(dt_neg, 1)
                dve.wait_ge(dt_exp, L + 1)
                nc.vector.tensor_scalar(dt_w, dt_u, 1.0, None, ALU.add).then_inc(dt_one, 1)
                dve.drain()
                nc.vector.tensor_scalar(dt_e, dt_w, 1.0, None, ALU.is_equal)
                nc.vector.tensor_scalar(dt_d, dt_w, -1.0, None, ALU.add)
                dve.drain()
                nc.vector.tensor_tensor(dt_d, dt_d, dt_e, ALU.add)
                dve.drain()
                nc.vector.reciprocal(dt_d, dt_d)
                dve.wait_ge(dt_log, L + 1)
                nc.vector.tensor_tensor(dt_e, dt_e, dt_ln, ALU.add)
                dve.drain()
                nc.vector.tensor_tensor(dt_e, dt_e, dt_d, ALU.mult)
                dve.drain()
                nc.vector.tensor_tensor(dt_e, dt_e, dt_u, ALU.mult)
                dve.drain()
                nc.vector.scalar_tensor_tensor(dt, dt_x, 0.0, dt_e, ALU.max, ALU.add)
                dve.drain()
                nc.vector.scalar_tensor_tensor(th(da), th(dt), -1.0, apos[:, L, :].unsqueeze(1).broadcast_to([P, 2, 16]),
                                               ALU.mult, ALU.mult).then_inc(dt_done, 1)

            for i in range(14):
                if i == 13:
                    attention_dve(dve, s, attention_steps(s)[:1])
                ahead_a(lo_slot_a, dve, s.a0 + i + 2)
                if i in HY_ROPES:
                    rope(HY_ROPES[i][0])
                if HY_SLOTS[i][0] == "xbc":
                    taps(i, HY_SLOTS[i][1])
                if HY_SLOTS[i][0] == "dt":
                    softplus()
            dve.wait_ge(bc_half, L + 1)
            nc.vector.tensor_copy(cs, tp[:, 0, 256:304])
            dve.drain()
            nc.vector.tensor_tensor(csd, cs[:, 32:48], cs[:, 0:16], ALU.subtract).then_inc(cs_out, 1)
            attention_dve(dve, s, attention_steps(s)[1:])
            def heads(v):
                return v.rearrange("p (h d) -> p h d", d=HD)

            def per_head(v):
                return v.unsqueeze(2).broadcast_to([P, SSM_HEADS, HD])

            dve.wait_ge(xs_act, L + 1)
            dve.wait_ge(decays, L + 1)
            nc.vector.tensor_tensor(heads(xdt[:, 0, :]), heads(xs[:, 0, :]), per_head(dt[:, 0:16]), ALU.mult)
            dve.drain()
            nc.vector.tensor_tensor(heads(xdec), heads(xdt[:, 0, :]), per_head(dec0), ALU.mult).then_inc(xdec_ready, 1)
            dve.wait_ge(x_turned, 2 * L + 2)
            for c in range(NT):
                for q4 in range(4):
                    dve.wait_ge(row_ps, 8 * L + 4 * c + q4 + 1)
                    for e in range(4):
                        h = 4 * q4 + e
                        ins = nc.vector.scalar_tensor_tensor(mTs[c][:, h, :], acc[:, q4, e * P:(e + 1) * P],
                                                             cs[:, 16 * c + h:16 * c + h + 1], C("negtri"),
                                                             ALU.subtract, ALU.add)
                    ins.then_inc(seg_ready, 1)
                if c == 0:
                    nc.vector.tensor_copy(xs[:, 1, :], tp[:, :, :].rearrange("p g n -> p (g n)")).then_inc(xs_dve, 1)
                    dve.drain()
                    nc.vector.tensor_tensor(heads(xdt[:, 1, :]), heads(xs[:, 1, :]), per_head(dt[:, 16:32]), ALU.mult)
                for g in range(SSM_GROUPS):
                    dve.wait_ge(seg_exp, 8 * L + 4 * c + 2 * g + 2)
                    m = mTs[c][:, 8 * g:8 * g + 8, :]
                    nc.vector.tensor_tensor(m, m, cbT[:, c, g, :].unsqueeze(1).broadcast_to([P, 8, P]), ALU.mult).then_inc(m_ready, 1)
            for c in range(NT):
                dve.wait_ge(skip_ready, 2 * L + c + 1)
                dve.wait_ge(ydiag_ps, 2 * L + c + 1)
                banks = tp if c == 0 else acc[:, 0:2, :]
                nc.vector.tensor_tensor(y[:, c, :], banks[:, :, :].rearrange("p g n -> p (g n)"), y[:, c, :], ALU.add)
                if c == 1:
                    dve.wait_ge(yoff_ps, L + 1)
                    nc.vector.tensor_tensor(heads(xs[:, 1, :]), heads(gu[:, :, :].rearrange("p g n -> p (g n)")),
                                            per_head(ecs1), ALU.mult)
                    dve.drain()
                    nc.vector.tensor_tensor(y[:, 1, :], y[:, 1, :], xs[:, 1, :], ALU.add)
                dve.drain()
                nc.vector.tensor_tensor(y[:, c, :], y[:, c, :], zsil[:, c, :], ALU.mult).then_inc(y_ready, 1)
            for c in range(NT):
                dve.wait_ge(rstd_ready, 2 * s.rms0 + 3 + c)
                for g in range(SSM_GROUPS):
                    yy = y[:, c, g * 512:(g + 1) * 512]
                    ins = nc.vector.tensor_scalar(yy, yy, rstd[:, 4 + 2 * c + g:5 + 2 * c + g], None, ALU.mult)
                ins.then_inc(xn_ready, 1)
            turn_dve(dve, s.turn0 + 1, oT_hi, oT_lo, 4, ssm_col(s), turn_others)
            out_split(lo_slot_a, dve, s)
            post_dve(dve, s, lambda: dve.wait_ge(a_used, s.a0 + 20))

        def skip_pool(pool, s):
            L = s.layer
            pool.wait_ge(o_lo, s.pair0 + 4)
            for c in range(NT):
                pool.wait_ge((xs_act, xs_dve)[c], L + 1)
                nc.gpsimd.tensor_tensor(y[:, c, :].rearrange("p (h d) -> p h d", d=HD), xs[:, c, :].rearrange("p (h d) -> p h d", d=HD),
                                        dskip[:, L, :].unsqueeze(2).broadcast_to([P, SSM_HEADS, HD]), ALU.mult)\
                    .then_inc(skip_ready, 1)

        def flip_banks():
            return [acc[:, 0, :], acc[:, 1, :], acc[:, 2, :], acc[:, 3, :], gu[:, 0, :], gu[:, 1, :], tp[:, 0, :], tp[:, 1, :]]

        def final_sync(sp, s):
            load_gain(sp, s, T["final_norm"])
            sp.wait_ge(scratch_out, 16)
            src = bass.AP(scratch.tensor, 0, [[1, P], [384, NH], [1, 256]])
            sp.dma_start(bias_rev, src).then_inc(scratch_in, 16)

        def final_pe(pe, s):
            pe.wait_ge(x_ready, 2 * s.k)
            pe.wait_ge(scratch_in, 16)
            for b, bank in enumerate(flip_banks()):
                nc.tensor.matmul(bank, C("flip"), bias_rev[:, 2 * b:2 * b + 2, :], start=True, stop=True).then_inc(flip_ready, 1)

        def flip_out(copy, b):
            bank = flip_banks()[b].rearrange("p (h c) -> p h c", h=2)
            for c0, src in ((0, P), (P, 0), (2 * P, P)):
                ins = copy(bias[:, 2 * b:2 * b + 2, c0:c0 + P], bank[:, :, src:src + P])
            return ins

        def final_act(act, s):
            for t in range(NT):
                stage_start(act, s, t)
                rms_sum_act(act, s.rms0, t, x[:, t, :], D ** -0.5)
            for b in range(4, 8):
                act.wait_ge(flip_ready, b + 1)
                flip_out(lambda o, i: nc.scalar.activation(o, i, ACT.Copy), b).then_inc(flip_act, 1)

        def final_dve(dve, s):
            dve.wait_ge(gain_full, 16 * (s.gain0 + 1))
            for b in range(4):
                dve.wait_ge(flip_ready, b + 1)
                flip_out(nc.vector.tensor_copy, b)
            dve.wait_ge(flip_act, 4)
            for t in range(NT):
                dve.wait_ge(rstd_ready, 2 * s.rms0 + t + 1)
                o = 2 * (s.rms0 % 2) + t
                nc.vector.scalar_tensor_tensor(x[:, t, :], x[:, t, :], rstd[:, o:o + 1], gain_b, ALU.mult, ALU.mult)\
                    .then_inc(x_ready, 1)

        def setup_loads():
            yield const[:, :], T["constants"][:, 0:KEPT_COLS]
            yield setup_const, T["constants"][:, KEPT_COLS:CONST_COLS]
            yield x[:, :, :], T["x"][0].rearrange("(t p) d -> p t d", p=P)
            yield rows[0:96, 0, :], T["conv_w"].rearrange("l t (k c) -> (l t k) c", c=P)
            yield rows[96:120, 0, :], T["conv_b"].rearrange("l (k c) -> (l k) c", c=P)
            yield rows[0:16, 1, :], T["norm_mix"].rearrange("l (k c) -> (l k) c", c=P)
            yield rows[16:32, 1, :], T["norm_ffn"].rearrange("l (k c) -> (l k) c", c=P)
            yield rows[32:48, 1, :], T["ssm_norm"].rearrange("l (k c) -> (l k) c", c=P)
            yield rows[48:80, 1, :], T["b_cmp_pos_2"][0].rearrange("m (j l) d -> (m j) (l d)", l=2)
            for i in range(2):
                yield rows[0:96, 2 + i, :], T["norm_g_2"][2 * i:2 * i + 2].rearrange("l g (k c) -> (l g k) c", c=P)
            yield posb.bitcast(I32), T["positions"][0].partition_broadcast(P)
            for dst, name in ((dtb, "dt_bias"), (alog, "a_log"), (dskip, "d_skip"), (sinks, "a_sinks_2")):
                yield dst, T[name].partition_broadcast(P)
            yield rtab[0:NBUCKET, :], T["rel_bias_2"]

        LOADS = 17
        ROWS = (120, 80, 96, 96)

        def setup_pe(pe):
            pe.wait_ge(loaded, 16 * LOADS)
            for k, r in enumerate(ROWS):
                mm = nc.tensor.transpose(tp[:, 0, k * P:k * P + r], rows[0:r, k, :], ident[0:r, 0:r])
            mm.then_inc(cols_ps, 1)
            nc.tensor.matmul(tp[0:NH, 1, 0:384], rtab[0:NBUCKET, :], C("bucket", NBUCKET), start=True, stop=True).then_inc(rows_ps, 1)

        def setup_dve_(dve):
            nc.vector.memset(mhalf, -0.5)
            nc.vector.memset(ones, 1.0)
            dve.wait_ge(loaded, 16 * LOADS)
            posf, ang = setup_t[:, 0, :], setup_t[:, 1, :]
            nc.vector.tensor_copy(posf, posb.bitcast(I32))
            dve.drain()
            nc.vector.tensor_scalar(ang, posf, C("invf"), None, ALU.mult)
            dve.drain()
            two_pi = (6.28125, 0.0019340515136719, 1.2556659146e-6)
            nc.vector.tensor_scalar(setup_t[:, 3, :], ang, math.pi / 2, None, ALU.add)
            nc.vector.tensor_copy(setup_t[:, 2, :], ang)
            dve.drain()
            arg, turns_ = setup_t[:, 2:4, :], setup_t[:, 4:6, :]
            magic = 1.5 * 2.0 ** 23
            nc.vector.tensor_scalar(turns_, arg, 1.0 / (2 * math.pi), magic, ALU.mult, ALU.add)
            dve.drain()
            nc.vector.tensor_scalar(turns_, turns_, magic, None, ALU.subtract)
            dve.drain()
            for part in two_pi:
                nc.vector.scalar_tensor_tensor(arg, turns_, -part, arg, ALU.mult, ALU.add)
                dve.drain()
            nc.vector.tensor_scalar(arg, arg, 3.1415925, -3.1415925, ALU.min, ALU.max).then_inc(angles, 1)
            dve.wait_ge(cols_ps, 1)
            for k, r in enumerate(ROWS):
                nc.vector.tensor_copy(cols[:, k, 0:r], tp[:, 0, k * P:k * P + r])
            nc.vector.tensor_scalar(nsinks, sinks, -1.0, None, ALU.mult).then_inc(setup_dve, 1)
            dve.wait_ge(rows_ps, 1)
            nc.vector.tensor_tensor(bias_row[0:NH, :], tp[0:NH, 1, 0:384], C("future", NH), ALU.add).then_inc(bias_row_ready, 1)
            for n in range(2):
                lo_slot_a(dve, n)

        def setup_act_(act):
            act.wait_ge(loaded, 16 * LOADS)
            nc.scalar.activation(apos, alog, ACT.Exp)
            act.wait_ge(angles, 1)
            nc.scalar.activation(sin, setup_t[:, 2, :], ACT.Sin)
            nc.scalar.activation(cos, setup_t[:, 3, :], ACT.Sin).then_inc(setup_act, 1)
            for n in range(2):
                hi_slot_a(act, n)

        block = ctx.enter_context(nc.Block())

        @block.sync
        def _(sp):
            for dst, src in setup_loads():
                sp.dma_start(dst, src).then_inc(loaded, 16)
            for s in stages:
                {"ffn": ffn_sync, "final": final_sync}.get(s.kind, mixer_sync)(sp, s)
            sp.wait_ge(x_ready, 2 * len(stages))
            sp.dma_start(out[0].rearrange("(t p) d -> p t d", p=P), x[:, :, :]).then_inc(stored, 16)
            sp.wait_ge(stored, 16)

        @block.gpsimd
        def _(pool):
            if any(s.kind == "final" for s in stages):
                pool.wait_ge(bias_row_ready, 1)
                pool.dma_start(scratch, bias_row[0:NH, :]).then_inc(scratch_out, 16)
                pool.wait_ge(scratch_out, 16)
            for s in stages:
                rms_pow_pool(pool, s.rms0, eps_of(s))
                if s.kind in KINDS:
                    normalise_pool(pool, s)
                if s.kind == "hybrid":
                    skip_pool(pool, s)
                    for c in range(NT):
                        pool.wait_ge(sq_act, 2 * s.rms0 + 3 + c)
                        o = slice(4 + 2 * c, 6 + 2 * c)
                        nc.gpsimd.tensor_scalar(ms[:, o], ssg[:, 2 * c:2 * c + 2], float(SSM_GROUPS) / SSM_INNER, EPS1, ALU.mult, ALU.add)
                        pool.drain()
                        nc.gpsimd.tensor_tensor(rstd[:, o], ms[:, o], mhalf[:, 0:2], ALU.pow).then_inc(rstd_ready, 1)
                elif s.kind != "final" and added_norm(s):
                    rms_pow_pool(pool, s.rms0 + 1, (4 if s.kind == "ffn" else 1) * EPS2)

        @block.scalar
        def _(act):
            setup_act_(act)
            for s in stages:
                {"ffn": ffn_act, "final": final_act, "hybrid": hybrid_act, "B": b_act}.get(s.kind, ac_act)(act, s)

        @block.vector
        def _(dve):
            setup_dve_(dve)
            for s in stages:
                {"ffn": ffn_dve, "final": final_dve, "hybrid": hybrid_dve, "B": b_dve}.get(s.kind, ac_dve)(dve, s)

        @block.tensor
        def _(pe):
            setup_pe(pe)
            for s in stages:
                {"ffn": ffn_pe, "final": final_pe, "hybrid": hybrid_pe, "B": b_pe}.get(s.kind, ac_pe)(pe, s)


NAMES = ("x", "positions", "norm_mix", "w_in", "conv_w", "conv_b", "dt_bias", "a_log", "d_skip", "ssm_norm", "w_out",
         "norm_ffn", "w_gate", "w_up", "w_down", "final_norm", "rel_bias_2", "norm_g_2", "ffn_w_in_2", "ffn_w_out_2",
         "a_w_in_2", "a_w_out_2", "a_sinks_2", "b_w_in_2", "b_w_out_2", "b_cmp_pos_2", "b_cmp_w1_2", "b_cmp_w2_2",
         "c_w_in_2", "c_w_out_2")


def kernel(**inputs):
    import concourse.bacc as bacc
    from concourse.bass_utils import run_bass_kernel_spmd

    nc = bacc.Bacc("TRN2", target_bir_lowering=False, num_devices=1)
    arrays = {f"in_{n}": np.ascontiguousarray(inputs[n]) for n in NAMES}
    arrays["in_constants"] = constants()
    T = {n[3:]: nc.dram_tensor(n, a.shape, mybir.dt.from_np(a.dtype), kind="ExternalInput").ap() for n, a in arrays.items()}
    out = nc.dram_tensor("out", (1, SEQ, D), F32, kind="ExternalOutput").ap()
    build_block(nc, T, out, plan_stages())
    return run_bass_kernel_spmd(nc, [arrays], core_ids=[0]).results[0]["out"]
```
